# Optimizing a Trainium2 kernel written in Bass

```python
import jax, jax.numpy as jnp
from jax import lax
import numpy as np
import math

D_MODEL = 1024
BATCH = 1
SEQ = 256
DEPTH = 1

GRID_W = 64
CTX_LEN = 256
HG_HEADS = 4
HG_DK = 128
HG_DV = 128
GLA_HEADS = 4
GLA_DK = 64
GLA_DV = 128
GLA_GATE_RANK = 16
GLA_GATE_NORM = 16.0
HG_KW = HG_HEADS * HG_DK
HG_VW = HG_HEADS * HG_DV
GLA_KW = GLA_HEADS * GLA_DK
GLA_VW = GLA_HEADS * GLA_DV
D_MIX = HG_VW + GLA_VW
CHUNK = 64
PEER_HEADS = 8
PEER_NKEYS = 128
PEER_EXPERTS = PEER_NKEYS * PEER_NKEYS
PEER_DQ = 256
PEER_TOPK = 16
PEER_BLOCK = 128
ALPHA = (2.0 * DEPTH) ** 0.25
BETA = (8.0 * DEPTH) ** -0.25
EPS = 1e-6
LB_FLOOR = 1e-30
IN_SPLITS = (HG_KW, HG_KW, HG_KW, HG_VW, HG_VW, GLA_KW, GLA_KW, GLA_VW, GLA_VW, GLA_GATE_RANK, GLA_GATE_RANK)
D_IN = sum(IN_SPLITS)
IN_SPLIT_POINTS = [int(p) for p in np.cumsum(IN_SPLITS)[:-1]]


def layer_norm(x, gamma=None, beta=None):
    xf = x.astype(jnp.float32)
    mu = jnp.mean(xf, axis=-1, keepdims=True)
    var = jnp.mean(jnp.square(xf - mu), axis=-1, keepdims=True)
    y = (xf - mu) * lax.rsqrt(var + EPS)
    if gamma is not None:
        y = y * gamma.astype(jnp.float32) + beta.astype(jnp.float32)
    return y.astype(x.dtype)

def modulate(x, shift, scale):
    return layer_norm(x) * (1.0 + scale) + shift

def heads(t, n):
    B, L, _ = t.shape
    return t.reshape(B, L, n, -1).transpose(0, 2, 1, 3).astype(jnp.float32)

def head_rms_merge(o, gain):
    o = o * lax.rsqrt(jnp.mean(o * o, axis=-1, keepdims=True) + EPS) * gain.astype(jnp.float32)
    B, n, L, d = o.shape
    return o.transpose(0, 2, 1, 3).reshape(B, L, n * d)

def to_col_major(t, rows):
    B, L, C = t.shape
    return t.reshape(B, rows, GRID_W, C).transpose(0, 2, 1, 3).reshape(B, L, C)

def from_col_major(t, rows):
    B, L, C = t.shape
    return t.reshape(B, GRID_W, rows, C).transpose(0, 2, 1, 3).reshape(B, L, C)

def chunk_scan(q, k, v, log_a, s0):
    B, H, L, dk = q.shape
    dv = v.shape[-1]
    n = L // CHUNK

    def split(t):
        return jnp.moveaxis(t.reshape(B, H, n, CHUNK, t.shape[-1]), 2, 0)

    incl = jnp.tril(jnp.ones((CHUNK, CHUNK), dtype=bool))[:, :, None]

    def step(s, inp):
        qc, kc, vc, ac = inp
        b = jnp.cumsum(ac, axis=-2)
        rel = b[..., :, None, :] - b[..., None, :, :]
        decay = jnp.where(incl, jnp.exp(jnp.minimum(rel, 0.0)), 0.0)
        scores = jnp.einsum('bhtk,bhsk,bhtsk->bhts', qc, kc, decay)
        o = jnp.einsum('bhts,bhsv->bhtv', scores, vc) + jnp.einsum('bhtk,bhkv->bhtv', qc * jnp.exp(b), s)
        b_end = b[..., -1:, :]
        s_new = jnp.exp(b_end[..., 0, :])[..., None] * s + jnp.einsum('bhsk,bhsv->bhkv', kc * jnp.exp(b_end - b), vc)
        return s_new, o

    s_end, o = lax.scan(step, s0, (split(q), split(k), split(v), split(log_a)))
    return jnp.moveaxis(o, 0, 2).reshape(B, H, L, dv), s_end

def scan_two_way(ctx_parts, lat_parts):
    qc, vc, kcf, acf, kcb, acb = ctx_parts
    ql, vl, klf, alf, klb, alb = lat_parts
    B, H, _, dk = qc.shape
    s0 = jnp.zeros((B, H, dk, vc.shape[-1]), jnp.float32)
    flip = lambda t: jnp.flip(t, axis=2)
    oc_f, sc_f = chunk_scan(qc, kcf, vc, acf, s0)
    ol_f, _ = chunk_scan(ql, klf, vl, alf, sc_f)
    oc_b, sc_b = chunk_scan(flip(qc), flip(kcb), flip(vc), flip(acb), s0)
    ol_b, _ = chunk_scan(flip(ql), flip(klb), flip(vl), flip(alb), sc_b)
    return oc_f + flip(oc_b), ol_f + flip(ol_b)

def hgrn2_inputs(hq, hff, hfb, hi, lb_f, lb_b):
    def gate(z, lb):
        z = z.astype(jnp.float32)
        log_lb = jnp.log(jnp.maximum(lb, LB_FLOOR))
        log_f = jnp.logaddexp(log_lb, jnp.log1p(-lb) + jax.nn.log_sigmoid(z))
        k = (1.0 - lb) * jax.nn.sigmoid(-z)
        return heads(k, HG_HEADS), heads(log_f, HG_HEADS)
    kf, af = gate(hff, lb_f)
    kb, ab = gate(hfb, lb_b)
    return (heads(hq, HG_HEADS), heads(hi, HG_HEADS), kf, af, kb, ab)

def gla_inputs(gq, gk, gv, glf, glb, w_gk2, b_gk):
    def gate(r, w, b):
        la = jax.nn.log_sigmoid((r @ w + b).astype(jnp.float32)) / GLA_GATE_NORM
        return heads(la, GLA_HEADS)
    k = heads(gk, GLA_HEADS)
    q = heads(gq, GLA_HEADS) * (GLA_DK ** -0.5)
    return (q, heads(gv, GLA_HEADS), k, gate(glf, w_gk2[0], b_gk[0]), k, gate(glb, w_gk2[1], b_gk[1]))

def token_mixer(u_c, u_l, rows, lb_f, lb_b, w_gk2, b_gk, hg_gain, gla_gain):
    pc = jnp.split(u_c, IN_SPLIT_POINTS, axis=-1)
    pl = jnp.split(u_l, IN_SPLIT_POINTS, axis=-1)
    a_c, a_l = scan_two_way(hgrn2_inputs(pc[0], pc[1], pc[2], pc[3], lb_f, lb_b),
                            hgrn2_inputs(pl[0], pl[1], pl[2], pl[3], lb_f, lb_b))
    out_a_c = head_rms_merge(a_c, hg_gain).astype(u_c.dtype) * jax.nn.silu(pc[4])
    out_a_l = head_rms_merge(a_l, hg_gain).astype(u_l.dtype) * jax.nn.silu(pl[4])
    gl = [to_col_major(pl[j], rows) for j in (5, 6, 7, 9, 10)]
    b_c, b_l = scan_two_way(gla_inputs(pc[5], pc[6], pc[7], pc[9], pc[10], w_gk2, b_gk),
                            gla_inputs(gl[0], gl[1], gl[2], gl[3], gl[4], w_gk2, b_gk))
    out_b_c = head_rms_merge(b_c, gla_gain).astype(u_c.dtype) * jax.nn.silu(pc[8])
    out_b_l = from_col_major(head_rms_merge(b_l, gla_gain), rows).astype(u_l.dtype) * jax.nn.silu(pl[8])
    return (jnp.concatenate([out_a_c, out_b_c], axis=-1), jnp.concatenate([out_a_l, out_b_l], axis=-1))

def peer(h, w_query, sub_keys, expert_u, expert_v):
    B, L, D = h.shape
    tok = h.reshape(-1, PEER_BLOCK, D)
    k1 = sub_keys[0].astype(jnp.float32)
    k2 = sub_keys[1].astype(jnp.float32)

    def block(t):
        q = (t @ w_query).reshape(PEER_BLOCK, PEER_HEADS, 2, PEER_DQ // 2).astype(jnp.float32)
        s1 = jnp.einsum('thd,nd->thn', q[:, :, 0], k1)
        s2 = jnp.einsum('thd,nd->thn', q[:, :, 1], k2)
        v1, i1 = lax.top_k(s1, PEER_TOPK)
        v2, i2 = lax.top_k(s2, PEER_TOPK)
        cand_s = (v1[..., :, None] + v2[..., None, :]).reshape(PEER_BLOCK, PEER_HEADS, PEER_TOPK * PEER_TOPK)
        cand_i = (i1[..., :, None] * PEER_NKEYS + i2[..., None, :]).reshape(PEER_BLOCK, PEER_HEADS, PEER_TOPK * PEER_TOPK)
        top_s, pos = lax.top_k(cand_s, PEER_TOPK)
        idx = jnp.take_along_axis(cand_i, pos, axis=-1)
        g = jax.nn.softmax(top_s, axis=-1)
        act = jax.nn.gelu(jnp.einsum('thkd,td->thk', expert_u[idx], t).astype(jnp.float32))
        return jnp.einsum('thk,thkd->td', (g * act).astype(t.dtype), expert_v[idx])

    return lax.map(block, tok).reshape(B, L, D)

def first_inputs(seed: int = 0) -> dict:
    key = jax.random.key(seed)
    ks = jax.random.split(key, 20)
    f32 = jnp.float32
    nrm = lambda k, shape, s: jax.random.normal(k, shape, f32) * s
    return {
        'x': nrm(ks[0], (BATCH, SEQ, D_MODEL), 1.0),
        'c': nrm(ks[1], (BATCH, D_MODEL), 1.0),
        'ctx': nrm(ks[2], (BATCH, CTX_LEN, D_MODEL), 1.0),
        'c_ctx': nrm(ks[3], (D_MODEL,), 1.0),
        'w_ada': nrm(ks[4], (DEPTH, D_MODEL, 6 * D_MODEL), 0.5 * D_MODEL ** -0.5),
        'b_ada': nrm(ks[5], (DEPTH, 6 * D_MODEL), 0.01),
        'w_in': nrm(ks[6], (DEPTH, D_MODEL, D_IN), D_MODEL ** -0.5),
        'w_gk2': nrm(ks[7], (DEPTH, 2, GLA_GATE_RANK, GLA_KW), GLA_GATE_RANK ** -0.5),
        'b_gk': nrm(ks[8], (DEPTH, 2, GLA_KW), 0.01),
        'hg_lower_bounds': nrm(ks[9], (2, DEPTH, HG_KW), 0.1),
        'hg_norm': 1.0 + nrm(ks[10], (DEPTH, HG_DV), 0.01),
        'gla_norm': 1.0 + nrm(ks[11], (DEPTH, GLA_DV), 0.01),
        'w_out': nrm(ks[12], (DEPTH, D_MIX, D_MODEL), BETA * D_MIX ** -0.5),
        'ln_gamma': 1.0 + nrm(ks[13], (DEPTH, 2, D_MODEL), 0.01),
        'ln_beta': nrm(ks[14], (DEPTH, 2, D_MODEL), 0.01),
        'peer_w_query': nrm(ks[15], (DEPTH, D_MODEL, PEER_HEADS * PEER_DQ), D_MODEL ** -0.5),
        'peer_sub_keys': nrm(ks[16], (DEPTH, 2, PEER_NKEYS, PEER_DQ // 2), (PEER_DQ // 2) ** -0.5),
        'peer_u': nrm(ks[17], (DEPTH, PEER_EXPERTS, D_MODEL), D_MODEL ** -0.5),
        'peer_v': nrm(ks[18], (DEPTH, PEER_EXPERTS, D_MODEL), BETA),
    }

def first_block(x, c, ctx, c_ctx, w_ada, b_ada, w_in, w_gk2, b_gk, hg_lower_bounds, hg_norm, gla_norm,
              w_out, ln_gamma, ln_beta, peer_w_query, peer_sub_keys, peer_u, peer_v):
    rows = x.shape[1] // GRID_W
    sm = jax.nn.softmax(hg_lower_bounds.astype(jnp.float32), axis=1)
    lb_all = jnp.clip(jnp.cumsum(sm, axis=1) - sm[:, :1], 0.0, 1.0 - 1e-6)
    xc = ctx
    for i in range(DEPTH):
        last = i == DEPTH - 1
        m_l = jax.nn.silu(c) @ w_ada[i] + b_ada[i]
        m_c = jax.nn.silu(c_ctx) @ w_ada[i] + b_ada[i]
        sh1_l, sc1_l, g1_l, sh2_l, sc2_l, g2_l = [t[:, None, :] for t in jnp.split(m_l, 6, axis=-1)]
        sh1_c, sc1_c, g1_c, sh2_c, sc2_c, g2_c = jnp.split(m_c, 6, axis=-1)
        u_l = modulate(x, sh1_l, sc1_l) @ w_in[i]
        u_c = modulate(xc, sh1_c, sc1_c) @ w_in[i]
        mix_c, mix_l = token_mixer(u_c, u_l, rows, lb_all[0, i], lb_all[1, i], w_gk2[i], b_gk[i],
                                   hg_norm[i], gla_norm[i])
        x = layer_norm(ALPHA * x + g1_l * (mix_l @ w_out[i]), ln_gamma[i, 0], ln_beta[i, 0])
        if not last:
            xc = layer_norm(ALPHA * xc + g1_c * (mix_c @ w_out[i]), ln_gamma[i, 0], ln_beta[i, 0])
        y_l = peer(modulate(x, sh2_l, sc2_l), peer_w_query[i], peer_sub_keys[i], peer_u[i], peer_v[i])
        x = layer_norm(ALPHA * x + g2_l * y_l, ln_gamma[i, 1], ln_beta[i, 1])
        if not last:
            y_c = peer(modulate(xc, sh2_c, sc2_c), peer_w_query[i], peer_sub_keys[i], peer_u[i], peer_v[i])
            xc = layer_norm(ALPHA * xc + g2_c * y_c, ln_gamma[i, 1], ln_beta[i, 1])
    return x


DEPTH_2 = 2

N_MIXERS = 2
N_SSM_LAYERS = (DEPTH_2 + 1) // 2
N_ATT_LAYERS = DEPTH_2 // 2
SSM_WIDTH = D_MODEL // 2
SSM_CH = 16
SSM_GROUPS = SSM_WIDTH // SSM_CH
SSM_STATE = 64
DT_MIN, DT_MAX = 1e-3, 1e-1
HEAD_DIM = 64
N_HEADS = D_MODEL // HEAD_DIM
N_KV_HEADS = N_HEADS // 4
KV_GROUP = N_HEADS // N_KV_HEADS
IDX_HEADS = max(4, D_MODEL // 128)
IDX_DIM = 64
TOPK_MAX = 256
Q_BLOCK = 128
ROPE_THETA = 10000.0
ATT_SPLITS = (N_HEADS * HEAD_DIM, N_KV_HEADS * HEAD_DIM, N_KV_HEADS * HEAD_DIM,
              IDX_HEADS * IDX_DIM, IDX_DIM, IDX_HEADS)
ATT_IN_COLS = sum(ATT_SPLITS)
D_FF = 4 * D_MODEL
NORM_EPS = 1e-6


def rms_norm(x, g):
    xf = x.astype(jnp.float32)
    y = xf * lax.rsqrt(jnp.mean(xf * xf, axis=-1, keepdims=True) + NORM_EPS)
    return (y * g.astype(jnp.float32)).astype(x.dtype)

def rope_tables(seq_len, dim, dtype):
    half = dim // 2
    inv_freq = ROPE_THETA ** (-jnp.arange(half, dtype=jnp.float32) * 2.0 / dim)
    ang = jnp.arange(seq_len, dtype=jnp.float32)[:, None] * inv_freq[None, :]
    cos = jnp.concatenate([jnp.cos(ang), jnp.cos(ang)], axis=-1)
    sin = jnp.concatenate([jnp.sin(ang), jnp.sin(ang)], axis=-1)
    return cos.astype(dtype), sin.astype(dtype)

def apply_rope(x, cos, sin):
    half = x.shape[-1] // 2
    rot = jnp.concatenate([-x[..., half:], x[..., :half]], axis=-1)
    return x * cos[None, :, None, :] + rot * sin[None, :, None, :]

def s5_mixer(h, w_in, lam_re, lam_im, log_dt, b_re, b_im, c_re, c_im, d_skip, w_glu, w_out):
    bsz, seq, _ = h.shape
    dt_ = h.dtype
    u = (h @ w_in).reshape(bsz, seq, SSM_GROUPS, SSM_CH)
    lr = lam_re.astype(jnp.float32); li = lam_im.astype(jnp.float32)
    dt = jnp.exp(log_dt.astype(jnp.float32))[:, None]
    mag = jnp.exp(lr * dt)
    abar_re = mag * jnp.cos(li * dt)
    abar_im = mag * jnp.sin(li * dt)
    den = lr * lr + li * li
    nr = abar_re - 1.0
    ni = abar_im
    fr = (nr * lr + ni * li) / den
    fi = (ni * lr - nr * li) / den
    br = b_re.astype(jnp.float32); bi = b_im.astype(jnp.float32)
    bbar_re = (fr[..., None] * br - fi[..., None] * bi).astype(dt_)
    bbar_im = (fr[..., None] * bi + fi[..., None] * br).astype(dt_)
    bu_re = jnp.einsum('bsgc,gpc->bsgp', u, bbar_re)
    bu_im = jnp.einsum('bsgc,gpc->bsgp', u, bbar_im)
    a_re = jnp.broadcast_to(abar_re.astype(dt_), bu_re.shape)
    a_im = jnp.broadcast_to(abar_im.astype(dt_), bu_im.shape)

    def combine(left, right):
        a1r, a1i, b1r, b1i = left
        a2r, a2i, b2r, b2i = right
        return (a2r * a1r - a2i * a1i,
                a2r * a1i + a2i * a1r,
                a2r * b1r - a2i * b1i + b2r,
                a2r * b1i + a2i * b1r + b2i)

    _, _, xs_re, xs_im = lax.associative_scan(combine, (a_re, a_im, bu_re, bu_im), axis=1)
    y = (jnp.einsum('bsgp,gcp->bsgc', xs_re, c_re)
         - jnp.einsum('bsgp,gcp->bsgc', xs_im, c_im)
         + d_skip[None, None] * u)
    z = jax.nn.gelu(y.reshape(bsz, seq, SSM_WIDTH))
    z = z * jax.nn.sigmoid(z @ w_glu)
    return z @ w_out

def dsa_mixer(h, w_in, w_out):
    bsz, seq, _ = h.shape
    dt_ = h.dtype
    proj = h @ w_in
    offs = np.cumsum(ATT_SPLITS)[:-1].tolist()
    q, k, v, qi, ki, wi = jnp.split(proj, offs, axis=-1)
    cos, sin = rope_tables(seq, HEAD_DIM, dt_)
    q = apply_rope(q.reshape(bsz, seq, N_HEADS, HEAD_DIM), cos, sin)
    k = apply_rope(k.reshape(bsz, seq, N_KV_HEADS, HEAD_DIM), cos, sin)
    v = v.reshape(bsz, seq, N_KV_HEADS, HEAD_DIM)
    qi = apply_rope(qi.reshape(bsz, seq, IDX_HEADS, IDX_DIM), cos, sin)
    ki = apply_rope(ki[:, :, None, :], cos, sin)[:, :, 0, :]
    wi = wi * (IDX_HEADS ** -0.5 * IDX_DIM ** -0.5)

    k_sel = min(TOPK_MAX, seq // 4)
    n_blk = seq // Q_BLOCK
    to_blocks = lambda a: jnp.swapaxes(a.reshape((bsz, n_blk, Q_BLOCK) + a.shape[2:]), 0, 1)
    q_b, qi_b, wi_b = to_blocks(q), to_blocks(qi), to_blocks(wi)
    starts = jnp.arange(n_blk, dtype=jnp.int32) * Q_BLOCK
    key_pos = jnp.arange(seq, dtype=jnp.int32)
    b_idx = jnp.arange(bsz)[:, None, None]
    scale = HEAD_DIM ** -0.5

    def block(args):
        q_blk, qi_blk, wi_blk, t0 = args
        t = t0 + jnp.arange(Q_BLOCK, dtype=jnp.int32)
        rel = jax.nn.relu(jnp.einsum('bthd,bsd->bths', qi_blk, ki).astype(jnp.float32))
        score = jnp.einsum('bths,bth->bts', rel, wi_blk.astype(jnp.float32))
        causal = key_pos[None, :] <= t[:, None]
        score = jnp.where(causal[None], score, -jnp.inf)
        _, idx = lax.top_k(score, k_sel)
        kg = k[b_idx, idx]
        vg = v[b_idx, idx]
        qg = q_blk.reshape(bsz, Q_BLOCK, N_KV_HEADS, KV_GROUP, HEAD_DIM)
        att = jnp.einsum('btngd,btknd->btngk', qg, kg).astype(jnp.float32) * scale
        valid = idx <= t[None, :, None]
        att = jnp.where(valid[:, :, None, None, :], att, -jnp.inf)
        p = jax.nn.softmax(att, axis=-1).astype(dt_)
        o = jnp.einsum('btngk,btknd->btngd', p, vg)
        return o.reshape(bsz, Q_BLOCK, N_HEADS * HEAD_DIM)

    out = lax.map(block, (q_b, qi_b, wi_b, starts))
    out = jnp.swapaxes(out, 0, 1).reshape(bsz, seq, N_HEADS * HEAD_DIM)
    return out @ w_out

def sq_relu_mlp(h, w1, w2):
    a = jax.nn.relu(h @ w1)
    return (a * a) @ w2

def second_inputs(seed: int = 0) -> dict:
    key = jax.random.key(seed)
    ks = jax.random.split(key, 20)
    nA, nB = N_SSM_LAYERS, N_ATT_LAYERS
    G, P, C, E = SSM_GROUPS, SSM_STATE, SSM_CH, SSM_WIDTH
    nrm = lambda k, shape, fan: jax.random.normal(k, shape, jnp.float32) * (fan ** -0.5)
    x = jax.random.normal(ks[0], (BATCH, SEQ, D_MODEL), jnp.float32)
    norm_g = 1.0 + 0.01 * jax.random.normal(ks[1], (DEPTH_2, 4, D_MODEL), jnp.float32)
    mlp_w1 = nrm(ks[2], (DEPTH_2, D_MODEL, D_FF), D_MODEL)
    mlp_w2 = nrm(ks[3], (DEPTH_2, D_FF, D_MODEL), D_FF)
    ssm_w_in = nrm(ks[4], (nA, D_MODEL, E), D_MODEL)
    n_idx = jnp.arange(P, dtype=jnp.float32)
    ssm_lam_re = -0.5 + 0.01 * jax.random.normal(ks[5], (nA, G, P), jnp.float32)
    ssm_lam_im = math.pi * n_idx[None, None, :] + 0.01 * jax.random.normal(ks[6], (nA, G, P), jnp.float32)
    ssm_log_dt = jax.random.uniform(ks[7], (nA, G), jnp.float32, math.log(DT_MIN), math.log(DT_MAX))
    ssm_b_re = nrm(ks[8], (nA, G, P, C), 2 * C)
    ssm_b_im = nrm(ks[9], (nA, G, P, C), 2 * C)
    ssm_c_re = nrm(ks[10], (nA, G, C, P), 2 * P)
    ssm_c_im = nrm(ks[11], (nA, G, C, P), 2 * P)
    ssm_d = jax.random.normal(ks[12], (nA, G, C), jnp.float32)
    ssm_w_glu = nrm(ks[13], (nA, E, E), E)
    ssm_w_out = nrm(ks[14], (nA, E, D_MODEL), E)
    att_w_in = nrm(ks[15], (nB, D_MODEL, ATT_IN_COLS), D_MODEL)
    att_w_out = nrm(ks[16], (nB, N_HEADS * HEAD_DIM, D_MODEL), N_HEADS * HEAD_DIM)
    return {"x": x, "norm_g": norm_g, "mlp_w1": mlp_w1, "mlp_w2": mlp_w2,
            "ssm_w_in": ssm_w_in, "ssm_lam_re": ssm_lam_re, "ssm_lam_im": ssm_lam_im,
            "ssm_log_dt": ssm_log_dt, "ssm_b_re": ssm_b_re, "ssm_b_im": ssm_b_im,
            "ssm_c_re": ssm_c_re, "ssm_c_im": ssm_c_im, "ssm_d": ssm_d,
            "ssm_w_glu": ssm_w_glu, "ssm_w_out": ssm_w_out,
            "att_w_in": att_w_in, "att_w_out": att_w_out}

def second_block(x, norm_g, mlp_w1, mlp_w2, ssm_w_in, ssm_lam_re, ssm_lam_im, ssm_log_dt,
              ssm_b_re, ssm_b_im, ssm_c_re, ssm_c_im, ssm_d, ssm_w_glu, ssm_w_out,
              att_w_in, att_w_out):
    h = x
    for i in range(DEPTH_2):
        j = i // N_MIXERS
        pre = rms_norm(h, norm_g[i, 0])
        if i % N_MIXERS == 0:
            mix = s5_mixer(pre, ssm_w_in[j], ssm_lam_re[j], ssm_lam_im[j], ssm_log_dt[j],
                           ssm_b_re[j], ssm_b_im[j], ssm_c_re[j], ssm_c_im[j], ssm_d[j],
                           ssm_w_glu[j], ssm_w_out[j])
        else:
            mix = dsa_mixer(pre, att_w_in[j], att_w_out[j])
        h = h + rms_norm(mix, norm_g[i, 1])
        ff = sq_relu_mlp(rms_norm(h, norm_g[i, 2]), mlp_w1[i], mlp_w2[i])
        h = h + rms_norm(ff, norm_g[i, 3])
    return h


def setup_inputs(seed=0):
    out = dict(first_inputs(seed))
    for name, value in second_inputs(seed + 1).items():
        if name != "x":
            out[name + "_2"] = value
    return out


def reference(
    x, c, ctx, c_ctx, w_ada, b_ada, w_in, w_gk2, b_gk, hg_lower_bounds, hg_norm, gla_norm,
    w_out, ln_gamma, ln_beta, peer_w_query, peer_sub_keys, peer_u, peer_v, norm_g_2, mlp_w1_2,
    mlp_w2_2, ssm_w_in_2, ssm_lam_re_2, ssm_lam_im_2, ssm_log_dt_2, ssm_b_re_2, ssm_b_im_2,
    ssm_c_re_2, ssm_c_im_2, ssm_d_2, ssm_w_glu_2, ssm_w_out_2, att_w_in_2, att_w_out_2,
):
    x = first_block(
        x, c, ctx, c_ctx, w_ada, b_ada, w_in, w_gk2, b_gk, hg_lower_bounds, hg_norm, gla_norm,
        w_out, ln_gamma, ln_beta, peer_w_query, peer_sub_keys, peer_u, peer_v,
    )
    return second_block(
        x, norm_g_2, mlp_w1_2, mlp_w2_2, ssm_w_in_2, ssm_lam_re_2, ssm_lam_im_2, ssm_log_dt_2,
        ssm_b_re_2, ssm_b_im_2, ssm_c_re_2, ssm_c_im_2, ssm_d_2, ssm_w_glu_2, ssm_w_out_2,
        att_w_in_2, att_w_out_2,
    )


_drawn_inputs = setup_inputs


def setup_inputs(seed=0):
    import zlib

    import numpy as np

    out = dict(_drawn_inputs(seed))
    spreads = {}
    factors = {'b_gk': 8.0, 'hg_norm': 6.187, 'gla_norm': 5.782, 'ssm_lam_re_2': 8.0}
    for name, (base, spread) in spreads.items():
        noise = np.random.default_rng([zlib.crc32(name.encode()), seed]).standard_normal(out[name].shape)
        drawn = base * np.exp(spread * noise) if base else spread * noise
        out[name] = __import__('jax').numpy.asarray(drawn.astype(out[name].dtype))
    for name, factor in factors.items():
        out[name] = (out[name] * factor).astype(out[name].dtype)
    return out
```

```python
from contextlib import ExitStack
from math import pi

import concourse.bass as bass
from concourse import mybir

F32 = mybir.dt.float32
U32 = mybir.dt.uint32
I32 = mybir.dt.int32
U8 = mybir.dt.uint8
ALU = mybir.AluOpType
ACT = mybir.ActivationFunctionType
AX_X = mybir.AxisListType.X

P = 128
D = 1024
KC = D // P
L = 256
TT = L // P
HALF = 4
WIDE = 512
SLOTS = 6
EPS = 1e-6
ALPHA = 2.0 ** 0.25
BANKS = 8

HG_HEADS, GLA_HEADS = 4, 4
HEADS = HG_HEADS + GLA_HEADS
UNITS = 6
GRID_W = 64
ROWS = L // GRID_W
RANK = 16
LEVELS = [64, 32, 16, 8, 4, 2, 1]

PEER_HEADS = 8
NKEYS = 128
TOPK = 16
GATHERS = PEER_HEADS * TOPK
GSLOTS = 8

D_FF = 4096
SSM = 512
NSTATE = 16
N_HEADS, N_KV, HD = 16, 4, 64
IDX_HEADS = 8
K_SEL = 64
ATT_COLS = 2120
ROPED = 1024 + 256 + 512 + 64
NEG = -1.0e30


def build(nc, A, out):
    with ExitStack() as ctx:
        def sb(name, shape, dt=F32):
            return ctx.enter_context(nc.sbuf_tensor(name, shape, dt))

        def sem(name):
            return ctx.enter_context(nc.semaphore(name))

        bank = [ctx.enter_context(nc.psum_tensor(f"bank{b}", [P, WIDE], F32)) for b in range(BANKS)]
        bank_full = [sem(f"bank_full{b}") for b in range(BANKS)]
        bank_free = [sem(f"bank_free{b}") for b in range(BANKS)]
        jobs = {}
        njobs = [0]

        def alloc(name, n):
            jobs[name] = njobs[0]
            njobs[0] += n

        def ps(job):
            return bank[job % BANKS]

        def wait_bank_free(pe, job):
            if job >= BANKS:
                pe.wait_ge(bank_free[job % BANKS], job // BANKS)

        def wait_bank_full(eng, job):
            eng.wait_ge(bank_full[job % BANKS], job // BANKS + 1)

        def full(job):
            return bank_full[job % BANKS]

        def free(job):
            return bank_free[job % BANKS]

        arena = sb("arena", [P, 38400])

        def carve(off, *shape, dt=None):
            n = 1
            for s in shape:
                n *= s
            ap = arena[:, off:off + n]
            if dt is not None:
                ap = ap.bitcast(dt)
            if len(shape) == 2:
                ap = ap.rearrange("p (a b) -> p a b", a=shape[0])
            if len(shape) == 3:
                ap = ap.rearrange("p (a b c) -> p a b c", a=shape[0], b=shape[1])
            if len(shape) == 4:
                ap = ap.rearrange("p (a b c d) -> p a b c d", a=shape[0], b=shape[1], c=shape[2])
            return ap

        ring = sb("ring", [P, SLOTS, HALF * WIDE])
        ident = sb("ident", [P, P])
        ones = sb("ones", [P, L])
        select = sb("select", [2, 2, P])
        eps = sb("eps", [P, 1])
        level_mask = sb("level_mask", [P, 2, len(LEVELS), P], U8)
        stat = sb("stat", [P, 64])
        small = sb("small", [P, 768])

        x_lat = carve(0, TT, D)
        mods = carve(2048, 4, D)
        mod1 = carve(6144, 4, D)
        val = carve(6144, 4, D)
        b_ada = arena[0:2, 10240:10240 + 6144]
        decay = carve(10240, 2, 2 * UNITS, L)
        key = carve(16384, 2, 2 * UNITS, L)
        h_in = carve(16384, 4, D)
        qry = carve(22528, UNITS, L)
        gate_tmp = carve(24064, 2, 2, WIDE)
        state = carve(24064, 2 * UNITS, P)
        PB = 26112
        x_ctx = carve(PB, TT, D)
        hT = carve(PB + 2048, KC, 2 * L)
        hT_col = carve(PB, KC, L)
        rank_act = carve(PB + 6144, 2, 2 * L)
        gk2 = carve(PB + 7168, 2, L)
        m_row = carve(PB + 7680, 2, WIDE)
        w_rank = carve(PB + 8704, KC, 32)
        crow = carve(PB + 9216, 1, P)
        keyT = carve(PB, TT, 2 * UNITS, P)
        lvlW = carve(PB, 2, UNITS, L)
        q_state = carve(PB + 3072, 2 * UNITS, L)
        sc_in = carve(PB + 3072, HEADS, TT, P)
        sc_x = carve(PB + 5120, HEADS, 2, P)
        lvlE = carve(PB + 7168, 2, UNITS, L)
        o_mix = carve(10240, TT, D)
        gate_out = carve(36352, TT, D)
        mixT = carve(PB + 7168, KC, L)
        sq_tmp = carve(PB, 2, D)
        row_a = carve(22528, 2, D)
        h2 = carve(6144, TT, D)
        h2T = carve(8192, KC, L)
        qT = carve(10240, 16, L)
        keys_raw = carve(14336, 2, P)
        keysT = carve(14592, 2, P)
        s_key = carve(16384, 16, P)
        s_work = carve(18432, P)
        cand = carve(18560, PEER_HEADS, L)
        c_work = carve(20608, L)
        onehot = carve(20864, PEER_HEADS, TOPK, TOPK)
        top_v = carve(24576, 16, TOPK)
        top_i = carve(24832, 16, TOPK, dt=U32)
        top_f = carve(25088, 16, TOPK)
        best_v = carve(25344, PEER_HEADS, TOPK)
        best_p = carve(25472, PEER_HEADS, TOPK, dt=U32)
        part_i = carve(25600, PEER_HEADS, TOPK, dt=U32)
        part_f = carve(25728, PEER_HEADS, TOPK)
        pick = carve(25856, 2, PEER_HEADS * TOPK)
        iota_i = carve(26112, TOPK, dt=U32)
        iota_f = carve(26128, TOPK)
        gate_w = carve(26144, TT, GATHERS)
        act_w = carve(26400, TT, GATHERS)
        rows_i = carve(26656, TT, GATHERS, dt=U32)
        sm8 = carve(26912, 2, PEER_HEADS)
        now_i = carve(26928, GSLOTS, dt=U32)
        gath = carve(27136, GSLOTS, D)
        y_acc = carve(35328, TT, D)

        hT2 = carve(2048, KC, L)
        mix2 = carve(4096, TT, D)
        row_b = carve(6144, 2, D)
        h_tok = carve(8192, TT, D)
        ff = carve(10240, 32, L)
        er = carve(10240, NSTATE, L)
        ei = carve(14336, NSTATE, L)
        Bz = carve(18432, 2, NSTATE, P)
        BT = carve(22528, 2, NSTATE, P)
        Cz = carve(26624, 2, NSTATE, P)
        braw = carve(30720, 2, NSTATE, 16)
        bbar = carve(31232, 2, NSTATE, 16)
        craw = carve(31744, 2, 4, P)
        CT = carve(32768, 2, 4, P)
        uT = carve(33792, 4, L)
        zT = carve(34816, 4, L)
        xs = carve(35840, 2, 2, L)
        rt = carve(36864, 2, 2, L)
        dT = carve(37888, 4)
        proj = carve(10240, TT, ATT_COLS)
        roped = carve(14592, TT, 24, 64)
        krope = carve(17664, TT, 5, P)
        qTa = carve(18944, 8, L)
        qiT = carve(20992, 4, L)
        kTa = carve(22016, 5, L)
        rope = carve(23296, TT, 2, HD)
        rope_t = carve(23552, TT, 29 * HD)
        idx_s = carve(27264, TT, L)
        idx_w = carve(27776, TT, L)
        keep = carve(28288, TT, L)
        rel = carve(28800, 2, 2, L)
        prob = carve(29824, 2, N_HEADS, L)
        pT = carve(14592, 2, N_HEADS, P)
        o_att = carve(8192, TT, D)

        w_full = [sem(f"w_full{s}") for s in range(SLOTS)]
        w_used = sem("w_used")
        dve_step = sem("dve_step")
        act_step = sem("act_step")
        pool_step = sem("pool_step")
        load_c, load_x, load_bada, load_gate, load_gain, load_rows, load_keys, load_norm, load_s5, \
            load_rope = [sem(f"load_{n}") for n in "c x bada gate gain rows keys norm s5 rope".split()]
        consts = sem("consts")
        c_silu = sem("c_silu")
        var_ready = sem("var_ready")
        std_ready = sem("std_ready")
        tok_ready = sem("tok_ready")
        masks_ready = sem("masks_ready")
        hT_col_ready = sem("hT_col_ready")
        lb_exp = sem("lb_exp")
        lb_sum = sem("lb_sum")
        lb_log = sem("lb_log")
        gate_abs = sem("gate_abs")
        gate_diff = sem("gate_diff")
        gate_k = sem("gate_k")
        gate_log = sem("gate_log")
        gate_done = sem("gate_done")
        scans_done = sem("scans_done")
        ctx_exp = sem("ctx_exp")
        ctx_key = sem("ctx_key")
        q_exp = sem("q_exp")
        q_state_ready = sem("q_state_ready")
        lvl_diff = sem("lvl_diff")
        lvl_exp = sem("lvl_exp")
        lvl_ready = sem("lvl_ready")
        mixed = sem("mixed")
        skey_used = sem("skey_used")
        best_ready = sem("best_ready")
        soft_ready = sem("soft_ready")
        rows_ready = sem("rows_ready")
        gathered = [sem(f"gathered{s}") for s in range(GSLOTS)]
        row_used = sem("row_used")
        gelu_done = sem("gelu_done")
        index_ready = sem("index_ready")
        rows_free = sem("rows_free")
        s5_exp = sem("s5_exp")
        s5_theta = sem("s5_theta")
        s5_sin = sem("s5_sin")
        s5_b = sem("s5_b")
        s5_dt = sem("s5_dt")
        x_state = sem("x_state")
        y_used = sem("y_used")
        y_ready = sem("y_ready")
        z_ready = sem("z_ready")
        glu_sig = sem("glu_sig")
        ff_relu = sem("ff_relu")
        ff_ready = sem("ff_ready")
        roped_ready = sem("roped_ready")
        rel_used = sem("rel_used")
        idx_causal = sem("idx_causal")
        keep_ready = sem("keep_ready")
        keep_causal = sem("keep_causal")
        logits_ready = sem("logits_ready")
        prob_ready = sem("prob_ready")
        out_ready = sem("out_ready")
        stored = sem("stored")

        NORM_USES = [("ln_in", 4), ("head", 16), ("post1", 2), ("mod2", 2), ("post2", 2)] + [
            (f"rms{i}", 2) for i in range(8)]
        norm_no = {n: i for i, (n, _) in enumerate(NORM_USES)}
        tok_no, at = {}, 0
        for n, c in [("in", 4), ("mix", 2), ("h2", 2), ("ssm", 2), ("mlp0", 2), ("att", 2), ("mlp1", 2)]:
            tok_no[n] = at
            at += c

        alloc("cT", 1)
        for n in range(12):
            alloc(f"ada{n}", 1)
            if n:
                alloc(f"adab{n - 1}", 2 if n - 1 < 4 else 1)
        alloc("adab11", 1)
        alloc("T_in", 8)
        for name, n in [("lb", 1), ("hff", 4), ("hfb", 4), ("rank", 2), ("gla_gate", 4), ("gqk", 4), ("hq", 4), ("hi", 4),
                        ("gv", 4), ("hg", 2), ("gg", 2), ("keyT", 6), ("state", 4), ("inter", 6),
                        ("scx", 4), ("diag", 4)]:
            alloc(name, n)
        for lv in range(len(LEVELS)):
            alloc(f"lvl{lv}", 8)
        for name, n in [("o", 4), ("T_mix", 4), ("out", 4), ("T_h2", 4), ("keys", 1), ("wq", 8), ("skey", 8),
                        ("s5p", 1), ("CT", 2), ("BT", 8), ("T_ssm", 4), ("ssm_in", 2)]:
            alloc(name, n)
        for j in range(NSTATE):
            if j % 4 == 0:
                alloc(f"y{j // 4}", 1)
            alloc(f"bu{j}", 1)
        for name, n in [("glu", 2), ("ssm_out", 4), ("T_mlp0", 4), ("mlp0a", 16), ("mlp0b", 4), ("T_att", 4),
                        ("att", 10), ("rT", 10), ("idx", 8), ("att_s0", 8), ("att_s1", 8), ("pT0", 4), ("pv0", 2),
                        ("pT1", 8), ("pv1", 2), ("T_atto", 4), ("att_out", 4), ("T_mlp1", 4), ("mlp1a", 16),
                        ("mlp1b", 4)]:
            alloc(name, n)

        stream, tile_no, given_back = [], {}, {}

        def weights(name, w, col0, cols, job, inside=False):
            tile_no[name] = len(stream)
            for r in range(0, w.shape[0], HALF * P):
                if not inside or r + HALF * P >= w.shape[0]:
                    given_back[len(stream)] = job
                stream.append(w[r:r + HALF * P, col0:col0 + cols].rearrange("(k p) n -> p k n", p=P))

        def wtile(n, cols=WIDE):
            return ring[:, n % SLOTS, 0:HALF * cols].rearrange("p (k n) -> p k n", k=HALF)

        def wait_weights(pe, n):
            pe.wait_ge(w_full[n % SLOTS], 16 * (n // SLOTS + 1))

        w_in = A["w_in"][0]
        for n in range(12):
            weights(f"ada{n}", A["w_ada"][0], n * WIDE, WIDE, jobs[f"ada{n}"])
        for name, c0, n in [("hff", 512, 4), ("hfb", 1024, 4), ("gqk", 2560, 4), ("hq", 0, 4), ("hi", 1536, 4),
                            ("gv", 3072, 4), ("hg", 2048, 2), ("gg", 3584, 2)]:
            weights(name, w_in, c0, WIDE, jobs[name] + n - 1)
        for n in range(2):
            weights(f"out{n}", A["w_out"][0], n * WIDE, WIDE, jobs["out"] + 2 * n + 1)
        for n in range(4):
            weights(f"wq{n}", A["peer_w_query"][0], n * WIDE, WIDE, jobs["wq"] + 2 * n + 1)
        weights("ssm_in", A["ssm_w_in_2"][0], 0, WIDE, jobs["ssm_in"] + 1)
        weights("glu", A["ssm_w_glu_2"][0], 0, WIDE, jobs["glu"] + 1)
        for n in range(2):
            weights(f"ssm_out{n}", A["ssm_w_out_2"][0], n * WIDE, WIDE, jobs["ssm_out"] + 2 * n + 1)
        for i in range(2):
            for n in range(8):
                weights(f"mlp{i}a{n}", A["mlp_w1_2"][i], n * WIDE, WIDE, jobs[f"mlp{i}a"] + 2 * n + 1)
            for n in range(2):
                weights(f"mlp{i}b{n}", A["mlp_w2_2"][i], n * WIDE, WIDE, jobs[f"mlp{i}b"] + 2 * n + 1, inside=True)
            if i == 0:
                for n in range(5):
                    weights(f"att{n}", A["att_w_in_2"][0], n * WIDE, min(WIDE, ATT_COLS - n * WIDE),
                            jobs["att"] + 2 * n + 1)
                for n in range(2):
                    weights(f"att_out{n}", A["att_w_out_2"][0], n * WIDE, WIDE, jobs["att_out"] + 2 * n + 1)

        bgk_raw = small[:, 0:128]
        lb_raw = small[:, 128:256]
        gain = small[:, 256:512].rearrange("p (a b) -> p a b", a=2)
        bgk = small[:, 512:516]
        one_lb = small[:, 516:524]
        log_lb = small[:, 524:532]
        log1m_lb = small[:, 532:540]
        lb = small[:, 540:548]
        cT = small[:, 548:564].rearrange("p (k w) -> p k w", w=2)
        b_end = small[:, 564:576]
        lb_t = small[:, 576:584]
        S5 = {n: small[:, 16 * i:16 * i + 16] for i, n in enumerate(
            "lr li dt mag th kk r sn hs cs ar ai den nr fr fi t1 t2 pr pi qr qi".split())}
        d_col = small[:, 360:364]
        s5_raw = carve(36864, 3, P)
        d_raw = carve(37300, P)
        dt_raw = carve(37430, 2)
        wi_col = small[:, 0:16].rearrange("p (t h) -> p t h", t=2)
        m8 = small[:, 16:24]
        mx16 = small[:, 24:56].rearrange("p (t h) -> p t h", t=2)
        sum16 = small[:, 56:88].rearrange("p (t h) -> p t h", t=2)
        it_t = gate_out[:, 0, 0:P].bitcast(I32)
        it_s = gate_out[:, 0, P:2 * P].bitcast(I32)
        it_x = gate_out[:, 0, 2 * P:3 * P].bitcast(I32)
        it_f = gate_out[:, 0, 3 * P:4 * P]
        it_g = gate_out[:, 0, 4 * P:5 * P]

        HEAD_AT = [0, 1, 2, 3, 4, 6, 5, 7]

        def unit_rows(place):
            head = HEAD_AT[place]
            if head < HG_HEADS:
                return head, slice(0, P)
            g = head - HG_HEADS
            return HG_HEADS + g // 2, slice(64 * (g % 2), 64 * (g % 2) + 64)

        counts = {}

        def step(eng, name, ins):
            counts[name] = counts.get(name, 0) + 1
            ins.then_inc({"dve": dve_step, "act": act_step, "pool": pool_step}[name], 1)
            eng.wait_ge({"dve": dve_step, "act": act_step, "pool": pool_step}[name], counts[name])

        def mark(eng, ins, s):
            counts[s.name] = counts.get(s.name, 0) + 1
            ins.then_inc(s, 1)
            eng.wait_ge(s, counts[s.name])

        def read_out(eng, ins, job):
            ins.then_inc(free(job), 1)
            eng.wait_ge(free(job), job // BANKS + 1)

        def wait_read_out(eng, job):
            eng.wait_ge(free(job), job // BANKS + 1)

        def by_cols(ap):
            return ap.rearrange("p (w r) -> p r w", r=ROWS)

        def by_rows(ap):
            return ap.rearrange("p (r w) -> p r w", r=ROWS)

        block = ctx.enter_context(nc.Block())

        @block.sync
        def _(sp):
            used = 0
            for n, src in enumerate(stream):
                if n >= SLOTS:
                    old = n - SLOTS
                    if old in given_back:
                        wait_bank_full(sp, given_back[old])
                    else:
                        used += 1
                        sp.wait_ge(w_used, used)
                sp.dma_start(wtile(n, src.shape[2]), src).then_inc(w_full[n % SLOTS], 16)
            sp.wait_ge(out_ready, 1)
            sp.dma_start(out[0].rearrange("(t p) d -> p t d", p=P), x_lat).then_inc(stored, 16)
            sp.wait_ge(stored, 16)

        @block.gpsimd
        def _(pool):
            def do(ins):
                step(pool, "pool", ins)

            pool.memset(ones[:], 1.0).then_inc(consts, 1)
            pool.memset(eps[:], EPS).then_inc(consts, 1)
            pool.iota(it_t, [[1, P]], base=0, channel_multiplier=0).then_inc(consts, 1)
            pool.iota(it_s, [[0, P]], base=0, channel_multiplier=1).then_inc(consts, 1)
            do(pool.memset(ident[:], 0.0))
            pool.affine_select(out=ident[:], in_=ident[:], compare_op=ALU.not_equal, fill=1.0, base=0,
                               pattern=[[-1, P]], channel_multiplier=1).then_inc(consts, 1)
            do(pool.memset(select[:], 0.0))
            pool.affine_select(out=select[:], in_=select[:], compare_op=ALU.not_equal, fill=1.0, base=0,
                               pattern=[[-1, 2], [0, P]], channel_multiplier=1).then_inc(consts, 1)

            for j in range(4, 8):
                wait_read_out(pool, jobs["T_in"] + j)
            for k in range(KC):
                ins = pool.tensor_copy(by_cols(hT_col[:, k, :]), by_rows(hT[:, k, L:2 * L]))
                if k < KC - 1:
                    do(ins)
            mark(pool, ins, hT_col_ready)

            pool.wait_ge(rows_ready, TT)
            loop = 0
            for table in (A["peer_u"][0], A["peer_v"][0]):
                for t in range(TT):
                    def gather(s):
                        pool.indirect_dma_start(
                            out=gath[:, s, :], out_offset=None, in_=table,
                            in_offset=bass.IndirectOffsetOnAxis(ap=now_i[:, s:s + 1], axis=0),
                        ).then_inc(gathered[s], 16)

                    if loop == 0:
                        for s in range(GSLOTS):
                            do(pool.tensor_copy(now_i[:, s:s + 1], rows_i[:, t, s:s + 1]))
                            gather(s)
                    first = counts["pool"]
                    base = loop * GATHERS
                    start = GSLOTS if loop == 0 else 0
                    with pool.Fori(start // GSLOTS, GATHERS // GSLOTS) as turn:
                        i = turn * GSLOTS
                        for s in range(GSLOTS):
                            pool.wait_ge(row_used, i + (base + s + 1 - GSLOTS))
                            pool.tensor_copy(now_i[:, s:s + 1], rows_i[:, t, bass.ds(i + s, 1)]).then_inc(pool_step, 1)
                            pool.wait_ge(pool_step, i + (first - start + s + 1))
                            pool.sem_inc(index_ready, 1)
                            gather(s)
                    counts["pool"] += GATHERS - start
                    loop += 1

            for t in range(TT):
                pool.wait_ge(rel_used, 4 * t + 4)
                pool.affine_select(out=idx_s[:, t, :], in_=idx_s[:, t, :], compare_op=ALU.is_ge, fill=-1.0e38,
                                   base=t * P, pattern=[[-1, L]], channel_multiplier=1).then_inc(idx_causal, 1)
            for t in range(TT):
                pool.wait_ge(keep_ready, t + 1)
                pool.affine_select(out=keep[:, t, :], in_=keep[:, t, :], compare_op=ALU.is_ge, fill=NEG,
                                   base=t * P, pattern=[[-1, L]], channel_multiplier=1).then_inc(keep_causal, 1)

        def mm(o, lhsT, rhs, first, last):
            return nc.tensor.matmul(o, lhsT, rhs, start=first, stop=last)

        def pe_feature(pe, job0, tile, kc, n_blocks, cols, x, per_job):
            for m in range((kc + HALF - 1) // HALF):
                wait_weights(pe, tile + m)
            for b in range(n_blocks):
                job = job0 + b // per_job
                c0 = (b % per_job) * cols
                if b % per_job == 0:
                    wait_bank_free(pe, job)
                for k in range(kc):
                    last = mm(ps(job)[:, c0:c0 + cols], wtile(tile + k // HALF)[:, k % HALF, b * P:(b + 1) * P],
                              x(k), k == 0, k == kc - 1)
                if b % per_job == per_job - 1:
                    last.then_inc(full(job), 1)

        def pe_token(pe, job0, tile, kc, xs_of_tile, cols=WIDE):
            for m in range((kc + HALF - 1) // HALF):
                wait_weights(pe, tile + m)
            for i, x in enumerate(xs_of_tile):
                wait_bank_free(pe, job0 + i)
                for k in range(kc):
                    last = mm(ps(job0 + i)[:, 0:cols], x(k), wtile(tile + k // HALF, cols)[:, k % HALF, :],
                              k == 0, k == kc - 1)
                last.then_inc(full(job0 + i), 1)

        def pe_transpose(pe, name, tiles, n_tiles):
            for t in range(n_tiles):
                if name == "atto":
                    for g in range(2):
                        wait_read_out(pe, jobs[f"pv{t}"] + g)
                else:
                    pe.wait_ge(tok_ready, tok_no[name] + t + 1)
                for g in range(2):
                    job = jobs["T_" + name] + 2 * t + g
                    wait_bank_free(pe, job)
                    for b in range(4):
                        last = nc.tensor.transpose(ps(job)[:, b * P:(b + 1) * P],
                                                   tiles[:, t, (4 * g + b) * P:(4 * g + b + 1) * P], ident[:])
                    last.then_inc(full(job), 1)

        def wait_transposed(pe, name, t0, n_tiles):
            for j in range(2 * t0, 2 * (t0 + n_tiles)):
                wait_read_out(pe, jobs["T_" + name] + j)

        def tile_of(xT, t):
            return lambda k: xT[:, k, t * P:(t + 1) * P]

        def pe_ada(pe):
            pe.wait_ge(consts, 6)
            pe.wait_ge(c_silu, 1)
            nc.tensor.transpose(ps(jobs["cT"])[:, 0:16], crow[0:16, 0, :], ident[0:16, 0:16]).then_inc(full(jobs["cT"]), 1)
            wait_read_out(pe, jobs["cT"])
            for n in range(13):
                if n < 12:
                    job = jobs[f"ada{n}"]
                    wait_weights(pe, tile_no[f"ada{n}"])
                    wait_weights(pe, tile_no[f"ada{n}"] + 1)
                    wait_bank_free(pe, job)
                    for k in range(KC):
                        last = mm(ps(job)[0:2, :], cT[:, k, :], wtile(tile_no[f"ada{n}"] + k // HALF)[:, k % HALF, :],
                                  k == 0, k == KC - 1)
                    last.then_inc(full(job), 1)
                if n:
                    wait_read_out(pe, jobs[f"ada{n - 1}"])
                    for w in range(2 if n - 1 < 4 else 1):
                        job = jobs[f"adab{n - 1}"] + w
                        wait_bank_free(pe, job)
                        mm(ps(job)[:, :], select[:, w, :], m_row[0:2, (n - 1) % 2, :], True, True).then_inc(full(job), 1)

        def pe_project(pe):
            pe_transpose(pe, "in", h_in, 4)
            job = jobs["lb"]
            wait_bank_free(pe, job)
            pe.wait_ge(load_gate, 64)
            nc.tensor.transpose(ps(job)[:, 0:8], lb_raw[0:8, :], ident[0:8, 0:8])
            nc.tensor.transpose(ps(job)[:, 8:12], bgk_raw[0:4, :], ident[0:4, 0:4]).then_inc(full(job), 1)
            wait_transposed(pe, "in", 0, 4)
            every = lambda k: hT[:, k, :]
            latent = lambda k: hT[:, k, L:2 * L]
            for name in ("hff", "hfb"):
                pe_feature(pe, jobs[name], tile_no[name], KC, 4, 2 * L, every, 1)
            for d in range(2):
                job = jobs["rank"] + d
                wait_bank_free(pe, job)
                for k in range(KC):
                    last = mm(ps(job)[0:RANK, :], w_rank[:, k, RANK * d:RANK * (d + 1)], hT[:, k, :], k == 0, k == KC - 1)
                last.then_inc(full(job), 1)
            for j in range(4):
                job = jobs["gla_gate"] + j
                wait_read_out(pe, jobs["rank"] + j // 2)
                wait_bank_free(pe, job)
                mm(ps(job)[:, :], gk2[0:RANK, j // 2, (j % 2) * P:(j % 2 + 1) * P], rank_act[0:RANK, j // 2, :],
                   True, True).then_inc(full(job), 1)
            for m in range(2):
                wait_weights(pe, tile_no["gqk"] + m)
            for b in range(4):
                job = jobs["gqk"] + b
                wait_bank_free(pe, job)
                cols = 2 * L if b >= 2 else L
                for k in range(KC):
                    last = mm(ps(job)[:, 0:cols], wtile(tile_no["gqk"] + k // HALF)[:, k % HALF, b * P:(b + 1) * P],
                              hT[:, k, 2 * L - cols:2 * L], k == 0, k == KC - 1)
                last.then_inc(full(job), 1)
            pe_feature(pe, jobs["hq"], tile_no["hq"], KC, 4, L, latent, 1)

            def row_major(tok):
                return lambda k: hT[:, k, tok * P:(tok + 1) * P]

            def col_major(t):
                return lambda k: hT_col[:, k, t * P:(t + 1) * P]

            pe_token(pe, jobs["hi"], tile_no["hi"], KC, [row_major(i) for i in range(4)])
            pe.wait_ge(hT_col_ready, 1)
            pe_token(pe, jobs["gv"], tile_no["gv"], KC, [row_major(0), row_major(1), col_major(0), col_major(1)])
            pe_token(pe, jobs["hg"], tile_no["hg"], KC, [row_major(2), row_major(3)])
            pe_token(pe, jobs["gg"], tile_no["gg"], KC, [col_major(0), col_major(1)])

        def pe_states(pe):
            pe.wait_ge(ctx_key, 1)
            for t in range(TT):
                for g in range(3):
                    job = jobs["keyT"] + 3 * t + g
                    wait_bank_free(pe, job)
                    for b in range(4):
                        last = nc.tensor.transpose(ps(job)[:, b * P:(b + 1) * P],
                                                   decay[:, 0, 4 * g + b, t * P:(t + 1) * P], ident[:])
                    last.then_inc(full(job), 1)
            for j in range(6):
                wait_read_out(pe, jobs["keyT"] + j)
            for name in ("hi", "gv"):
                for j in range(4):
                    wait_read_out(pe, jobs[name] + j)
            for j in range(4):
                d, gla = j % 2, j // 2
                job = jobs["state"] + j
                wait_bank_free(pe, job)
                for b in range(2 if gla else 4):
                    w = 2 * P if gla else P
                    for t in range(TT):
                        last = mm(ps(job)[:, b * w:(b + 1) * w], keyT[:, t, d * UNITS + 4 * gla + b, :],
                                  val[:, t, 512 * gla + b * w:512 * gla + (b + 1) * w], t == 0, t == TT - 1)
                last.then_inc(full(job), 1)
            pe.wait_ge(q_state_ready, 1)
            for j in range(4):
                wait_read_out(pe, jobs["state"] + j)
            for t in range(TT):
                for g, (p0, p1) in enumerate(((0, 4), (4, 6), (6, 8))):
                    job = jobs["inter"] + 3 * t + g
                    wait_bank_free(pe, job)
                    for b in range(p1 - p0):
                        u, rows = unit_rows(p0 + b)
                        for d in range(2):
                            last = mm(ps(job)[:, b * P:(b + 1) * P], q_state[rows, d * UNITS + u, t * P:(t + 1) * P],
                                      state[rows, d * UNITS + u, :], d == 0, d == 1)
                    last.then_inc(full(job), 1)

        def pe_scores(pe):
            pe.wait_ge(lvl_ready, 1)
            first, second = slice(0, P), slice(P, 2 * P)
            for j in range(4):
                job = jobs["scx"] + j
                wait_bank_free(pe, job)
                for b in range(4):
                    u, rows = unit_rows(2 * j + b // 2)
                    d = b % 2
                    ks, qs = (first, second) if d == 0 else (second, first)
                    last = mm(ps(job)[:, b * P:(b + 1) * P], lvlW[rows, d, u, ks], lvlW[rows, d, u, qs], True, True)
                last.then_inc(full(job), 1)
            for j in range(4):
                job = jobs["diag"] + j
                wait_bank_free(pe, job)
                for b in range(4):
                    u, rows = unit_rows(2 * j + b // 2)
                    t = b % 2
                    for d in range(2):
                        last = mm(ps(job)[:, b * P:(b + 1) * P], key[rows, 1, d * UNITS + u, t * P:(t + 1) * P],
                                  qry[rows, u, t * P:(t + 1) * P], d == 0, d == 1)
                last.then_inc(full(job), 1)
            for lv in range(len(LEVELS)):
                pe.wait_ge(lvl_ready, lv + 2)
                for j in range(8):
                    job = jobs[f"lvl{lv}"] + j
                    wait_bank_free(pe, job)
                    d = j // 4
                    for b in range(4):
                        u, rows = unit_rows(2 * (j % 4) + b // 2)
                        w = lvlW[rows, d, u, (b % 2) * P:(b % 2 + 1) * P]
                        last = mm(ps(job)[:, b * P:(b + 1) * P], w, w, True, True)
                    last.then_inc(full(job), 1)
            for j in range(8):
                wait_read_out(pe, jobs[f"lvl{len(LEVELS) - 1}"] + j)
            for t in range(TT):
                for g in range(2):
                    job = jobs["o"] + 2 * t + g
                    wait_bank_free(pe, job)
                    for b in range(4):
                        h = HEAD_AT.index(4 * g + b)
                        v = slice((4 * g + b) * P, (4 * g + b + 1) * P)
                        mm(ps(job)[:, b * P:(b + 1) * P], sc_in[:, h, t, :], val[:, 2 + t, v], True, False)
                        last = mm(ps(job)[:, b * P:(b + 1) * P], sc_x[:, h, 1 - t, :], val[:, 3 - t, v], False, True)
                    last.then_inc(full(job), 1)

        def pe_experts(pe):
            pe_transpose(pe, "mix", o_mix, 2)
            wait_transposed(pe, "mix", 0, 2)
            for n in range(2):
                pe_token(pe, jobs["out"] + 2 * n, tile_no[f"out{n}"], KC, [tile_of(mixT, t) for t in range(TT)])
            pe_transpose(pe, "h2", h2, 2)
            job = jobs["keys"]
            wait_bank_free(pe, job)
            pe.wait_ge(load_keys, 16)
            nc.tensor.transpose(ps(job)[:, 0:P], keys_raw[:, 0, :], ident[:])
            nc.tensor.transpose(ps(job)[:, P:2 * P], keys_raw[:, 1, :], ident[:]).then_inc(full(job), 1)
            wait_transposed(pe, "h2", 0, 2)
            for n in range(4):
                pe_feature(pe, jobs["wq"] + 2 * n, tile_no[f"wq{n}"], KC, 4, L, lambda k: h2T[:, k, :], 2)
            wait_read_out(pe, jobs["keys"])
            for j in range(8):
                wait_read_out(pe, jobs["wq"] + j)
            for t in range(TT):
                for g in range(4):
                    job = jobs["skey"] + 4 * t + g
                    wait_bank_free(pe, job)
                    for b in range(4):
                        last = mm(ps(job)[:, b * P:(b + 1) * P], qT[:, 4 * g + b, t * P:(t + 1) * P],
                                  keysT[:, b % 2, :], True, True)
                    last.then_inc(full(job), 1)

        def pe_s5(pe):
            job = jobs["s5p"]
            wait_bank_free(pe, job)
            pe.wait_ge(load_s5, 16 * 10)
            pe.wait_ge(s5_dt, 1)
            for i in range(3):
                nc.tensor.transpose(ps(job)[:, 16 * i:16 * i + 16], s5_raw[0:16, i, :], ident[0:16, 0:16])
            nc.tensor.transpose(ps(job)[:, 48:52], d_raw[0:4, :], ident[0:4, 0:4]).then_inc(full(job), 1)
            for r in range(2):
                job = jobs["CT"] + r
                wait_bank_free(pe, job)
                for b in range(4):
                    last = nc.tensor.transpose(ps(job)[:, b * P:(b + 1) * P], craw[:, r, b, :], ident[:])
                last.then_inc(full(job), 1)
            pe.wait_ge(s5_b, 1)
            for r in range(2):
                for g in range(4):
                    job = jobs["BT"] + 4 * r + g
                    wait_bank_free(pe, job)
                    for b in range(4):
                        last = nc.tensor.transpose(ps(job)[:, b * P:(b + 1) * P], Bz[:, r, 4 * g + b, :], ident[:])
                    last.then_inc(full(job), 1)
            pe_transpose(pe, "ssm", h_tok, 2)
            wait_transposed(pe, "ssm", 0, 2)
            pe_feature(pe, jobs["ssm_in"], tile_no["ssm_in"], KC, 4, L, lambda k: hT2[:, k, :], 2)
            for j in range(2):
                wait_read_out(pe, jobs["ssm_in"] + j)
            for j in range(8):
                wait_read_out(pe, jobs["BT"] + j)

            def output(j):
                a = j // 4
                if j % 4 == 0:
                    wait_bank_free(pe, jobs[f"y{a}"])
                pe.wait_ge(x_state, j + 1)
                mm(ps(jobs[f"y{a}"])[:, 0:L], Cz[:, 0, j, :], xs[:, j % 2, 0, :], j % 4 == 0, False)
                last = mm(ps(jobs[f"y{a}"])[:, 0:L], Cz[:, 1, j, :], xs[:, j % 2, 1, :], False, j % 4 == 3)
                last.then_inc(*((full(jobs[f"y{a}"]), 1) if j % 4 == 3 else (y_used, 1)))

            for j in range(NSTATE):
                job = jobs[f"bu{j}"]
                wait_bank_free(pe, job)
                for r in range(2):
                    last = mm(ps(job)[:, r * L:(r + 1) * L], BT[:, r, j, :], uT[:, j // 4, :], True, True)
                last.then_inc(full(job), 1)
                if j:
                    output(j - 1)
            output(NSTATE - 1)
            for j in range(4):
                pe.wait_ge(z_ready, j + 1)
            pe_feature(pe, jobs["glu"], tile_no["glu"], HALF, 4, L, lambda k: zT[:, k, :], 2)
            pe.wait_ge(y_ready, 1)
            for n in range(2):
                pe_token(pe, jobs["ssm_out"] + 2 * n, tile_no[f"ssm_out{n}"], HALF, [tile_of(zT, t) for t in range(TT)])

        def pe_mlp(pe, i):
            pe_transpose(pe, f"mlp{i}", h_tok, 2)
            wait_transposed(pe, f"mlp{i}", 0, 2)
            for n in range(8):
                pe_feature(pe, jobs[f"mlp{i}a"] + 2 * n, tile_no[f"mlp{i}a{n}"], KC, 4, L, lambda k: hT2[:, k, :], 2)
            for n in range(2):
                for t in range(TT):
                    wait_bank_free(pe, jobs[f"mlp{i}b"] + 2 * n + t)
                for kh in range(8):
                    tile = tile_no[f"mlp{i}b{n}"] + kh
                    wait_weights(pe, tile)
                    if n == 0:
                        pe.wait_ge(ff_ready, 16 * i + 2 * kh + 2)
                    for t in range(TT):
                        job = jobs[f"mlp{i}b"] + 2 * n + t
                        for k in range(HALF):
                            last = mm(ps(job)[:, :], ff[:, HALF * kh + k, t * P:(t + 1) * P], wtile(tile)[:, k, :],
                                      kh == 0 and k == 0, kh == 7 and k == HALF - 1)
                        if kh == 7:
                            last.then_inc(full(job), 1)
                    if kh < 7:
                        last.then_inc(w_used, 1)

        def pe_attention(pe):
            pe_transpose(pe, "att", h_tok, 2)
            wait_transposed(pe, "att", 0, 2)
            for n in range(5):
                pe_token(pe, jobs["att"] + 2 * n, tile_no[f"att{n}"], KC, [tile_of(hT2, t) for t in range(TT)],
                         min(WIDE, ATT_COLS - n * WIDE))
            for t in range(TT):
                pe.wait_ge(roped_ready, t + 1)
                blocks = [roped[:, t, 2 * i:2 * i + 2, :] for i in range(12)] + [krope[:, t, i, :] for i in range(5)]
                for g in range(5):
                    job = jobs["rT"] + 5 * t + g
                    wait_bank_free(pe, job)
                    for b, x in enumerate(blocks[4 * g:4 * g + 4]):
                        last = nc.tensor.transpose(ps(job)[:, b * P:(b + 1) * P], x, ident[:])
                    last.then_inc(full(job), 1)
            for j in range(10):
                wait_read_out(pe, jobs["rT"] + j)
            for t in range(TT):
                for g in range(4):
                    job = jobs["idx"] + 4 * t + g
                    wait_bank_free(pe, job)
                    rows = slice(64 * (g % 2), 64 * (g % 2) + 64)
                    for b in range(2):
                        last = mm(ps(job)[:, b * L:(b + 1) * L], qiT[rows, 2 * (g // 2) + b, t * P:(t + 1) * P],
                                  kTa[rows, 4, :], True, True)
                    last.then_inc(full(job), 1)
            for t in range(TT):
                for g in range(8):
                    job = jobs[f"att_s{t}"] + g
                    wait_bank_free(pe, job)
                    rows = slice(64 * (g % 2), 64 * (g % 2) + 64)
                    for b in range(2):
                        last = mm(ps(job)[:, b * L:(b + 1) * L], qTa[rows, 2 * (g // 2) + b, t * P:(t + 1) * P],
                                  kTa[rows, g // 2, :], True, True)
                    last.then_inc(full(job), 1)
            for t in range(TT):
                pe.wait_ge(prob_ready, t + 1)
                for s in range(t + 1):
                    for g in range(4):
                        job = jobs[f"pT{t}"] + 4 * s + g
                        wait_bank_free(pe, job)
                        for b in range(4):
                            last = nc.tensor.transpose(ps(job)[:, b * P:(b + 1) * P],
                                                       prob[:, t, 4 * g + b, s * P:(s + 1) * P], ident[:])
                        last.then_inc(full(job), 1)
                for j in range(4 * (t + 1)):
                    wait_read_out(pe, jobs[f"pT{t}"] + j)
                for g in range(2):
                    job = jobs[f"pv{t}"] + g
                    wait_bank_free(pe, job)
                    for b in range(8):
                        h = 8 * g + b
                        c = 1280 + HD * (h // 4)
                        for s in range(t + 1):
                            last = mm(ps(job)[:, b * HD:(b + 1) * HD], pT[:, s, h, :], proj[:, s, c:c + HD], s == 0, s == t)
                    last.then_inc(full(job), 1)
            pe_transpose(pe, "atto", o_att, 2)
            wait_transposed(pe, "atto", 0, 2)
            for n in range(2):
                pe_token(pe, jobs["att_out"] + 2 * n, tile_no[f"att_out{n}"], KC, [tile_of(hT2, t) for t in range(TT)])

        @block.tensor
        def _(pe):
            pe_ada(pe)
            pe_project(pe)
            pe_states(pe)
            pe_scores(pe)
            pe_experts(pe)
            pe_s5(pe)
            pe_mlp(pe, 0)
            pe_attention(pe)
            pe_mlp(pe, 1)

        def act_transposed(act, name, xT, n_tiles):
            for t in range(n_tiles):
                for g in range(2):
                    job = jobs["T_" + name] + 2 * t + g
                    wait_bank_full(act, job)
                    read_out(act, act.activation(xT[:, 4 * g:4 * g + 4, t * P:(t + 1) * P],
                                                 ps(job)[:, :].rearrange("p (k t) -> p k t", k=4), ACT.Copy), job)

        def norm_sqrt(act, name, scale):
            cols = dict(NORM_USES)[name]
            act.wait_ge(var_ready, norm_no[name] + 1)
            mark(act, act.activation(stat[:, 0:cols], stat[:, 0:cols], ACT.Sqrt, bias=eps[:, 0:1], scale=scale), std_ready)

        def act_ada(act):
            act.wait_ge(load_c, 32)
            mark(act, act.activation(crow[0:16, 0, :], crow[0:16, 0, :], ACT.Silu), c_silu)
            wait_bank_full(act, jobs["cT"])
            read_out(act, act.activation(cT, ps(jobs["cT"])[:, 0:16].rearrange("p (w k) -> p k w", w=2), ACT.Copy), jobs["cT"])
            act.wait_ge(consts, 6)
            norm_sqrt(act, "ln_in", 1.0)
            for n in range(12):
                s, c = n // 2, slice((n % 2) * WIDE, (n % 2 + 1) * WIDE)
                for w in range(2 if n < 4 else 1):
                    job = jobs[f"adab{n}"] + w
                    wait_bank_full(act, job)
                    dst = mod1[:, 2 * s + w, c] if n < 4 else mods[:, s - 2, c]
                    if s in (1, 4):
                        ins = act.activation(dst, ps(job)[:, :], ACT.Identity, bias=ones[:, 0:1])
                    else:
                        ins = act.activation(dst, ps(job)[:, :], ACT.Copy)
                    read_out(act, ins, job)
            act_transposed(act, "in", hT, 4)

        def act_gates(act):
            act.wait_ge(lb_sum, 1)
            mark(act, act.activation(lb_t, lb_t, ACT.Exp), lb_exp)
            act.wait_ge(lb_sum, 2)
            step(act, "act", act.activation(log_lb, log_lb, ACT.Ln, scale=2.0 ** 50))
            mark(act, act.activation(log1m_lb, one_lb, ACT.Ln), lb_log)

            def first(j):
                job = jobs["hff"] + j
                wait_bank_full(act, job)
                if j >= 2:
                    act.wait_ge(gate_done, j - 1)
                T = gate_tmp[:, j % 2, 0, :]
                step(act, "act", act.activation(T, ps(job)[:, :], ACT.Abs))
                step(act, "act", act.activation(T, T, ACT.Exp, scale=-1.0))
                mark(act, act.activation(T, T, ACT.Ln, bias=ones[:, 0:1]), gate_abs)

            def second(j):
                u = j % 4 + UNITS * (j // 4)
                wait_read_out(act, jobs["hff"] + j)
                mark(act, act.activation(key[:, :, u, :], key[:, :, u, :], ACT.Exp), gate_k)
                act.wait_ge(gate_diff, j + 1)
                T = gate_tmp[:, j % 2, 0, :]
                step(act, "act", act.activation(T, T, ACT.Abs))
                step(act, "act", act.activation(T, T, ACT.Exp, scale=-1.0))
                mark(act, act.activation(T, T, ACT.Ln, bias=ones[:, 0:1]), gate_log)

            for j in range(9):
                if j < 8:
                    first(j)
                if j:
                    second(j - 1)
            for d in range(2):
                job = jobs["rank"] + d
                wait_bank_full(act, job)
                step(act, "act", act.activation(rank_act[0:RANK, d, 0:L], ps(job)[0:RANK, 0:L], ACT.Copy))
                read_out(act, act.activation(by_cols(rank_act[0:RANK, d, L:2 * L]), by_rows(ps(job)[0:RANK, L:2 * L]),
                                             ACT.Copy), job)
            for j in range(4):
                job = jobs["gla_gate"] + j
                wait_bank_full(act, job)
                act.wait_ge(gate_done, 8 + j - 1)
                T = gate_tmp[:, j % 2, 0, :]
                step(act, "act", act.activation(T, ps(job)[:, :], ACT.Abs, bias=bgk[:, j:j + 1]))
                step(act, "act", act.activation(T, T, ACT.Exp, scale=-1.0))
                mark(act, act.activation(T, T, ACT.Ln, bias=ones[:, 0:1]), gate_abs)

        def act_project(act):
            for b in range(4):
                job = jobs["gqk"] + b
                wait_bank_full(act, job)
                if b < 2:
                    ins = act.activation(by_cols(qry[:, HG_HEADS + b, :]), by_rows(ps(job)[:, 0:L]), ACT.Copy, scale=0.125)
                else:
                    step(act, "act", act.activation(key[:, 0, HG_HEADS + b - 2, :], ps(job)[:, 0:L], ACT.Copy))
                    ins = act.activation(by_cols(key[:, 1, HG_HEADS + b - 2, :]), by_rows(ps(job)[:, L:2 * L]), ACT.Copy)
                read_out(act, ins, job)
            for b in range(4):
                job = jobs["hq"] + b
                wait_bank_full(act, job)
                read_out(act, act.activation(qry[:, b, :], ps(job)[:, 0:L], ACT.Copy), job)
            for name, c0 in (("hi", 0), ("gv", WIDE)):
                for i in range(4):
                    job = jobs[name] + i
                    wait_bank_full(act, job)
                    read_out(act, act.activation(val[:, i, c0:c0 + WIDE], ps(job)[:, :], ACT.Copy), job)
            act.wait_ge(masks_ready, 1)
            for name, c0 in (("hg", 0), ("gg", WIDE)):
                for t in range(TT):
                    job = jobs[name] + t
                    wait_bank_full(act, job)
                    read_out(act, act.activation(gate_out[:, t, c0:c0 + WIDE], ps(job)[:, :], ACT.Silu), job)

        def act_states(act):
            act.wait_ge(scans_done, 1)
            for u in range(2 * UNITS):
                ins = act.activation(decay[:, 0, u, :], decay[:, 0, u, :], ACT.Exp, bias=b_end[:, u:u + 1], scale=-1.0)
                if u < 2 * UNITS - 1:
                    step(act, "act", ins)
            mark(act, ins, ctx_exp)
            mark(act, act.activation(q_state, decay[:, 1, :, :], ACT.Exp), q_exp)
            for j in range(6):
                job = jobs["keyT"] + j
                wait_bank_full(act, job)
                g = j % 3
                read_out(act, act.activation(keyT[:, j // 3, 4 * g:4 * g + 4, :],
                                             ps(job)[:, :].rearrange("p (u c) -> p u c", u=4), ACT.Copy), job)
            for j in range(4):
                job = jobs["state"] + j
                d = j % 2
                wait_bank_full(act, job)
                if j < 2:
                    ins = act.activation(state[:, d * UNITS:d * UNITS + 4, :],
                                         ps(job)[:, :].rearrange("p (u c) -> p u c", u=4), ACT.Copy)
                else:
                    s, o = ps(job)[:, :].rearrange("p (k c) -> p k c", k=2), slice(d * UNITS + 4, d * UNITS + 6)
                    step(act, "act", act.activation(state[0:64, o, :], s[0:64, :, 0:P], ACT.Copy))
                    ins = act.activation(state[64:128, o, :], s[64:128, :, P:2 * P], ACT.Copy)
                read_out(act, ins, job)
            for t in range(TT):
                for g in range(3):
                    job = jobs["inter"] + 3 * t + g
                    wait_bank_full(act, job)
                    if g == 0:
                        o, n = o_mix[:, t, 0:WIDE].rearrange("p (h c) -> p h c", h=4), 4
                    else:
                        o, n = o_mix[:, t, WIDE:D].rearrange("p (h e c) -> p h e c", h=2, e=2)[:, :, g - 1, :], 2
                    read_out(act, act.activation(o, ps(job)[:, 0:n * P].rearrange("p (h c) -> p h c", h=n), ACT.Copy), job)

        def act_scores(act):
            def decays(i):
                act.wait_ge(lvl_diff, i + 1)
                mark(act, act.activation(lvlE, lvlE, ACT.Exp), lvl_exp)

            decays(0)
            for name, dst in (("scx", sc_x), ("diag", sc_in)):
                for j in range(4):
                    job = jobs[name] + j
                    wait_bank_full(act, job)
                    read_out(act, act.activation(dst[:, 2 * j:2 * j + 2, :, :],
                                                 ps(job)[:, :].rearrange("p (h b c) -> p h b c", h=2, b=2), ACT.Copy), job)
                if name == "scx":
                    decays(1)
            for i in range(2, len(LEVELS) + 1):
                decays(i)

        def load_row_pair(act, dst, a, b, s):
            act.dma_start(dst[:, 0, :], a.to_broadcast([P, D])).then_inc(s, 16)
            act.dma_start(dst[:, 1, :], b.to_broadcast([P, D])).then_inc(s, 16)

        def act_experts(act):
            norm_sqrt(act, "head", 1.0 / P)
            for t in range(TT):
                for g in range(2):
                    job = jobs["T_mix"] + 2 * t + g
                    wait_bank_full(act, job)
                    i = ps(job)[:, :].rearrange("p (k t) -> p k t", k=4)
                    if g == 0:
                        ins = act.activation(mixT[:, 0:4, t * P:(t + 1) * P], i, ACT.Copy)
                    else:
                        w = P // ROWS
                        for k in range(4):
                            o = mixT[:, 4 + k, :].rearrange("p (r w) -> p w r", r=ROWS)[:, t * w:(t + 1) * w, :]
                            ins = act.activation(o, i[:, k, :].rearrange("p (w r) -> p w r", r=ROWS), ACT.Copy)
                            if k < 3:
                                step(act, "act", ins)
                    read_out(act, ins, job)
            gamma, beta = A["ln_gamma"][0], A["ln_beta"][0]
            load_row_pair(act, row_a, gamma[0:1, :], beta[0:1, :], load_rows)
            act.dma_start(keys_raw, A["peer_sub_keys"][0].rearrange("s n d -> n s d")).then_inc(load_keys, 16)
            norm_sqrt(act, "post1", 1.0)
            norm_sqrt(act, "mod2", 1.0)
            act_transposed(act, "h2", h2T, 2)
            job = jobs["keys"]
            wait_bank_full(act, job)
            read_out(act, act.activation(keysT, ps(job)[:, 0:2 * P].rearrange("p (a b) -> p a b", a=2), ACT.Copy), job)
            for j in range(8):
                job = jobs["wq"] + j
                wait_bank_full(act, job)
                read_out(act, act.activation(qT[:, 2 * j:2 * j + 2, :],
                                             ps(job)[:, :].rearrange("p (a b) -> p a b", a=2), ACT.Copy), job)
            for t in range(TT):
                if t:
                    act.wait_ge(skey_used, t)
                for g in range(4):
                    job = jobs["skey"] + 4 * t + g
                    wait_bank_full(act, job)
                    read_out(act, act.activation(s_key[:, 4 * g:4 * g + 4, :],
                                                 ps(job)[:, :].rearrange("p (a b) -> p a b", a=4), ACT.Copy), job)
                act.wait_ge(best_ready, t + 1)
                mark(act, act.activation(gate_w[:, t, :], gate_w[:, t, :], ACT.Exp), soft_ready)
            load_row_pair(act, row_a, gamma[1:2, :], beta[1:2, :], load_rows)
            for t in range(TT):
                act.wait_ge(row_used, GATHERS * (t + 1))
                mark(act, act.activation(act_w[:, t, :], act_w[:, t, :], ACT.Gelu_apprx_tanh), gelu_done)

        def act_rms(act, i):
            norm_sqrt(act, f"rms{i}", 1.0 / D)

        def load_norm_pair(act, k):
            if k:
                act.wait_ge(rows_free, k)
            g = A["norm_g_2"]
            load_row_pair(act, row_b, g[k // 2, 2 * (k % 2):2 * (k % 2) + 1, :],
                          g[k // 2, 2 * (k % 2) + 1:2 * (k % 2) + 2, :], load_norm)

        def act_tail(act, name):
            for n in range(2):
                for t in range(TT):
                    job = jobs[name] + 2 * n + t
                    wait_bank_full(act, job)
                    read_out(act, act.activation(mix2[:, t, n * WIDE:(n + 1) * WIDE], ps(job)[:, :], ACT.Copy), job)

        def act_s5(act):
            norm_sqrt(act, "post2", 1.0)
            load_norm_pair(act, 0)
            act.dma_start(s5_raw[0:16, 0, :], A["ssm_lam_re_2"][0].rearrange("(j g) p -> j (g p)", g=2)).then_inc(load_s5, 16)
            act.dma_start(s5_raw[0:16, 1, :], A["ssm_lam_im_2"][0].rearrange("(j g) p -> j (g p)", g=2)).then_inc(load_s5, 16)
            act.dma_start(dt_raw[0:16, :], A["ssm_log_dt_2"][0].rearrange("(j g) -> j g", g=2)).then_inc(load_s5, 16)
            act.dma_start(d_raw[0:4, :], A["ssm_d_2"][0].rearrange("(a g) c -> a (g c)", a=4)).then_inc(load_s5, 16)
            for r, n in enumerate(("ssm_b_re_2", "ssm_b_im_2")):
                act.dma_start(braw[:, r, :, :], A[n][0].rearrange("(j g) p c -> (g p) j c", g=2)).then_inc(load_s5, 16)
            for r, n in enumerate(("ssm_c_re_2", "ssm_c_im_2")):
                for half in range(2):
                    act.dma_start(craw[:, r, :, 64 * half:64 * half + 64],
                                  A[n][0].rearrange("(a g) c p -> (g c) a p", a=4)).then_inc(load_s5, 16)
            wait_read_out(act, jobs["s5p"])
            mark(act, act.activation(S5["dt"], S5["dt"], ACT.Exp), s5_exp)
            act.wait_ge(s5_theta, 1)
            step(act, "act", act.activation(S5["mag"], S5["mag"], ACT.Exp))
            step(act, "act", act.activation(S5["sn"], S5["r"], ACT.Sin))
            mark(act, act.activation(S5["hs"], S5["r"], ACT.Sin, scale=0.5), s5_sin)
            for r in range(2):
                job = jobs["CT"] + r
                wait_bank_full(act, job)
                read_out(act, act.activation(CT[:, r, :, :], ps(job)[:, :].rearrange("p (a b) -> p a b", a=4), ACT.Copy), job)
            for r in range(2):
                for g in range(4):
                    job = jobs["BT"] + 4 * r + g
                    wait_bank_full(act, job)
                    read_out(act, act.activation(BT[:, r, 4 * g:4 * g + 4, :],
                                                 ps(job)[:, :].rearrange("p (a b) -> p a b", a=4), ACT.Copy), job)
            act_rms(act, 0)
            act_transposed(act, "ssm", hT2, 2)
            for j in range(2):
                job = jobs["ssm_in"] + j
                wait_bank_full(act, job)
                read_out(act, act.activation(uT[:, 2 * j:2 * j + 2, :],
                                             ps(job)[:, :].rearrange("p (a b) -> p a b", a=2), ACT.Copy), job)
            for a in range(4):
                wait_read_out(act, jobs[f"y{a}"])
                mark(act, act.activation(zT[:, a, :], zT[:, a, :], ACT.Gelu_apprx_tanh), z_ready)
            sg = rt.rearrange("p a b t -> p (a b) t")
            for j in range(2):
                job = jobs["glu"] + j
                wait_bank_full(act, job)
                read_out(act, act.activation(sg[:, 2 * j:2 * j + 2, :],
                                             ps(job)[:, :].rearrange("p (a b) -> p a b", a=2), ACT.Sigmoid), job)
            act_tail(act, "ssm_out")
            act_rms(act, 1)
            load_norm_pair(act, 1)

        def act_mlp(act, i):
            act_rms(act, 4 * i + 2)
            act_transposed(act, f"mlp{i}", hT2, 2)
            for j in range(16):
                job = jobs[f"mlp{i}a"] + j
                wait_bank_full(act, job)
                read_out(act, act.activation(ff[:, 2 * j:2 * j + 2, :],
                                             ps(job)[:, :].rearrange("p (a b) -> p a b", a=2), ACT.Relu), job)
            act_tail(act, f"mlp{i}b")
            act_rms(act, 4 * i + 3)

        def act_attention(act):
            load_norm_pair(act, 2)
            act_rms(act, 4)
            act_transposed(act, "att", hT2, 2)
            act.dma_start(rope, A["rope_table"].rearrange("(t p) c d -> p t c d", p=P)).then_inc(load_rope, 16)
            for n in range(5):
                cols = min(WIDE, ATT_COLS - n * WIDE)
                for t in range(TT):
                    job = jobs["att"] + 2 * n + t
                    wait_bank_full(act, job)
                    read_out(act, act.activation(proj[:, t, n * WIDE:n * WIDE + cols], ps(job)[:, 0:cols], ACT.Copy), job)
            for t in range(TT):
                dst = [qTa[:, 0:4], qTa[:, 4:8], qiT[:, 0:4], kTa[:, 0:4], kTa[:, 4:5]]
                for g in range(5):
                    job = jobs["rT"] + 5 * t + g
                    n = 4 if g < 4 else 1
                    wait_bank_full(act, job)
                    read_out(act, act.activation(dst[g][:, :, t * P:(t + 1) * P],
                                                 ps(job)[:, 0:n * P].rearrange("p (a b) -> p a b", a=n), ACT.Copy), job)
            for j in range(8):
                job = jobs["idx"] + j
                wait_bank_full(act, job)
                if j >= 2:
                    act.wait_ge(rel_used, j - 1)
                read_out(act, act.activation(rel[:, j % 2, :, :], ps(job)[:, :].rearrange("p (a b) -> p a b", a=2),
                                             ACT.Relu), job)
            for t in range(TT):
                act.wait_ge(logits_ready, t + 1)
                for h in range(N_HEADS):
                    ins = act.activation(prob[:, t, h, :], prob[:, t, h, :], ACT.Exp, bias=mx16[:, t, h:h + 1],
                                         accum_out=sum16[:, t, h:h + 1])
                    if h < N_HEADS - 1:
                        step(act, "act", ins)
                mark(act, ins, prob_ready)
            for t in range(TT):
                for s in range(t + 1):
                    for g in range(4):
                        job = jobs[f"pT{t}"] + 4 * s + g
                        wait_bank_full(act, job)
                        read_out(act, act.activation(pT[:, s, 4 * g:4 * g + 4, :],
                                                     ps(job)[:, :].rearrange("p (a b) -> p a b", a=4), ACT.Copy), job)
            act_transposed(act, "atto", hT2, 2)
            act_tail(act, "att_out")
            act_rms(act, 5)
            load_norm_pair(act, 3)

        @block.scalar
        def _(act):
            act.dma_start(crow[0:8, 0, :], A["c"][0].rearrange("(k p) -> k p", p=P)).then_inc(load_c, 16)
            act.dma_start(crow[8:16, 0, :], A["c_ctx"].rearrange("(k p) -> k p", p=P)).then_inc(load_c, 16)
            act.dma_start(x_ctx, A["ctx"][0].rearrange("(t p) d -> p t d", p=P)).then_inc(load_x, 16)
            act.dma_start(x_lat, A["x"][0].rearrange("(t p) d -> p t d", p=P)).then_inc(load_x, 16)
            act.dma_start(b_ada, A["b_ada"].to_broadcast([2, 6 * D])).then_inc(load_bada, 16)
            act.dma_start(w_rank, w_in[:, 4096:4128].rearrange("(k p) n -> p k n", p=P)).then_inc(load_gate, 16)
            act.dma_start(gk2[0:RANK, :, :], A["w_gk2"][0].rearrange("d r c -> r d c")).then_inc(load_gate, 16)
            act.dma_start(bgk_raw[0:4, :], A["b_gk"][0].rearrange("d (j p) -> (d j) p", p=P)).then_inc(load_gate, 16)
            act.dma_start(lb_raw[0:8, :], A["hg_lower_bounds"][:, 0, :].rearrange("d (j p) -> (d j) p", p=P)).then_inc(load_gate, 16)
            act.dma_start(gain[:, 0, :], A["hg_norm"].to_broadcast([P, P])).then_inc(load_gain, 16)
            act.dma_start(gain[:, 1, :], A["gla_norm"].to_broadcast([P, P])).then_inc(load_gain, 16)
            act_ada(act)
            act_gates(act)
            act_project(act)
            act_states(act)
            act_scores(act)
            act_experts(act)
            act_s5(act)
            act_mlp(act, 0)
            act_attention(act)
            act_mlp(act, 1)

        @block.vector
        def _(dve):
            def do(ins):
                step(dve, "dve", ins)

            def tt(o, a, b, op):
                return dve.tensor_tensor(o, a, b, op)

            def invert_std(name):
                cols = dict(NORM_USES)[name]
                dve.wait_ge(std_ready, norm_no[name] + 1)
                do(dve.reciprocal(stat[:, 0:cols], stat[:, 0:cols]))

            def layer_stats(tiles):
                for i, x in enumerate(tiles):
                    do(dve.bn_stats(stat[:, 24:30], x[:, 0:512]))
                    do(dve.bn_stats(stat[:, 30:36], x[:, 512:1024]))
                    do(dve.bn_aggr(stat[:, 40 + 2 * i:42 + 2 * i], stat[:, 24:36].rearrange("p (a b) -> p a b", a=2)))
                    ins = dve.tensor_copy(stat[:, i:i + 1], stat[:, 41 + 2 * i:42 + 2 * i])
                    if i < len(tiles) - 1:
                        do(ins)
                mark(dve, ins, var_ready)

            def normalized(o, x, i):
                return dve.tensor_scalar(o, x, stat[:, 40 + 2 * i:41 + 2 * i], stat[:, i:i + 1], ALU.subtract, ALU.mult)

            def square_sums(tiles, junk):
                for t, x in enumerate(tiles):
                    ins = dve.scalar_tensor_tensor(out=junk[:, t, :], in0=x, scalar=1.0, in1=x, op0=ALU.mult,
                                                   op1=ALU.mult, accum_out=stat[:, t:t + 1])
                    if t == 0:
                        do(ins)
                mark(dve, ins, var_ready)

            dve.wait_ge(consts, 6)
            do(tt(it_x, it_t, it_s, ALU.bitwise_xor))
            do(dve.tensor_copy(it_f, it_x))
            for d, op in enumerate((ALU.is_ge, ALU.is_le)):
                do(tt(it_g, it_s, it_t, op))
                do(dve.scalar_tensor_tensor(out=it_g, in0=it_g, scalar=1000.0, in1=it_f, op0=ALU.mult, op1=ALU.add))
                for i, h in enumerate(LEVELS):
                    ins = dve.tensor_scalar(level_mask[:, d, i, :], it_g, float(2 * h), None, ALU.is_lt)
                    if (d, i) != (1, len(LEVELS) - 1):
                        do(ins)
            mark(dve, ins, masks_ready)

            dve.wait_ge(load_x, 32)
            toks = [x_ctx[:, 0, :], x_ctx[:, 1, :], x_lat[:, 0, :], x_lat[:, 1, :]]
            layer_stats(toks)
            invert_std("ln_in")
            dve.wait_ge(load_bada, 16)

            def biased_row(n):
                job = jobs[f"ada{n}"]
                wait_bank_full(dve, job)
                if n >= 2:
                    wait_bank_full(dve, jobs[f"adab{n - 2}"] + (1 if n - 2 < 4 else 0))
                ins = tt(m_row[0:2, n % 2, :], ps(job)[0:2, :], b_ada[:, n * WIDE:(n + 1) * WIDE], ALU.add)
                read_out(dve, ins, job)

            def modulated(i):
                w = 1 if i < 2 else 0
                do(normalized(h_in[:, i, :], toks[i], i))
                do(tt(h_in[:, i, :], h_in[:, i, :], mod1[:, 2 + w, :], ALU.mult))
                mark(dve, tt(h_in[:, i, :], h_in[:, i, :], mod1[:, w, :], ALU.add), tok_ready)

            for n in range(12):
                biased_row(n)
                if 4 <= n < 8:
                    if n == 4:
                        wait_read_out(dve, jobs["adab3"] + 1)
                        for k in range(4):
                            for w in range(2):
                                wait_read_out(dve, jobs[f"adab{k}"] + w)
                    modulated(n - 4)

            job = jobs["lb"]
            wait_bank_full(dve, job)
            do(dve.tensor_copy(lb, ps(job)[:, 0:8]))
            read_out(dve, dve.tensor_copy(bgk, ps(job)[:, 8:12]), job)
            mark(dve, tt(lb_t, lb, lb, ALU.subtract), lb_sum)
            dve.wait_ge(lb_exp, 1)
            do(dve.reciprocal(lb, lb_t))
            do(tt(lb_t, lb, lb_t, ALU.mult))
            do(tt(lb, lb_t, lb_t, ALU.subtract))
            do(dve.tensor_scalar(lb, lb, 0.0, 1.0 - 1e-6, ALU.max, ALU.min))
            do(dve.tensor_scalar(one_lb, lb, -1.0, 1.0, ALU.mult, ALU.add))
            mark(dve, dve.tensor_scalar(log_lb, lb, 1e-30, None, ALU.max), lb_sum)
            dve.wait_ge(lb_log, 1)
            do(dve.tensor_scalar(log_lb, log_lb, -50.0 * 0.6931471805599453, None, ALU.add))

            def first(j):
                u = j % 4 + UNITS * (j // 4)
                job = jobs["hff"] + j
                T, S = gate_tmp[:, j % 2, 0, :], gate_tmp[:, j % 2, 1, :]
                wait_bank_full(dve, job)
                dve.wait_ge(gate_abs, j + 1)
                do(dve.scalar_tensor_tensor(out=S, in0=ps(job)[:, :], scalar=0.0, in1=T, op0=ALU.min, op1=ALU.subtract))
                read_out(dve, tt(key[:, :, u, :], S.rearrange("p (s t) -> p s t", s=2),
                                 ps(job)[:, :].rearrange("p (s t) -> p s t", s=2), ALU.subtract), job)
                do(dve.tensor_scalar(S, S, log1m_lb[:, j:j + 1], None, ALU.add))
                mark(dve, dve.tensor_scalar(T, S, log_lb[:, j:j + 1], None, ALU.subtract), gate_diff)

            def second(j):
                u = j % 4 + UNITS * (j // 4)
                T, S = gate_tmp[:, j % 2, 0, :], gate_tmp[:, j % 2, 1, :]
                dve.wait_ge(gate_k, j + 1)
                do(dve.tensor_scalar(key[:, :, u, :], key[:, :, u, :], one_lb[:, j:j + 1], None, ALU.mult))
                dve.wait_ge(gate_log, j + 1)
                mark(dve, dve.scalar_tensor_tensor(out=decay[:, :, u, :], in0=S.rearrange("p (s t) -> p s t", s=2),
                                                   scalar=log_lb[:, j:j + 1], in1=T.rearrange("p (s t) -> p s t", s=2),
                                                   op0=ALU.max, op1=ALU.add), gate_done)

            for j in range(9):
                if j < 8:
                    first(j)
                if j:
                    second(j - 1)
            for j in range(4):
                u = UNITS * (j // 2) + HG_HEADS + j % 2
                job = jobs["gla_gate"] + j
                T, S = gate_tmp[:, j % 2, 0, :], gate_tmp[:, j % 2, 1, :]
                wait_bank_full(dve, job)
                dve.wait_ge(gate_abs, 8 + j + 1)
                read_out(dve, dve.tensor_scalar(S, ps(job)[:, :], bgk[:, j:j + 1], 0.0, ALU.add, ALU.min), job)
                do(tt(S, S, T, ALU.subtract))
                mark(dve, dve.tensor_scalar(decay[:, :, u, :], S.rearrange("p (s t) -> p s t", s=2), 1.0 / 16.0, None,
                                            ALU.mult), gate_done)
            for u in range(2 * UNITS):
                for s in range(2):
                    a = decay[:, s, u, :] if u < UNITS else decay[:, s, u, ::-1]
                    do(dve.tensor_tensor_scan(a, ones[:, :], a, 0.0, ALU.mult, ALU.add))
            do(dve.tensor_copy(b_end[:, 0:UNITS], decay[:, 0, 0:UNITS, L - 1]))
            mark(dve, dve.tensor_copy(b_end[:, UNITS:2 * UNITS], decay[:, 0, UNITS:2 * UNITS, 0]), scans_done)
            for b in (2, 3):
                wait_read_out(dve, jobs["gqk"] + b)
            do(dve.tensor_copy(key[:, :, UNITS + HG_HEADS:2 * UNITS, :], key[:, :, HG_HEADS:UNITS, :]))
            dve.wait_ge(ctx_exp, 1)
            mark(dve, tt(decay[:, 0, :, :], decay[:, 0, :, :], key[:, 0, :, :], ALU.mult), ctx_key)

            bL = decay[:, 1, :, :].rearrange("p u t -> p (u t)")
            kL = key[:, 1, :, :].rearrange("p u t -> p (u t)")
            qL = qry.rearrange("p u t -> p (u t)")
            EL = lvlE.rearrange("p d u t -> p (d u t)")
            WL = lvlW.rearrange("p d u t -> p (d u t)")
            span = UNITS * L

            def halves(flat, d, h):
                return flat[:, d * span:(d + 1) * span].rearrange("p (n c h) -> p n c h", c=2, h=h)

            def exponents(i, h):
                for d in range(2):
                    b, e = halves(bL, d, h), halves(EL, d, h)
                    n = span // (2 * h)
                    seam = (b[:, :, 0, h - 1:h] if d == 0 else b[:, :, 1, 0:1]).to_broadcast([P, n, h])
                    near, far = (0, 1) if d == 0 else (1, 0)
                    do(tt(e[:, :, near, :], seam, b[:, :, near, :], ALU.subtract))
                    ins = tt(e[:, :, far, :], b[:, :, far, :], seam, ALU.subtract)
                    if d == 0:
                        do(ins)
                mark(dve, ins, lvl_diff)

            def decayed(i, h):
                dve.wait_ge(lvl_exp, i + 1)
                for d in range(2):
                    w, e, k, q = halves(WL, d, h), halves(EL, d, h), halves(kL, d, h), halves(qL, 0, h)
                    near, far = (0, 1) if d == 0 else (1, 0)
                    do(tt(w[:, :, near, :], e[:, :, near, :], k[:, :, near, :], ALU.mult))
                    ins = tt(w[:, :, far, :], e[:, :, far, :], q[:, :, far, :], ALU.mult)
                    if d == 0:
                        do(ins)
                mark(dve, ins, lvl_ready)

            levels = [P] + LEVELS
            exponents_after = lambda i: exponents(i + 1, levels[i + 1]) if i + 1 < len(levels) else None
            dve.wait_ge(q_exp, 1)
            for b in range(2):
                wait_read_out(dve, jobs["gqk"] + b)
            for b in range(4):
                wait_read_out(dve, jobs["hq"] + b)
            do(tt(q_state[:, 0:UNITS, :], q_state[:, 0:UNITS, :], qry[:, :, :], ALU.mult))
            mark(dve, tt(q_state[:, UNITS:, :], q_state[:, UNITS:, :], qry[:, :, :], ALU.mult), q_state_ready)
            wait_bank_full(dve, jobs["gg"] + 1)
            exponents(0, P)
            wait_bank_full(dve, jobs["state"] + 3)
            decayed(0, P)
            exponents_after(0)
            for i, h in enumerate(LEVELS):
                if i == 0:
                    wait_bank_full(dve, jobs["scx"] + 3)
                decayed(i + 1, h)
                exponents_after(i + 1)
                if i == 0:
                    for j in range(4):
                        wait_read_out(dve, jobs["diag"] + j)
                for j in range(8):
                    job = jobs[f"lvl{i}"] + j
                    wait_bank_full(dve, job)
                    m = level_mask[:, j // 4, i:i + 1, :].to_broadcast([P, 4, P])
                    dst = sc_in[:, 2 * (j % 4):2 * (j % 4) + 2, :, :].rearrange("p h t c -> p (h t) c")
                    read_out(dve, dve.copy_predicated(dst, m, ps(job)[:, :].rearrange("p (b c) -> p b c", b=4)), job)

            for t in range(TT):
                for g in range(2):
                    job = jobs["o"] + 2 * t + g
                    wait_bank_full(dve, job)
                    o = o_mix[:, t, g * WIDE:(g + 1) * WIDE]
                    if t == 0 and g == 0:
                        for j in range(6):
                            wait_read_out(dve, jobs["inter"] + j)
                    read_out(dve, tt(o, ps(job)[:, :], o, ALU.add), job)
            for t in range(TT):
                do(tt(sq_tmp[:, t, :], o_mix[:, t, :], o_mix[:, t, :], ALU.mult))
                ins = dve.tensor_reduce(stat[:, HEADS * t:HEADS * (t + 1)],
                                        sq_tmp[:, t, :].rearrange("p (h c) -> p h c", h=HEADS), AX_X, ALU.add)
                if t == 0:
                    do(ins)
            mark(dve, ins, var_ready)
            invert_std("head")
            dve.wait_ge(load_gain, 32)
            for name in ("hg", "gg"):
                for j in range(2):
                    wait_read_out(dve, jobs[name] + j)
            for t in range(TT):
                o = o_mix[:, t, :].rearrange("p (h c) -> p h c", h=HEADS)
                do(tt(o, o, stat[:, HEADS * t:HEADS * (t + 1)].unsqueeze(2).to_broadcast([P, HEADS, P]), ALU.mult))
                for g in range(2):
                    do(tt(o[:, 4 * g:4 * g + 4, :], o[:, 4 * g:4 * g + 4, :], gain[:, g:g + 1, :].to_broadcast([P, 4, P]), ALU.mult))
                mark(dve, tt(o_mix[:, t, :], o_mix[:, t, :], gate_out[:, t, :], ALU.mult), tok_ready)

            for n in range(2):
                c = slice(n * WIDE, (n + 1) * WIDE)
                for t in range(TT):
                    job = jobs["out"] + 2 * n + t
                    wait_bank_full(dve, job)
                    read_out(dve, tt(sq_tmp[:, t, c], ps(job)[:, :], mods[:, 0, c], ALU.mult), job)
                    do(dve.scalar_tensor_tensor(out=x_lat[:, t, c], in0=x_lat[:, t, c], scalar=ALPHA,
                                                in1=sq_tmp[:, t, c], op0=ALU.mult, op1=ALU.add))

            def scaled_norm(name, load_count):
                layer_stats([x_lat[:, t, :] for t in range(TT)])
                invert_std(name)
                dve.wait_ge(load_rows, load_count)
                for t in range(TT):
                    do(normalized(x_lat[:, t, :], x_lat[:, t, :], t))
                    do(tt(x_lat[:, t, :], x_lat[:, t, :], row_a[:, 0, :], ALU.mult))
                    do(tt(x_lat[:, t, :], x_lat[:, t, :], row_a[:, 1, :], ALU.add))

            scaled_norm("post1", 32)
            layer_stats([x_lat[:, t, :] for t in range(TT)])
            invert_std("mod2")
            for t in range(TT):
                do(normalized(h2[:, t, :], x_lat[:, t, :], t))
                do(tt(h2[:, t, :], h2[:, t, :], mods[:, 2, :], ALU.mult))
                mark(dve, tt(h2[:, t, :], h2[:, t, :], mods[:, 1, :], ALU.add), tok_ready)

            dve.wait_ge(consts, 6)
            do(tt(iota_f, ones[:, 0:TOPK], ones[:, 0:TOPK], ALU.subtract))
            do(dve.tensor_tensor_scan(iota_f, ones[:, 0:TOPK], ones[:, 0:TOPK], -1.0, ALU.mult, ALU.add))
            for t in range(TT):
                for g in range(4):
                    wait_read_out(dve, jobs["skey"] + 4 * t + g)

                def best16(values, work, v, i):
                    do(dve.max(v[:, 0:8], values))
                    do(dve.max_index(i[:, 0:8], v[:, 0:8], values))
                    do(dve.match_replace(work, v[:, 0:8], values, -3.0e38))
                    do(dve.max(v[:, 8:16], work))
                    return dve.max_index(i[:, 8:16], v[:, 8:16], work)

                for b in range(16):
                    ins = best16(s_key[:, b, :], s_work, top_v[:, b, :], top_i[:, b, :])
                    if b < 15:
                        do(ins)
                mark(dve, ins, skey_used)
                do(dve.tensor_copy(top_f, top_i))
                v = top_v.rearrange("p (h c) i -> p h c i", c=2)
                f = top_f.rearrange("p (h c) i -> p h c i", c=2)
                full4 = [P, PEER_HEADS, TOPK, TOPK]
                do(tt(cand.rearrange("p h (i j) -> p h i j", i=TOPK), v[:, :, 0, :].unsqueeze(3).to_broadcast(full4),
                      v[:, :, 1, :].unsqueeze(2).to_broadcast(full4), ALU.add))
                for h in range(PEER_HEADS):
                    do(best16(cand[:, h, :], c_work, best_v[:, h, :], best_p[:, h, :]))
                for half in range(2):
                    if half == 0:
                        do(dve.tensor_scalar(part_i, best_p, 4, None, ALU.logical_shift_right))
                    else:
                        do(dve.tensor_scalar(part_i, best_p, 15, None, ALU.bitwise_and))
                    do(dve.tensor_copy(part_f, part_i))
                    do(tt(onehot, part_f.unsqueeze(3).to_broadcast(full4),
                          iota_f.unsqueeze(1).unsqueeze(1).to_broadcast(full4), ALU.is_equal))
                    do(tt(onehot, onehot, f[:, :, half, :].unsqueeze(2).to_broadcast(full4), ALU.mult))
                    do(dve.tensor_reduce(pick[:, half, :].rearrange("p (h k) -> p h k", h=PEER_HEADS), onehot, AX_X, ALU.add))
                do(dve.scalar_tensor_tensor(out=pick[:, 0, :], in0=pick[:, 0, :], scalar=float(NKEYS), in1=pick[:, 1, :],
                                            op0=ALU.mult, op1=ALU.add))
                mark(dve, dve.tensor_copy(rows_i[:, t, :], pick[:, 0, :]), rows_ready)
                gw = gate_w[:, t, :].rearrange("p (h k) -> p h k", h=PEER_HEADS)
                mark(dve, tt(gw, best_v, best_v[:, :, 0:1].to_broadcast([P, PEER_HEADS, TOPK]), ALU.subtract), best_ready)
                dve.wait_ge(soft_ready, t + 1)
                do(dve.tensor_reduce(sm8[:, 0, :], gw, AX_X, ALU.add))
                do(dve.reciprocal(sm8[:, 1, :], sm8[:, 0, :]))
                do(tt(gw, gw, sm8[:, 1, :].unsqueeze(2).to_broadcast([P, PEER_HEADS, TOPK]), ALU.mult))

            do(dve.memset(y_acc, 0.0))
            per_row = 16 // GSLOTS
            for t in range(TT):
                base = t * GATHERS
                with dve.Fori(0, GATHERS // GSLOTS) as turn:
                    i = turn * GSLOTS
                    for s in range(GSLOTS):
                        dve.wait_ge(gathered[s], i * per_row + (base * per_row + 16))
                        dve.scalar_tensor_tensor(out=gath[:, s, :], in0=gath[:, s, :], scalar=1.0, in1=h2[:, t, :],
                                                 op0=ALU.mult, op1=ALU.mult,
                                                 accum_out=act_w[:, t, bass.ds(i + s, 1)]).then_inc(row_used, 1)
            for t in range(TT):
                dve.wait_ge(gelu_done, t + 1)
                do(tt(act_w[:, t, :], act_w[:, t, :], gate_w[:, t, :], ALU.mult))
            for t in range(TT):
                base = (TT + t) * GATHERS
                with dve.Fori(0, GATHERS // GSLOTS) as turn:
                    i = turn * GSLOTS
                    for s in range(GSLOTS):
                        dve.wait_ge(gathered[s], i * per_row + (base * per_row + 16))
                        dve.wait_ge(row_used, i + (base + s))
                        dve.scalar_tensor_tensor(out=y_acc[:, t, :], in0=gath[:, s, :],
                                                 scalar=act_w[:, t, bass.ds(i + s, 1)], in1=y_acc[:, t, :],
                                                 op0=ALU.mult, op1=ALU.add).then_inc(row_used, 1)
            dve.wait_ge(row_used, 2 * TT * GATHERS)
            for t in range(TT):
                do(tt(y_acc[:, t, :], y_acc[:, t, :], mods[:, 3, :], ALU.mult))
                do(dve.scalar_tensor_tensor(out=x_lat[:, t, :], in0=x_lat[:, t, :], scalar=ALPHA, in1=y_acc[:, t, :],
                                            op0=ALU.mult, op1=ALU.add))
            scaled_norm("post2", 64)

            def pre_norm(i, row):
                square_sums([x_lat[:, t, :] for t in range(TT)], h_tok)
                invert_std(f"rms{i}")
                dve.wait_ge(load_norm, 32 * (i // 2 + 1))
                for t in range(TT):
                    mark(dve, dve.scalar_tensor_tensor(out=h_tok[:, t, :], in0=x_lat[:, t, :], scalar=stat[:, t:t + 1],
                                                       in1=row_b[:, row, :], op0=ALU.mult, op1=ALU.mult), tok_ready)

            def post_norm(i, row, name):
                for j in range(4):
                    wait_read_out(dve, jobs[name] + j)
                square_sums([mix2[:, t, :] for t in range(TT)], h_tok)
                invert_std(f"rms{i}")
                for t in range(TT):
                    ins = dve.scalar_tensor_tensor(out=mix2[:, t, :], in0=mix2[:, t, :], scalar=stat[:, t:t + 1],
                                                   in1=row_b[:, row, :], op0=ALU.mult, op1=ALU.mult)
                    if t == 0:
                        do(ins)
                mark(dve, ins, rows_free)
                for t in range(TT):
                    ins = tt(x_lat[:, t, :], x_lat[:, t, :], mix2[:, t, :], ALU.add)
                    if i < 7:
                        do(ins)
                    elif t == 0:
                        do(ins)
                    else:
                        mark(dve, ins, out_ready)

            s = S5
            dve.wait_ge(load_s5, 16 * 10)
            mark(dve, dve.tensor_copy(s5_raw[0:16, 2, :].rearrange("p (g n) -> p g n", g=2),
                                      dt_raw[0:16, :].unsqueeze(2).to_broadcast([16, 2, 64])), s5_dt)
            job = jobs["s5p"]
            wait_bank_full(dve, job)
            do(dve.tensor_copy(small[:, 0:48], ps(job)[:, 0:48]))
            do(dve.tensor_copy(d_col, ps(job)[:, 48:52]))
            read_out(dve, dve.tensor_copy(s["t1"], ps(job)[:, 32:48]), job)
            dve.wait_ge(s5_exp, 1)
            do(tt(s["mag"], s["lr"], s["dt"], ALU.mult))
            do(tt(s["th"], s["li"], s["dt"], ALU.mult))
            magic = 12582912.0
            do(dve.tensor_scalar(s["kk"], s["th"], 1.0 / (2 * pi), magic, ALU.mult, ALU.add))
            do(dve.tensor_scalar(s["kk"], s["kk"], magic, None, ALU.subtract))
            do(dve.scalar_tensor_tensor(out=s["r"], in0=s["kk"], scalar=-6.28125, in1=s["th"], op0=ALU.mult, op1=ALU.add))
            do(dve.scalar_tensor_tensor(out=s["r"], in0=s["kk"], scalar=-(2 * pi - 6.28125), in1=s["r"], op0=ALU.mult, op1=ALU.add))
            ins = dve.tensor_scalar(s["r"], s["r"], 3.1415925, -3.1415925, ALU.min, ALU.max)
            mark(dve, ins, s5_theta)
            dve.wait_ge(s5_sin, 1)
            do(tt(s["cs"], s["hs"], s["hs"], ALU.mult))
            do(dve.tensor_scalar(s["cs"], s["cs"], -2.0, 1.0, ALU.mult, ALU.add))
            do(tt(s["t1"], s["cs"], s["cs"], ALU.mult))
            do(tt(s["t2"], s["sn"], s["sn"], ALU.mult))
            do(tt(s["t1"], s["t1"], s["t2"], ALU.add))
            do(dve.tensor_scalar(s["t1"], s["t1"], -0.5, 1.5, ALU.mult, ALU.add))
            do(tt(s["cs"], s["cs"], s["t1"], ALU.mult))
            do(tt(s["sn"], s["sn"], s["t1"], ALU.mult))
            do(tt(s["ar"], s["mag"], s["cs"], ALU.mult))
            do(tt(s["ai"], s["mag"], s["sn"], ALU.mult))
            do(dve.tensor_scalar(s["nr"], s["ar"], -1.0, None, ALU.add))
            do(tt(s["t1"], s["lr"], s["lr"], ALU.mult))
            do(tt(s["t2"], s["li"], s["li"], ALU.mult))
            do(tt(s["den"], s["t1"], s["t2"], ALU.add))
            do(dve.reciprocal(s["den"], s["den"]))
            do(tt(s["t1"], s["nr"], s["lr"], ALU.mult))
            do(tt(s["t2"], s["ai"], s["li"], ALU.mult))
            do(tt(s["fr"], s["t1"], s["t2"], ALU.add))
            do(tt(s["fr"], s["fr"], s["den"], ALU.mult))
            do(tt(s["t1"], s["ai"], s["lr"], ALU.mult))
            do(tt(s["t2"], s["nr"], s["li"], ALU.mult))
            do(tt(s["fi"], s["t1"], s["t2"], ALU.subtract))
            do(tt(s["fi"], s["fi"], s["den"], ALU.mult))
            wide = [P, NSTATE, 16]
            fr, fi = s["fr"].unsqueeze(2).to_broadcast(wide), s["fi"].unsqueeze(2).to_broadcast(wide)
            tmp = er[:, 0, :].rearrange("p (j c) -> p j c", j=NSTATE)
            do(tt(bbar[:, 0, :, :], braw[:, 0, :, :], fr, ALU.mult))
            do(tt(tmp, braw[:, 1, :, :], fi, ALU.mult))
            do(tt(bbar[:, 0, :, :], bbar[:, 0, :, :], tmp, ALU.subtract))
            do(tt(bbar[:, 1, :, :], braw[:, 1, :, :], fr, ALU.mult))
            do(tt(tmp, braw[:, 0, :, :], fi, ALU.mult))
            do(tt(bbar[:, 1, :, :], bbar[:, 1, :, :], tmp, ALU.add))
            do(dve.memset(Bz, 0.0))
            do(dve.memset(Cz, 0.0))
            for r in range(2):
                for g in range(2):
                    for q in range(4):
                        rows, c = slice(64 * g, 64 * g + 64), slice(32 * q + 16 * g, 32 * q + 16 * g + 16)
                        o = Bz[rows, r, :, :].rearrange("p (a q) c -> p a q c", q=4)[:, :, q, c]
                        i = bbar[rows, r, :, :].rearrange("p (a q) c -> p a q c", q=4)[:, :, q, :]
                        ins = dve.tensor_copy(o, i)
                        if (r, g, q) != (1, 1, 3):
                            do(ins)
            mark(dve, ins, s5_b)
            for r in range(2):
                wait_read_out(dve, jobs["CT"] + r)
                for g in range(2):
                    for q in range(4):
                        rows, c = slice(64 * g, 64 * g + 64), slice(32 * q + 16 * g, 32 * q + 16 * g + 16)
                        o = Cz[rows, r, :, :].rearrange("p (a q) c -> p a q c", q=4)[:, :, q, c]
                        do(dve.tensor_scalar(o, CT[rows, r, :, c], 1.0 - 2.0 * r, None, ALU.mult))
            do(dve.memset(er[:, :, 0:1], 1.0))
            do(dve.memset(ei[:, :, 0:1], 0.0))
            do(dve.tensor_copy(s["pr"], s["cs"]))
            do(dve.tensor_copy(s["pi"], s["sn"]))
            scratch = arena[:, 35840:35840 + 2048]
            n = 1
            while n < L:
                sh = [P, NSTATE, n]
                pr, pi_ = s["pr"].unsqueeze(2).to_broadcast(sh), s["pi"].unsqueeze(2).to_broadcast(sh)
                e0, f0, e1, f1 = er[:, :, 0:n], ei[:, :, 0:n], er[:, :, n:2 * n], ei[:, :, n:2 * n]
                tmp = scratch[:, 0:NSTATE * n].rearrange("p (j t) -> p j t", j=NSTATE)
                do(tt(e1, e0, pr, ALU.mult))
                do(tt(tmp, f0, pi_, ALU.mult))
                do(tt(e1, e1, tmp, ALU.subtract))
                do(tt(f1, f0, pr, ALU.mult))
                do(tt(tmp, e0, pi_, ALU.mult))
                do(tt(f1, f1, tmp, ALU.add))
                do(tt(s["qr"], s["pr"], s["pr"], ALU.mult))
                do(tt(s["qi"], s["pi"], s["pi"], ALU.mult))
                do(tt(s["t1"], s["pr"], s["pi"], ALU.mult))
                do(tt(s["pr"], s["qr"], s["qi"], ALU.subtract))
                do(dve.tensor_scalar(s["pi"], s["t1"], 2.0, None, ALU.mult))
                n *= 2
            pre_norm(0, 0)

            def s5_out(a):
                job = jobs[f"y{a}"]
                wait_bank_full(dve, job)
                ins = dve.scalar_tensor_tensor(out=zT[:, a, :], in0=uT[:, a, :], scalar=d_col[:, a:a + 1],
                                               in1=ps(job)[:, 0:L], op0=ALU.mult, op1=ALU.add)
                read_out(dve, ins, job)

            for j in range(2):
                wait_read_out(dve, jobs["ssm_in"] + j)
            for j in range(NSTATE):
                job = jobs[f"bu{j}"]
                X = xs[:, j % 2, :, :]
                E_ = er[:, j:j + 1, :].to_broadcast([P, 2, L])
                F_ = ei[:, j:j + 1, :].to_broadcast([P, 2, L])
                wait_bank_full(dve, job)
                b = ps(job)[:, :].rearrange("p (r t) -> p r t", r=2)
                do(tt(rt[:, 0, :, :], b, E_, ALU.mult))
                read_out(dve, tt(rt[:, 1, :, :], b, F_, ALU.mult), job)
                if j >= 2:
                    if (j - 2) % 4 == 3:
                        wait_bank_full(dve, jobs[f"y{(j - 2) // 4}"])
                    else:
                        dve.wait_ge(y_used, j - 1 - (j - 2) // 4)
                do(tt(X[:, 0, :], rt[:, 0, 0, :], rt[:, 1, 1, :], ALU.add))
                do(tt(X[:, 1, :], rt[:, 0, 1, :], rt[:, 1, 0, :], ALU.subtract))
                r_ = s["mag"][:, j:j + 1].to_broadcast([P, L])
                for part in range(2):
                    do(dve.tensor_tensor_scan(X[:, part, :], r_, X[:, part, :], 0.0, ALU.mult, ALU.add))
                do(tt(rt[:, 0, :, :], X, E_, ALU.mult))
                do(tt(rt[:, 1, :, :], X, F_, ALU.mult))
                do(tt(X[:, 0, :], rt[:, 0, 0, :], rt[:, 1, 1, :], ALU.subtract))
                mark(dve, tt(X[:, 1, :], rt[:, 0, 1, :], rt[:, 1, 0, :], ALU.add), x_state)
                if j % 4 == 0 and j:
                    s5_out(j // 4 - 1)
            s5_out(3)
            for j in range(2):
                wait_read_out(dve, jobs["glu"] + j)
            mark(dve, tt(zT, zT, rt.rearrange("p a b t -> p (a b) t"), ALU.mult), y_ready)
            post_norm(1, 1, "ssm_out")

            def mlp(i):
                pre_norm(4 * i + 2, 0)
                for j in range(16):
                    wait_read_out(dve, jobs[f"mlp{i}a"] + j)
                    o = ff[:, 2 * j:2 * j + 2, :]
                    mark(dve, tt(o, o, o, ALU.mult), ff_ready)
                post_norm(4 * i + 3, 1, f"mlp{i}b")

            mlp(0)

            pre_norm(4, 0)
            for j in range(10):
                wait_read_out(dve, jobs["att"] + j)
            dve.wait_ge(load_rope, 16)
            t1 = rope_t[:, 0, :]
            t2 = rope_t[:, 1, :]
            for t in range(TT):
                groups = [(0, 16, [roped[:, t, 0:16, :]]), (1536, 8, [roped[:, t, 16:24, :]]),
                          (1024, 4, [krope[:, t, 0:4, 0:HD], krope[:, t, 0:4, HD:]]),
                          (2048, 1, [krope[:, t, 4:5, 0:HD], krope[:, t, 4:5, HD:]])]
                for c0, nh, dsts in groups:
                    x = proj[:, t, c0:c0 + nh * HD].rearrange("p (h d) -> p h d", h=nh)
                    a = t1[:, 0:nh * HD].rearrange("p (h d) -> p h d", h=nh)
                    b = t2[:, 0:nh * HD].rearrange("p (h d) -> p h d", h=nh)
                    cos, sin = rope[:, t, 0:1, :], rope[:, t, 1:2, :]
                    do(tt(a, x, cos.to_broadcast([P, nh, HD]), ALU.mult))
                    do(tt(b[:, :, 0:32], x[:, :, 32:64], sin[:, :, 0:32].to_broadcast([P, nh, 32]), ALU.mult))
                    do(tt(b[:, :, 32:64], x[:, :, 0:32], sin[:, :, 32:64].to_broadcast([P, nh, 32]), ALU.mult))
                    for k, o in enumerate(dsts):
                        ins = tt(o, a, b, ALU.add)
                        if not (c0 == 2048 and k == 1):
                            do(ins)
                mark(dve, ins, roped_ready)
            scale_w = IDX_HEADS ** -0.5 * HD ** -0.5
            do(dve.tensor_scalar(wi_col, proj[:, :, 2112:2120], scale_w, None, ALU.mult))
            for t in range(TT):
                for g in range(4):
                    wait_read_out(dve, jobs["idx"] + 4 * t + g)
                    for b in range(2):
                        h = 4 * (g // 2) + 2 * b + g % 2
                        w = wi_col[:, t, h:h + 1]
                        x = rel[:, g % 2, b, :]
                        if g == 0 and b == 0:
                            ins = dve.tensor_scalar(idx_s[:, t, :], x, w, None, ALU.mult)
                        else:
                            ins = dve.scalar_tensor_tensor(out=idx_s[:, t, :], in0=x, scalar=w, in1=idx_s[:, t, :],
                                                           op0=ALU.mult, op1=ALU.add)
                        if b == 0:
                            do(ins)
                    mark(dve, ins, rel_used)
            for t in range(TT):
                dve.wait_ge(idx_causal, t + 1)
                src = idx_s
                for r in range(K_SEL // 8):
                    do(dve.max(m8, src[:, t, :]))
                    do(dve.match_replace(idx_w[:, t, :], m8, src[:, t, :], -3.0e38))
                    src = idx_w
                do(dve.tensor_scalar(keep[:, t, :], idx_w[:, t, :], -2.0e38, 1.0, ALU.is_le, ALU.subtract))
                mark(dve, dve.tensor_scalar(keep[:, t, :], keep[:, t, :], -NEG, None, ALU.mult), keep_ready)
            for t in range(TT):
                dve.wait_ge(keep_causal, t + 1)
                for g in range(8):
                    job = jobs[f"att_s{t}"] + g
                    wait_bank_full(dve, job)
                    read_out(dve, dve.scalar_tensor_tensor(
                        out=prob[:, t, 4 * (g // 2):4 * (g // 2) + 4, :].rearrange("p (b e) s -> p b e s", e=2)[:, :, g % 2, :], in0=ps(job)[:, :].rearrange("p (a b) -> p a b", a=2),
                        scalar=HD ** -0.5, in1=keep[:, t:t + 1, :].to_broadcast([P, 2, L]), op0=ALU.mult, op1=ALU.add), job)
                do(dve.tensor_reduce(mx16[:, t, :], prob[:, t, :, :], AX_X, ALU.max))
                mark(dve, dve.tensor_scalar(mx16[:, t, :], mx16[:, t, :], -1.0, None, ALU.mult), logits_ready)
            for t in range(TT):
                dve.wait_ge(prob_ready, t + 1)
                do(dve.reciprocal(sum16[:, t, :], sum16[:, t, :]))
                for g in range(2):
                    job = jobs[f"pv{t}"] + g
                    wait_bank_full(dve, job)
                    read_out(dve, tt(o_att[:, t, 512 * g:512 * g + 512].rearrange("p (h d) -> p h d", h=8),
                                     ps(job)[:, :].rearrange("p (h d) -> p h d", h=8),
                                     sum16[:, t, 8 * g:8 * g + 8].unsqueeze(2).to_broadcast([P, 8, HD]), ALU.mult), job)
            post_norm(5, 1, "att_out")
            mlp(1)


_INS = ['x', 'c', 'ctx', 'c_ctx', 'w_ada', 'b_ada', 'w_in', 'w_gk2', 'b_gk', 'hg_lower_bounds', 'hg_norm', 'gla_norm',
        'w_out', 'ln_gamma', 'ln_beta', 'peer_w_query', 'peer_sub_keys', 'peer_u', 'peer_v', 'norm_g_2', 'mlp_w1_2',
        'mlp_w2_2', 'ssm_w_in_2', 'ssm_lam_re_2', 'ssm_lam_im_2', 'ssm_log_dt_2', 'ssm_b_re_2', 'ssm_b_im_2',
        'ssm_c_re_2', 'ssm_c_im_2', 'ssm_d_2', 'ssm_w_glu_2', 'ssm_w_out_2', 'att_w_in_2', 'att_w_out_2']


def kernel(**inputs):
    import numpy as _np
    import concourse.bacc as _bacc
    from concourse.bass_utils import run_bass_kernel_spmd as _run

    nc = _bacc.Bacc("TRN2", target_bir_lowering=False, num_devices=1)
    arrays, aps = {}, {}

    def give(name, a):
        arrays[f"in_{name}"] = a
        aps[name] = nc.dram_tensor(f"in_{name}", a.shape, mybir.dt.from_np(a.dtype), kind="ExternalInput").ap()

    for name in _INS:
        give(name, _np.ascontiguousarray(inputs[name]))
    half = HD // 2
    freq = _np.float32(10000.0) ** (-_np.arange(half, dtype=_np.float32) * _np.float32(2.0) / _np.float32(HD))
    ang = _np.arange(L, dtype=_np.float32)[:, None] * freq[None, :].astype(_np.float32)
    cos, sin = _np.cos(ang), _np.sin(ang)
    give("rope_table", _np.ascontiguousarray(
        _np.stack([_np.concatenate([cos, cos], 1), _np.concatenate([-sin, sin], 1)], 1).astype(_np.float32)))
    out = nc.dram_tensor("out_0", (1, L, D), F32, kind="ExternalOutput").ap()
    build(nc, aps, out)
    r = _run(nc, [arrays], core_ids=[0])
    return r.results[0]["out_0"]
```

```python
from contextlib import ExitStack
from math import pi

import concourse.bass as bass
from concourse import mybir

F32 = mybir.dt.float32
U32 = mybir.dt.uint32
I32 = mybir.dt.int32
U8 = mybir.dt.uint8
ALU = mybir.AluOpType
ACT = mybir.ActivationFunctionType
AX_X = mybir.AxisListType.X

P = 128
D = 1024
KC = D // P
L = 256
TT = L // P
HALF = 4
WIDE = 512
SLOTS = 6
EPS = 1e-6
ALPHA = 2.0 ** 0.25
BANKS = 8

HG_HEADS, GLA_HEADS = 4, 4
HEADS = HG_HEADS + GLA_HEADS
UNITS = 6
GRID_W = 64
ROWS = L // GRID_W
RANK = 16
LEVELS = [64, 32, 16, 8, 4, 2, 1]

PEER_HEADS = 8
NKEYS = 128
TOPK = 16
GATHERS = PEER_HEADS * TOPK
GSLOTS = TOPK

D_FF = 4096
SSM = 512
NSTATE = 16
N_HEADS, N_KV, HD = 16, 4, 64
IDX_HEADS = 8
K_SEL = 64
ATT_COLS = 2120
ROPED = 1024 + 256 + 512 + 64
NEG = -1.0e30


def build(nc, A, out):
    with ExitStack() as ctx:
        def sb(name, shape, dt=F32):
            return ctx.enter_context(nc.sbuf_tensor(name, shape, dt))

        def sem(name):
            return ctx.enter_context(nc.semaphore(name))

        bank = [ctx.enter_context(nc.psum_tensor(f"bank{b}", [P, WIDE], F32)) for b in range(BANKS)]
        bank_full = [sem(f"bank_full{b}") for b in range(BANKS)]
        bank_free = [sem(f"bank_free{b}") for b in range(BANKS)]
        jobs = {}
        njobs = [0]

        def alloc(name, n):
            jobs[name] = njobs[0]
            njobs[0] += n

        def ps(job):
            return bank[job % BANKS]

        def wait_bank_free(pe, job):
            if job >= BANKS:
                pe.wait_ge(bank_free[job % BANKS], job // BANKS)

        def wait_bank_full(eng, job):
            eng.wait_ge(bank_full[job % BANKS], job // BANKS + 1)

        def full(job):
            return bank_full[job % BANKS]

        def free(job):
            return bank_free[job % BANKS]

        arena = sb("arena", [P, 38400])

        def carve(off, *shape, dt=None):
            n = 1
            for s in shape:
                n *= s
            ap = arena[:, off:off + n]
            if dt is not None:
                ap = ap.bitcast(dt)
            if len(shape) == 2:
                ap = ap.rearrange("p (a b) -> p a b", a=shape[0])
            if len(shape) == 3:
                ap = ap.rearrange("p (a b c) -> p a b c", a=shape[0], b=shape[1])
            if len(shape) == 4:
                ap = ap.rearrange("p (a b c d) -> p a b c d", a=shape[0], b=shape[1], c=shape[2])
            return ap

        ring = sb("ring", [P, SLOTS, HALF * WIDE])
        ident = sb("ident", [P, P])
        ones = sb("ones", [P, L])
        select = sb("select", [P, 2, P])
        eps = sb("eps", [P, 1])
        level_mask = sb("level_mask", [P, 2, len(LEVELS), P], U8)
        stat = sb("stat", [P, 64])
        small = sb("small", [P, 1024])

        x_lat = carve(0, TT, D)
        mods = carve(2048, 4, D)
        mod1 = carve(6144, 4, D)
        val = carve(6144, 4, D)
        m_rows = [carve(10240, 2, WIDE), carve(16384, 2, WIDE)]
        b_rows = [arena[0:1, 11264:11264 + 2048].rearrange("p (a b) -> p a b", a=4),
                  arena[0:1, 17408:17408 + 2048].rearrange("p (a b) -> p a b", a=4)]
        decay = carve(10240, 2, 2 * UNITS, L)
        key = carve(16384, 2, 2 * UNITS, L)
        h_in = carve(16384, 4, D)
        qry = carve(22528, UNITS, L)
        gate_tmp = carve(24064, 2, 2, WIDE)
        state = carve(24064, 2 * UNITS, P)
        PB = 26112
        x_ctx = carve(PB, TT, D)
        hT = carve(PB + 2048, KC, 2 * L)
        hT_col = carve(PB, KC, L)
        rank_act = carve(PB + 6144, 2, 2 * L)
        gk2 = carve(PB + 7168, 2, L)
        w_rank = carve(PB + 8704, KC, 32)
        crow = carve(PB + 9216, 1, P)
        keyT = carve(PB, TT, 2 * UNITS, P)
        lvlW = carve(PB, 2, UNITS, L)
        q_state = carve(PB + 3072, 2 * UNITS, L)
        sc_in = carve(PB + 3072, HEADS, TT, P)
        sc_x = carve(PB + 5120, HEADS, 2, P)
        lvlE = carve(PB + 7168, 2, UNITS, L)
        o_mix = carve(10240, TT, D)
        gate_out = carve(36352, TT, D)
        mixT = carve(PB + 7168, KC, L)
        sq_tmp = carve(PB, 2, D)
        row_a = carve(22528, 2, D)
        h2 = carve(6144, TT, D)
        h2T = carve(8192, KC, L)
        qT = carve(10240, 16, L)
        keys_raw = carve(14336, 2, P)
        keysT = carve(14592, 2, P)
        s_key = [carve(16384, 16, P), carve(8192, 16, P)]
        s_work = carve(18432, 2, P)
        cand = carve(18688, TOPK, TOPK)
        c_work = carve(18944, L)
        onehot = carve(19200, 2, TOPK, TOPK)
        top_v = carve(24576, 2, TOPK)
        top_i = carve(24608, 2, TOPK, dt=U32)
        top_f = carve(24640, 2, TOPK)
        best_v = carve(24672, PEER_HEADS, TOPK)
        best_p = carve(24800, TOPK, dt=U32)
        part_i = carve(24816, 2, TOPK, dt=U32)
        part_f = carve(24848, 2, TOPK)
        pick = carve(24880, 2, TOPK)
        iota_f = carve(26128, TOPK)
        gate_w = carve(26144, TT, GATHERS)
        act_w = carve(26400, TT, GATHERS)
        rows_i = carve(26656, TT, GATHERS, dt=U32)
        sm8 = carve(26912, 2, PEER_HEADS)
        now_i = carve(26928, GSLOTS, dt=U32)
        gath = [arena[:, 27136 + D * i:27136 + D * (i + 1)] for i in range(8)] + [
            ring[:, i // 2, D * (i % 2):D * (i % 2 + 1)] for i in range(8)]
        y_acc = carve(35328, 2, D)

        hT2 = carve(2048, KC, L)
        mix2 = carve(4096, TT, D)
        row_b = carve(6144, 2, D)
        h_tok = carve(8192, TT, D)
        ff = carve(10240, 32, L)
        er = carve(8192, NSTATE, L)
        ei = carve(12288, NSTATE, L)
        Bz = carve(8192, NSTATE * 2, P).rearrange("p (r j) c -> p r j c", r=2)
        BT = carve(16384, 2, NSTATE, P)
        Cz = [carve(20480, NSTATE, P), carve(2048, NSTATE, P)]
        braw = carve(24576, 2, NSTATE, 16)
        bbar = carve(25088, 2, NSTATE, 16)
        craw = carve(4096, 2, 4, P)
        CT = carve(6144, 2, 4, P)
        e_tmp = carve(6144, 2 * D)
        b_tmp = carve(12288, NSTATE, 16)
        hT_s = carve(27136, KC, L)
        h_tok_s = carve(31232, TT, D)
        uT = carve(33792, 4, L)
        zT = carve(34816, 4, L)
        xs = carve(35840, 2, 2, L)
        rt = carve(36864, 2, 2, L)
        proj = carve(10240, TT, ATT_COLS)
        roped = carve(14592, TT, 24, 64)
        krope = carve(17664, TT, 5, P)
        qTa = carve(18944, 8, L)
        qiT = carve(20992, 4, L)
        kTa = carve(22016, 5, L)
        rope = carve(23296, TT, 2, HD)
        rope_t = carve(23552, TT, 29 * HD)
        idx_s = carve(27264, TT, L)
        idx_w = carve(27776, TT, L)
        keep = carve(28288, TT, L)
        rel = carve(28800, 2, 2, L)
        prob = carve(29824, 2, N_HEADS, L)
        pT = carve(14592, 2, N_HEADS, P)
        o_att = carve(8192, TT, D)

        w_full = [sem(f"w_full{s}") for s in range(SLOTS)]
        w_used = sem("w_used")
        dve_step = sem("dve_step")
        act_step = sem("act_step")
        pool_step = sem("pool_step")
        load_c, load_x, load_gate, load_gain, load_rows, load_keys, load_norm, load_s5, \
            load_rope = [sem(f"load_{n}") for n in "c x gate gain rows keys norm s5 rope".split()]
        load_b = [sem(f"load_b{i}") for i in range(4)]
        consts = sem("consts")
        c_silu = sem("c_silu")
        var_ready = sem("var_ready")
        std_ready = sem("std_ready")
        tok_ready = sem("tok_ready")
        masks_ready = sem("masks_ready")
        hT_col_ready = sem("hT_col_ready")
        lb_exp = sem("lb_exp")
        lb_sum = sem("lb_sum")
        lb_log = sem("lb_log")
        gate_abs = sem("gate_abs")
        gate_diff = sem("gate_diff")
        gate_k = sem("gate_k")
        gate_log = sem("gate_log")
        gate_done = sem("gate_done")
        scans_done = sem("scans_done")
        ctx_exp = sem("ctx_exp")
        ctx_key = sem("ctx_key")
        q_exp = sem("q_exp")
        q_state_ready = sem("q_state_ready")
        lvl_diff = sem("lvl_diff")
        lvl_exp = sem("lvl_exp")
        lvl_ready = sem("lvl_ready")
        mixed = sem("mixed")
        best_ready = sem("best_ready")
        soft_ready = sem("soft_ready")
        rows_ready = sem("rows_ready")
        gathered = [sem(f"gathered{s}") for s in range(GSLOTS)]
        row_used = sem("row_used")
        gelu_done = sem("gelu_done")
        index_ready = sem("index_ready")
        rows_free = sem("rows_free")
        s5_exp = sem("s5_exp")
        s5_theta = sem("s5_theta")
        s5_sin = sem("s5_sin")
        s5_bbar = sem("s5_bbar")
        s5_b = sem("s5_b")
        s5_c = sem("s5_c")
        s5_table = sem("s5_table")
        s5_dt = sem("s5_dt")
        x_state = sem("x_state")
        y_used = sem("y_used")
        y_ready = sem("y_ready")
        z_ready = sem("z_ready")
        glu_sig = sem("glu_sig")
        ff_relu = sem("ff_relu")
        ff_ready = sem("ff_ready")
        roped_ready = sem("roped_ready")
        rel_used = sem("rel_used")
        idx_causal = sem("idx_causal")
        keep_ready = sem("keep_ready")
        keep_causal = sem("keep_causal")
        logits_ready = sem("logits_ready")
        prob_ready = sem("prob_ready")
        out_ready = sem("out_ready")
        stored = sem("stored")

        NORM_USES = [("ln_in", 4), ("head", 16), ("post1", 2), ("mod2", 2), ("post2", 2)] + [
            (f"rms{i}", 2) for i in range(8)]
        norm_no = {n: i for i, (n, _) in enumerate(NORM_USES)}
        tok_no, at = {}, 0
        for n, c in [("in", 4), ("mix", 2), ("h2", 2), ("ssm", 2), ("mlp0", 2), ("att", 2), ("mlp1", 2)]:
            tok_no[n] = at
            at += c

        alloc("cT", 1)
        for n in range(4):
            alloc(f"ada{n}", 1)
            if n:
                alloc(f"adab{n - 1}", 2)
        alloc("adab3", 2)
        alloc("T_in", 8)
        for name, n in [("lb", 1), ("hff", 4), ("hfb", 4), ("rank", 2), ("gqk", 4), ("hq", 4), ("gla_gate", 4),
                        ("hi", 4), ("gv", 4), ("hg", 2), ("gg", 2), ("keyT", 6), ("state", 4), ("inter", 6),
                        ("ada4", 1), ("scx", 4), ("diag", 4), ("ada5", 1), ("adab4", 1)]:
            alloc(name, n)
        for lv in range(len(LEVELS)):
            alloc(f"lvl{lv}", 8)
            if lv + 6 < 12:
                alloc(f"ada{lv + 6}", 1)
            alloc(f"adab{lv + 5}", 1)
        for name, n in [("o", 4), ("T_mix", 4), ("out", 4), ("T_h2", 4), ("keys", 1), ("wq", 8), ("skey", 8),
                        ("s5p", 1), ("CT", 2), ("BT", 8), ("T_ssm", 4), ("ssm_in", 2)]:
            alloc(name, n)
        for j in range(NSTATE):
            if j % 4 == 0:
                alloc(f"y{j // 4}", 1)
            alloc(f"bu{j}", 1)
        for name, n in [("glu", 2), ("ssm_out", 4), ("T_mlp0", 4), ("mlp0a", 16), ("mlp0b", 4), ("T_att", 4),
                        ("att", 10), ("rT", 10), ("idx", 8), ("att_s0", 8), ("att_s1", 8), ("pT0", 4), ("pv0", 2),
                        ("pT1", 8), ("pv1", 2), ("T_atto", 4), ("att_out", 4), ("T_mlp1", 4), ("mlp1a", 16),
                        ("mlp1b", 4)]:
            alloc(name, n)

        stream, tile_no, given_back = [], {}, {}

        def weights(name, w, col0, cols, job, inside=False):
            tile_no[name] = len(stream)
            for r in range(0, w.shape[0], HALF * P):
                if not inside or r + HALF * P >= w.shape[0]:
                    given_back[len(stream)] = job
                stream.append(w[r:r + HALF * P, col0:col0 + cols].rearrange("(k p) n -> p k n", p=P))

        def wtile(n, cols=WIDE):
            return ring[:, n % SLOTS, 0:HALF * cols].rearrange("p (k n) -> p k n", k=HALF)

        def wait_weights(pe, n):
            pe.wait_ge(w_full[n % SLOTS], 16 * (n // SLOTS + 1))

        w_in = A["w_in"][0]
        for n in range(4):
            weights(f"ada{n}", A["w_ada"][0], n * WIDE, WIDE, jobs[f"ada{n}"])
        for name, c0, n in [("hff", 512, 4), ("hfb", 1024, 4), ("gqk", 2560, 4), ("hq", 0, 4), ("hi", 1536, 4),
                            ("gv", 3072, 4), ("hg", 2048, 2), ("gg", 3584, 2)]:
            weights(name, w_in, c0, WIDE, jobs[name] + n - 1)
        for n in range(4, 12):
            weights(f"ada{n}", A["w_ada"][0], n * WIDE, WIDE, jobs[f"ada{n}"])
        for n in range(2):
            weights(f"out{n}", A["w_out"][0], n * WIDE, WIDE, jobs["out"] + 2 * n + 1)
        for n in range(4):
            weights(f"wq{n}", A["peer_w_query"][0], n * WIDE, WIDE, jobs["wq"] + 2 * n + 1)
        weights("ssm_in", A["ssm_w_in_2"][0], 0, WIDE, jobs["ssm_in"] + 1)
        weights("glu", A["ssm_w_glu_2"][0], 0, WIDE, jobs["glu"] + 1)
        for n in range(2):
            weights(f"ssm_out{n}", A["ssm_w_out_2"][0], n * WIDE, WIDE, jobs["ssm_out"] + 2 * n + 1)
        for i in range(2):
            for n in range(8):
                weights(f"mlp{i}a{n}", A["mlp_w1_2"][i], n * WIDE, WIDE, jobs[f"mlp{i}a"] + 2 * n + 1)
            for n in range(2):
                weights(f"mlp{i}b{n}", A["mlp_w2_2"][i], n * WIDE, WIDE, jobs[f"mlp{i}b"] + 2 * n + 1, inside=True)
            if i == 0:
                for n in range(5):
                    weights(f"att{n}", A["att_w_in_2"][0], n * WIDE, min(WIDE, ATT_COLS - n * WIDE),
                            jobs["att"] + 2 * n + 1)
                for n in range(2):
                    weights(f"att_out{n}", A["att_w_out_2"][0], n * WIDE, WIDE, jobs["att_out"] + 2 * n + 1)

        bgk_raw = small[:, 0:128]
        lb_raw = small[:, 128:256]
        gain = small[:, 256:512].rearrange("p (a b) -> p a b", a=2)
        bgk = small[:, 512:516]
        one_lb = small[:, 516:524]
        log_lb = small[:, 524:532]
        log1m_lb = small[:, 532:540]
        lb = small[:, 540:548]
        cT = small[:, 592:848].rearrange("p (k w) -> p k w", w=32)
        b_end = small[:, 564:576]
        lb_t = small[:, 576:584]
        S5 = {n: small[:, 16 * i:16 * i + 16] for i, n in enumerate(
            "lr li dt mag th kk r sn hs cs ar ai den nr fr fi t1 t2 pr pi qr qi".split())}
        d_col = small[:, 360:364]
        s5_raw = carve(25600, 3, P)
        d_raw = carve(25984, P)
        dt_raw = carve(26112, 2)
        wi_col = small[:, 0:16].rearrange("p (t h) -> p t h", t=2)
        m8 = small[:, 16:24]
        mx16 = small[:, 24:56].rearrange("p (t h) -> p t h", t=2)
        sum16 = small[:, 56:88].rearrange("p (t h) -> p t h", t=2)
        it_t = gate_out[:, 0, 0:P].bitcast(I32)
        it_s = gate_out[:, 0, P:2 * P].bitcast(I32)
        it_x = gate_out[:, 0, 2 * P:3 * P].bitcast(I32)
        it_f = gate_out[:, 0, 3 * P:4 * P]
        it_g = gate_out[:, 0, 4 * P:5 * P]

        HEAD_AT = [0, 1, 2, 3, 4, 6, 5, 7]

        def unit_rows(place):
            head = HEAD_AT[place]
            if head < HG_HEADS:
                return head, slice(0, P)
            g = head - HG_HEADS
            return HG_HEADS + g // 2, slice(64 * (g % 2), 64 * (g % 2) + 64)

        counts = {}

        def step(eng, name, ins):
            counts[name] = counts.get(name, 0) + 1
            ins.then_inc({"dve": dve_step, "act": act_step, "pool": pool_step}[name], 1)
            eng.wait_ge({"dve": dve_step, "act": act_step, "pool": pool_step}[name], counts[name])

        def mark(eng, ins, s):
            counts[s.name] = counts.get(s.name, 0) + 1
            ins.then_inc(s, 1)
            eng.wait_ge(s, counts[s.name])

        def read_out(eng, ins, job):
            ins.then_inc(free(job), 1)
            eng.wait_ge(free(job), job // BANKS + 1)

        def wait_read_out(eng, job):
            eng.wait_ge(free(job), job // BANKS + 1)

        def by_cols(ap):
            return ap.rearrange("p (w r) -> p r w", r=ROWS)

        def by_rows(ap):
            return ap.rearrange("p (r w) -> p r w", r=ROWS)

        block = ctx.enter_context(nc.Block())

        @block.sync
        def _(sp):
            used = 0
            ada_at = {tile_no[f"ada{n}"]: n for n in range(12)}
            for n, src in enumerate(stream):
                if n in ada_at:
                    b = ada_at[n]
                    if b >= 4:
                        wait_bank_full(sp, jobs[f"adab{b - 4}"] + (1 if b - 4 < 4 else 0))
                    if b == 4:
                        sp.wait_ge(ctx_key, 1)
                    sp.dma_start(b_rows[b >= 4][:, b % 4, :], A["b_ada"][:, b * WIDE:(b + 1) * WIDE]).then_inc(load_b[b % 4], 16)
                if n == tile_no["ssm_in"]:
                    sp.wait_ge(row_used, 2 * TT * GATHERS)
                if n >= SLOTS:
                    old = n - SLOTS
                    if old in given_back:
                        wait_bank_full(sp, given_back[old])
                    else:
                        used += 1
                        sp.wait_ge(w_used, used)
                sp.dma_start(wtile(n, src.shape[2]), src).then_inc(w_full[n % SLOTS], 16)
            sp.wait_ge(out_ready, 1)
            sp.dma_start(out[0].rearrange("(t p) d -> p t d", p=P), x_lat).then_inc(stored, 16)
            sp.wait_ge(stored, 16)

        @block.gpsimd
        def _(pool):
            def do(ins):
                step(pool, "pool", ins)

            pool.memset(cT, 0.0).then_inc(consts, 1)
            pool.memset(ones[:], 1.0).then_inc(consts, 1)
            pool.memset(eps[:], EPS).then_inc(consts, 1)
            pool.iota(it_t, [[1, P]], base=0, channel_multiplier=0).then_inc(consts, 1)
            pool.iota(it_s, [[0, P]], base=0, channel_multiplier=1).then_inc(consts, 1)
            do(pool.memset(ident[:], 0.0))
            pool.affine_select(out=ident[:], in_=ident[:], compare_op=ALU.not_equal, fill=1.0, base=0,
                               pattern=[[-1, P]], channel_multiplier=1).then_inc(consts, 1)
            do(pool.memset(select[:], 0.0))
            for i in range(4):
                ins = pool.affine_select(out=select[:], in_=select[:], compare_op=ALU.not_equal, fill=1.0, base=-32 * i,
                                         pattern=[[-1, 2], [0, P]], channel_multiplier=1)
                if i < 3:
                    do(ins)
            ins.then_inc(consts, 1)

            for j in range(4, 8):
                wait_read_out(pool, jobs["T_in"] + j)
            for k in range(KC):
                ins = pool.tensor_copy(by_cols(hT_col[:, k, :]), by_rows(hT[:, k, L:2 * L]))
                if k < KC - 1:
                    do(ins)
            mark(pool, ins, hT_col_ready)

            loop = 0
            for t in range(TT):
                for table in (A["peer_u"][0], A["peer_v"][0]):
                    base = loop * GATHERS

                    def gather(s):
                        pool.indirect_dma_start(
                            out=gath[s], out_offset=None, in_=table,
                            in_offset=bass.IndirectOffsetOnAxis(ap=now_i[:, s:s + 1], axis=0),
                        ).then_inc(gathered[s], 16)

                    if loop == 0:
                        pool.wait_ge(rows_ready, 1)
                        for s in range(GSLOTS):
                            do(pool.tensor_copy(now_i[:, s:s + 1], rows_i[:, t, s:s + 1]))
                            gather(s)
                    head0 = 1 if loop == 0 else 0
                    first = counts["pool"] - head0 * TOPK
                    with pool.Fori(head0, PEER_HEADS) as head:
                        if loop % 2 == 0:
                            pool.wait_ge(rows_ready, head + (PEER_HEADS * t + 1))
                        i = head * TOPK
                        for s in range(GSLOTS):
                            pool.wait_ge(row_used, i + (base + s + 1 - GSLOTS))
                            pool.tensor_copy(now_i[:, s:s + 1], rows_i[:, t, bass.ds(i + s, 1)]).then_inc(pool_step, 1)
                            pool.wait_ge(pool_step, i + (first + s + 1))
                            pool.sem_inc(index_ready, 1)
                            gather(s)
                    counts["pool"] = first + GATHERS
                    loop += 1

            for t in range(TT):
                pool.wait_ge(rel_used, 4 * t + 4)
                pool.affine_select(out=idx_s[:, t, :], in_=idx_s[:, t, :], compare_op=ALU.is_ge, fill=-1.0e38,
                                   base=t * P, pattern=[[-1, L]], channel_multiplier=1).then_inc(idx_causal, 1)
            for t in range(TT):
                pool.wait_ge(keep_ready, t + 1)
                pool.affine_select(out=keep[:, t, :], in_=keep[:, t, :], compare_op=ALU.is_ge, fill=NEG,
                                   base=t * P, pattern=[[-1, L]], channel_multiplier=1).then_inc(keep_causal, 1)

        def mm(o, lhsT, rhs, first, last):
            return nc.tensor.matmul(o, lhsT, rhs, start=first, stop=last)

        def pe_feature(pe, job0, tile, kc, n_blocks, cols, x, per_job):
            for m in range((kc + HALF - 1) // HALF):
                wait_weights(pe, tile + m)
            for b in range(n_blocks):
                job = job0 + b // per_job
                c0 = (b % per_job) * cols
                if b % per_job == 0:
                    wait_bank_free(pe, job)
                for k in range(kc):
                    last = mm(ps(job)[:, c0:c0 + cols], wtile(tile + k // HALF)[:, k % HALF, b * P:(b + 1) * P],
                              x(k), k == 0, k == kc - 1)
                if b % per_job == per_job - 1:
                    last.then_inc(full(job), 1)

        def pe_token(pe, job0, tile, kc, xs_of_tile, cols=WIDE):
            for m in range((kc + HALF - 1) // HALF):
                wait_weights(pe, tile + m)
            for i, x in enumerate(xs_of_tile):
                wait_bank_free(pe, job0 + i)
                for k in range(kc):
                    last = mm(ps(job0 + i)[:, 0:cols], x(k), wtile(tile + k // HALF, cols)[:, k % HALF, :],
                              k == 0, k == kc - 1)
                last.then_inc(full(job0 + i), 1)

        def pe_transpose(pe, name, tiles, n_tiles):
            for t in range(n_tiles):
                if name == "atto":
                    for g in range(2):
                        wait_read_out(pe, jobs[f"pv{t}"] + g)
                else:
                    pe.wait_ge(tok_ready, tok_no[name] + t + 1)
                for g in range(2):
                    job = jobs["T_" + name] + 2 * t + g
                    wait_bank_free(pe, job)
                    for b in range(4):
                        last = nc.tensor.transpose(ps(job)[:, b * P:(b + 1) * P],
                                                   tiles[:, t, (4 * g + b) * P:(4 * g + b + 1) * P], ident[:])
                    last.then_inc(full(job), 1)

        def wait_transposed(pe, name, t0, n_tiles):
            for j in range(2 * t0, 2 * (t0 + n_tiles)):
                wait_read_out(pe, jobs["T_" + name] + j)

        def tile_of(xT, t):
            return lambda k: xT[:, k, t * P:(t + 1) * P]

        def pe_ada(pe):
            pe.wait_ge(consts, 7)
            pe.wait_ge(c_silu, 1)
            nc.tensor.transpose(ps(jobs["cT"])[:, 0:16], crow[0:16, 0, :], ident[0:16, 0:16]).then_inc(full(jobs["cT"]), 1)
            wait_read_out(pe, jobs["cT"])
            for n in range(5):
                if n < 4:
                    pe_ada_rows(pe, n)
                if n:
                    pe_ada_spread(pe, n - 1)

        def pe_ada_rows(pe, n):
            job = jobs[f"ada{n}"]
            wait_weights(pe, tile_no[f"ada{n}"])
            wait_weights(pe, tile_no[f"ada{n}"] + 1)
            wait_bank_free(pe, job)
            for k in range(KC):
                c = k % 4
                last = nc.tensor.matmul(ps(job)[32 * c:32 * c + 32, :], cT[:, k, :],
                                        wtile(tile_no[f"ada{n}"] + k // HALF)[:, k % HALF, :],
                                        start=k < 4, stop=k >= 4, tile_position=(0, 32 * c))
            last.then_inc(full(job), 1)

        def pe_ada_spread(pe, n):
            wait_read_out(pe, jobs[f"ada{n}"])
            pe.wait_ge(load_b[n % 4], 16 * (n // 4 + 1))
            for w in range(2 if n < 4 else 1):
                job = jobs[f"adab{n}"] + w
                wait_bank_free(pe, job)
                mm(ps(job)[:, :], select[:, w, :], m_rows[n >= 4][:, n % 2, :], True, False)
                mm(ps(job)[:, :], ones[0:1, 0:P], b_rows[n >= 4][:, n % 4, :], False, True).then_inc(full(job), 1)

        def pe_project(pe):
            pe_transpose(pe, "in", h_in, 4)
            job = jobs["lb"]
            wait_bank_free(pe, job)
            pe.wait_ge(load_gate, 64)
            nc.tensor.transpose(ps(job)[:, 0:8], lb_raw[0:8, :], ident[0:8, 0:8])
            nc.tensor.transpose(ps(job)[:, 8:12], bgk_raw[0:4, :], ident[0:4, 0:4]).then_inc(full(job), 1)
            wait_transposed(pe, "in", 0, 4)
            every = lambda k: hT[:, k, :]
            latent = lambda k: hT[:, k, L:2 * L]
            for name in ("hff", "hfb"):
                pe_feature(pe, jobs[name], tile_no[name], KC, 4, 2 * L, every, 1)
            for d in range(2):
                job = jobs["rank"] + d
                wait_bank_free(pe, job)
                for k in range(KC):
                    last = mm(ps(job)[0:RANK, :], w_rank[:, k, RANK * d:RANK * (d + 1)], hT[:, k, :], k == 0, k == KC - 1)
                last.then_inc(full(job), 1)
            for m in range(2):
                wait_weights(pe, tile_no["gqk"] + m)
            for b in range(4):
                job = jobs["gqk"] + b
                wait_bank_free(pe, job)
                cols = 2 * L if b >= 2 else L
                for k in range(KC):
                    last = mm(ps(job)[:, 0:cols], wtile(tile_no["gqk"] + k // HALF)[:, k % HALF, b * P:(b + 1) * P],
                              hT[:, k, 2 * L - cols:2 * L], k == 0, k == KC - 1)
                last.then_inc(full(job), 1)
            pe_feature(pe, jobs["hq"], tile_no["hq"], KC, 4, L, latent, 1)
            for j in range(4):
                job = jobs["gla_gate"] + j
                wait_read_out(pe, jobs["rank"] + j // 2)
                wait_bank_free(pe, job)
                mm(ps(job)[:, :], gk2[0:RANK, j // 2, (j % 2) * P:(j % 2 + 1) * P], rank_act[0:RANK, j // 2, :],
                   True, True).then_inc(full(job), 1)

            def row_major(tok):
                return lambda k: hT[:, k, tok * P:(tok + 1) * P]

            def col_major(t):
                return lambda k: hT_col[:, k, t * P:(t + 1) * P]

            pe_token(pe, jobs["hi"], tile_no["hi"], KC, [row_major(i) for i in range(4)])
            pe.wait_ge(hT_col_ready, 1)
            pe_token(pe, jobs["gv"], tile_no["gv"], KC, [row_major(0), row_major(1), col_major(0), col_major(1)])
            pe_token(pe, jobs["hg"], tile_no["hg"], KC, [row_major(2), row_major(3)])
            pe_token(pe, jobs["gg"], tile_no["gg"], KC, [col_major(0), col_major(1)])

        def pe_states(pe):
            pe.wait_ge(ctx_key, 1)
            for t in range(TT):
                for g in range(3):
                    job = jobs["keyT"] + 3 * t + g
                    wait_bank_free(pe, job)
                    for b in range(4):
                        last = nc.tensor.transpose(ps(job)[:, b * P:(b + 1) * P],
                                                   decay[:, 0, 4 * g + b, t * P:(t + 1) * P], ident[:])
                    last.then_inc(full(job), 1)
            for j in range(6):
                wait_read_out(pe, jobs["keyT"] + j)
            for name in ("hi", "gv"):
                for j in range(4):
                    wait_read_out(pe, jobs[name] + j)
            for j in range(4):
                d, gla = j % 2, j // 2
                job = jobs["state"] + j
                wait_bank_free(pe, job)
                for b in range(2 if gla else 4):
                    w = 2 * P if gla else P
                    for t in range(TT):
                        last = mm(ps(job)[:, b * w:(b + 1) * w], keyT[:, t, d * UNITS + 4 * gla + b, :],
                                  val[:, t, 512 * gla + b * w:512 * gla + (b + 1) * w], t == 0, t == TT - 1)
                last.then_inc(full(job), 1)
            pe.wait_ge(q_state_ready, 1)
            for j in range(4):
                wait_read_out(pe, jobs["state"] + j)
            for t in range(TT):
                for g, (p0, p1) in enumerate(((0, 4), (4, 6), (6, 8))):
                    job = jobs["inter"] + 3 * t + g
                    wait_bank_free(pe, job)
                    for b in range(p1 - p0):
                        u, rows = unit_rows(p0 + b)
                        for d in range(2):
                            last = mm(ps(job)[:, b * P:(b + 1) * P], q_state[rows, d * UNITS + u, t * P:(t + 1) * P],
                                      state[rows, d * UNITS + u, :], d == 0, d == 1)
                    last.then_inc(full(job), 1)

        def pe_scores(pe):
            pe_ada_rows(pe, 4)
            pe.wait_ge(lvl_ready, 1)
            first, second = slice(0, P), slice(P, 2 * P)
            for j in range(4):
                job = jobs["scx"] + j
                wait_bank_free(pe, job)
                for b in range(4):
                    u, rows = unit_rows(2 * j + b // 2)
                    d = b % 2
                    ks, qs = (first, second) if d == 0 else (second, first)
                    last = mm(ps(job)[:, b * P:(b + 1) * P], lvlW[rows, d, u, ks], lvlW[rows, d, u, qs], True, True)
                last.then_inc(full(job), 1)
            for j in range(4):
                job = jobs["diag"] + j
                wait_bank_free(pe, job)
                for b in range(4):
                    u, rows = unit_rows(2 * j + b // 2)
                    t = b % 2
                    for d in range(2):
                        last = mm(ps(job)[:, b * P:(b + 1) * P], key[rows, 1, d * UNITS + u, t * P:(t + 1) * P],
                                  qry[rows, u, t * P:(t + 1) * P], d == 0, d == 1)
                last.then_inc(full(job), 1)
            pe_ada_rows(pe, 5)
            pe_ada_spread(pe, 4)
            for lv in range(len(LEVELS)):
                pe.wait_ge(lvl_ready, lv + 2)
                for j in range(8):
                    job = jobs[f"lvl{lv}"] + j
                    wait_bank_free(pe, job)
                    d = j // 4
                    for b in range(4):
                        u, rows = unit_rows(2 * (j % 4) + b // 2)
                        w = lvlW[rows, d, u, (b % 2) * P:(b % 2 + 1) * P]
                        last = mm(ps(job)[:, b * P:(b + 1) * P], w, w, True, True)
                    last.then_inc(full(job), 1)
                if lv + 6 < 12:
                    pe_ada_rows(pe, lv + 6)
                pe_ada_spread(pe, lv + 5)
            for j in range(8):
                wait_read_out(pe, jobs[f"lvl{len(LEVELS) - 1}"] + j)
            for t in range(TT):
                for g in range(2):
                    job = jobs["o"] + 2 * t + g
                    wait_bank_free(pe, job)
                    for b in range(4):
                        h = HEAD_AT.index(4 * g + b)
                        v = slice((4 * g + b) * P, (4 * g + b + 1) * P)
                        mm(ps(job)[:, b * P:(b + 1) * P], sc_in[:, h, t, :], val[:, 2 + t, v], True, False)
                        last = mm(ps(job)[:, b * P:(b + 1) * P], sc_x[:, h, 1 - t, :], val[:, 3 - t, v], False, True)
                    last.then_inc(full(job), 1)

        def pe_experts(pe):
            pe_transpose(pe, "mix", o_mix, 2)
            wait_transposed(pe, "mix", 0, 2)
            for n in range(2):
                pe_token(pe, jobs["out"] + 2 * n, tile_no[f"out{n}"], KC, [tile_of(mixT, t) for t in range(TT)])
            pe_transpose(pe, "h2", h2, 2)
            job = jobs["keys"]
            wait_bank_free(pe, job)
            pe.wait_ge(load_keys, 16)
            nc.tensor.transpose(ps(job)[:, 0:P], keys_raw[:, 0, :], ident[:])
            nc.tensor.transpose(ps(job)[:, P:2 * P], keys_raw[:, 1, :], ident[:]).then_inc(full(job), 1)
            wait_transposed(pe, "h2", 0, 2)
            for n in range(4):
                pe_feature(pe, jobs["wq"] + 2 * n, tile_no[f"wq{n}"], KC, 4, L, lambda k: h2T[:, k, :], 2)
            wait_read_out(pe, jobs["keys"])
            for j in range(8):
                wait_read_out(pe, jobs["wq"] + j)
            for t in range(TT):
                for g in range(4):
                    job = jobs["skey"] + 4 * t + g
                    wait_bank_free(pe, job)
                    for b in range(4):
                        last = mm(ps(job)[:, b * P:(b + 1) * P], qT[:, 4 * g + b, t * P:(t + 1) * P],
                                  keysT[:, b % 2, :], True, True)
                    last.then_inc(full(job), 1)

        def pe_s5(pe):
            job = jobs["s5p"]
            wait_bank_free(pe, job)
            pe.wait_ge(load_s5, 16 * 10)
            pe.wait_ge(s5_dt, 1)
            for i in range(3):
                nc.tensor.transpose(ps(job)[:, 16 * i:16 * i + 16], s5_raw[0:16, i, :], ident[0:16, 0:16])
            nc.tensor.transpose(ps(job)[:, 48:52], d_raw[0:4, :], ident[0:4, 0:4]).then_inc(full(job), 1)
            for r in range(2):
                job = jobs["CT"] + r
                wait_bank_free(pe, job)
                for b in range(4):
                    last = nc.tensor.transpose(ps(job)[:, b * P:(b + 1) * P], craw[:, r, b, :], ident[:])
                last.then_inc(full(job), 1)
            pe.wait_ge(s5_b, 1)
            for r in range(2):
                for g in range(4):
                    job = jobs["BT"] + 4 * r + g
                    wait_bank_free(pe, job)
                    for b in range(4):
                        last = nc.tensor.transpose(ps(job)[:, b * P:(b + 1) * P], Bz[:, r, 4 * g + b, :], ident[:])
                    last.then_inc(full(job), 1)
            pe_transpose(pe, "ssm", h_tok_s, 2)
            wait_transposed(pe, "ssm", 0, 2)
            pe_feature(pe, jobs["ssm_in"], tile_no["ssm_in"], KC, 4, L, lambda k: hT_s[:, k, :], 2)
            for j in range(2):
                wait_read_out(pe, jobs["ssm_in"] + j)
            for j in range(8):
                wait_read_out(pe, jobs["BT"] + j)
            pe.wait_ge(s5_c, 1)

            def output(j):
                a = j // 4
                if j % 4 == 0:
                    wait_bank_free(pe, jobs[f"y{a}"])
                pe.wait_ge(x_state, j + 1)
                mm(ps(jobs[f"y{a}"])[:, 0:L], Cz[0][:, j, :], xs[:, j % 2, 0, :], j % 4 == 0, False)
                last = mm(ps(jobs[f"y{a}"])[:, 0:L], Cz[1][:, j, :], xs[:, j % 2, 1, :], False, j % 4 == 3)
                last.then_inc(*((full(jobs[f"y{a}"]), 1) if j % 4 == 3 else (y_used, 1)))

            for j in range(NSTATE):
                job = jobs[f"bu{j}"]
                wait_bank_free(pe, job)
                for r in range(2):
                    last = mm(ps(job)[:, r * L:(r + 1) * L], BT[:, r, j, :], uT[:, j // 4, :], True, True)
                last.then_inc(full(job), 1)
                if j:
                    output(j - 1)
            output(NSTATE - 1)
            for j in range(4):
                pe.wait_ge(z_ready, j + 1)
            pe_feature(pe, jobs["glu"], tile_no["glu"], HALF, 4, L, lambda k: zT[:, k, :], 2)
            pe.wait_ge(y_ready, 1)
            for n in range(2):
                pe_token(pe, jobs["ssm_out"] + 2 * n, tile_no[f"ssm_out{n}"], HALF, [tile_of(zT, t) for t in range(TT)])

        def pe_mlp(pe, i):
            pe_transpose(pe, f"mlp{i}", h_tok, 2)
            wait_transposed(pe, f"mlp{i}", 0, 2)
            for n in range(8):
                pe_feature(pe, jobs[f"mlp{i}a"] + 2 * n, tile_no[f"mlp{i}a{n}"], KC, 4, L, lambda k: hT2[:, k, :], 2)
            for n in range(2):
                for t in range(TT):
                    wait_bank_free(pe, jobs[f"mlp{i}b"] + 2 * n + t)
                for kh in range(8):
                    tile = tile_no[f"mlp{i}b{n}"] + kh
                    wait_weights(pe, tile)
                    if n == 0:
                        pe.wait_ge(ff_ready, 16 * i + 2 * kh + 2)
                    for t in range(TT):
                        job = jobs[f"mlp{i}b"] + 2 * n + t
                        for k in range(HALF):
                            last = mm(ps(job)[:, :], ff[:, HALF * kh + k, t * P:(t + 1) * P], wtile(tile)[:, k, :],
                                      kh == 0 and k == 0, kh == 7 and k == HALF - 1)
                        if kh == 7:
                            last.then_inc(full(job), 1)
                    if kh < 7:
                        last.then_inc(w_used, 1)

        def pe_attention(pe):
            pe_transpose(pe, "att", h_tok, 2)
            wait_transposed(pe, "att", 0, 2)
            for n in range(5):
                pe_token(pe, jobs["att"] + 2 * n, tile_no[f"att{n}"], KC, [tile_of(hT2, t) for t in range(TT)],
                         min(WIDE, ATT_COLS - n * WIDE))
            for t in range(TT):
                pe.wait_ge(roped_ready, t + 1)
                blocks = [roped[:, t, 2 * i:2 * i + 2, :] for i in range(12)] + [krope[:, t, i, :] for i in range(5)]
                for g in range(5):
                    job = jobs["rT"] + 5 * t + g
                    wait_bank_free(pe, job)
                    for b, x in enumerate(blocks[4 * g:4 * g + 4]):
                        last = nc.tensor.transpose(ps(job)[:, b * P:(b + 1) * P], x, ident[:])
                    last.then_inc(full(job), 1)
            for j in range(10):
                wait_read_out(pe, jobs["rT"] + j)
            for t in range(TT):
                for g in range(4):
                    job = jobs["idx"] + 4 * t + g
                    wait_bank_free(pe, job)
                    rows = slice(64 * (g % 2), 64 * (g % 2) + 64)
                    for b in range(2):
                        last = mm(ps(job)[:, b * L:(b + 1) * L], qiT[rows, 2 * (g // 2) + b, t * P:(t + 1) * P],
                                  kTa[rows, 4, :], True, True)
                    last.then_inc(full(job), 1)
            for t in range(TT):
                for g in range(8):
                    job = jobs[f"att_s{t}"] + g
                    wait_bank_free(pe, job)
                    rows = slice(64 * (g % 2), 64 * (g % 2) + 64)
                    for b in range(2):
                        last = mm(ps(job)[:, b * L:(b + 1) * L], qTa[rows, 2 * (g // 2) + b, t * P:(t + 1) * P],
                                  kTa[rows, g // 2, :], True, True)
                    last.then_inc(full(job), 1)
            for t in range(TT):
                pe.wait_ge(prob_ready, t + 1)
                for s in range(t + 1):
                    for g in range(4):
                        job = jobs[f"pT{t}"] + 4 * s + g
                        wait_bank_free(pe, job)
                        for b in range(4):
                            last = nc.tensor.transpose(ps(job)[:, b * P:(b + 1) * P],
                                                       prob[:, t, 4 * g + b, s * P:(s + 1) * P], ident[:])
                        last.then_inc(full(job), 1)
                for j in range(4 * (t + 1)):
                    wait_read_out(pe, jobs[f"pT{t}"] + j)
                for g in range(2):
                    job = jobs[f"pv{t}"] + g
                    wait_bank_free(pe, job)
                    for b in range(8):
                        h = 8 * g + b
                        c = 1280 + HD * (h // 4)
                        for s in range(t + 1):
                            last = mm(ps(job)[:, b * HD:(b + 1) * HD], pT[:, s, h, :], proj[:, s, c:c + HD], s == 0, s == t)
                    last.then_inc(full(job), 1)
            pe_transpose(pe, "atto", o_att, 2)
            wait_transposed(pe, "atto", 0, 2)
            for n in range(2):
                pe_token(pe, jobs["att_out"] + 2 * n, tile_no[f"att_out{n}"], KC, [tile_of(hT2, t) for t in range(TT)])

        @block.tensor
        def _(pe):
            pe_ada(pe)
            pe_project(pe)
            pe_states(pe)
            pe_scores(pe)
            pe_experts(pe)
            pe_s5(pe)
            pe_mlp(pe, 0)
            pe_attention(pe)
            pe_mlp(pe, 1)

        def act_transposed(act, name, xT, n_tiles):
            for t in range(n_tiles):
                for g in range(2):
                    job = jobs["T_" + name] + 2 * t + g
                    wait_bank_full(act, job)
                    read_out(act, act.activation(xT[:, 4 * g:4 * g + 4, t * P:(t + 1) * P],
                                                 ps(job)[:, :].rearrange("p (k t) -> p k t", k=4), ACT.Copy), job)

        def norm_sqrt(act, name, scale):
            cols = dict(NORM_USES)[name]
            act.wait_ge(var_ready, norm_no[name] + 1)
            mark(act, act.activation(stat[:, 0:cols], stat[:, 0:cols], ACT.Sqrt, bias=eps[:, 0:1], scale=scale), std_ready)

        def act_ada_rows(act, n):
            job = jobs[f"ada{n}"]
            wait_bank_full(act, job)
            if n >= 2 and n != 4 and n != 5:
                wait_bank_full(act, jobs[f"adab{n - 2}"] + (1 if n - 2 < 4 else 0))
            read_out(act, act.activation(m_rows[n >= 4][:, n % 2, :], ps(job)[:, :], ACT.Copy), job)

        def act_ada_spread(act, n):
            s, c = n // 2, slice((n % 2) * WIDE, (n % 2 + 1) * WIDE)
            for w in range(2 if n < 4 else 1):
                job = jobs[f"adab{n}"] + w
                wait_bank_full(act, job)
                dst = mod1[:, 2 * s + w, c] if n < 4 else mods[:, s - 2, c]
                if s in (1, 4):
                    ins = act.activation(dst, ps(job)[:, :], ACT.Identity, bias=ones[:, 0:1])
                else:
                    ins = act.activation(dst, ps(job)[:, :], ACT.Copy)
                read_out(act, ins, job)

        def act_ada(act):
            act.wait_ge(load_c, 32)
            mark(act, act.activation(crow[0:16, 0, :], crow[0:16, 0, :], ACT.Silu), c_silu)
            wait_bank_full(act, jobs["cT"])
            act.wait_ge(consts, 7)
            read_out(act, act.activation(cT[:, :, 0:2], ps(jobs["cT"])[:, 0:16].rearrange("p (w k) -> p k w", w=2), ACT.Copy), jobs["cT"])
            norm_sqrt(act, "ln_in", 1.0)
            for n in range(5):
                if n < 4:
                    act_ada_rows(act, n)
                if n:
                    act_ada_spread(act, n - 1)
            act_transposed(act, "in", hT, 4)

        def act_gates(act):
            act.wait_ge(lb_sum, 1)
            mark(act, act.activation(lb_t, lb_t, ACT.Exp), lb_exp)
            act.wait_ge(lb_sum, 2)
            step(act, "act", act.activation(log_lb, log_lb, ACT.Ln, scale=2.0 ** 50))
            mark(act, act.activation(log1m_lb, one_lb, ACT.Ln), lb_log)

            def first(j):
                job = jobs["hff"] + j
                wait_bank_full(act, job)
                if j >= 2:
                    act.wait_ge(gate_done, j - 1)
                T = gate_tmp[:, j % 2, 0, :]
                step(act, "act", act.activation(T, ps(job)[:, :], ACT.Abs))
                step(act, "act", act.activation(T, T, ACT.Exp, scale=-1.0))
                mark(act, act.activation(T, T, ACT.Ln, bias=ones[:, 0:1]), gate_abs)

            def second(j):
                u = j % 4 + UNITS * (j // 4)
                wait_read_out(act, jobs["hff"] + j)
                mark(act, act.activation(key[:, :, u, :], key[:, :, u, :], ACT.Exp), gate_k)
                act.wait_ge(gate_diff, j + 1)
                T = gate_tmp[:, j % 2, 0, :]
                step(act, "act", act.activation(T, T, ACT.Abs))
                step(act, "act", act.activation(T, T, ACT.Exp, scale=-1.0))
                mark(act, act.activation(T, T, ACT.Ln, bias=ones[:, 0:1]), gate_log)

            for j in range(9):
                if j < 8:
                    first(j)
                if j:
                    second(j - 1)
            for d in range(2):
                job = jobs["rank"] + d
                wait_bank_full(act, job)
                step(act, "act", act.activation(rank_act[0:RANK, d, 0:L], ps(job)[0:RANK, 0:L], ACT.Copy))
                read_out(act, act.activation(by_cols(rank_act[0:RANK, d, L:2 * L]), by_rows(ps(job)[0:RANK, L:2 * L]),
                                             ACT.Copy), job)

        def act_project(act):
            for b in range(4):
                job = jobs["gqk"] + b
                wait_bank_full(act, job)
                if b < 2:
                    ins = act.activation(by_cols(qry[:, HG_HEADS + b, :]), by_rows(ps(job)[:, 0:L]), ACT.Copy, scale=0.125)
                else:
                    step(act, "act", act.activation(key[:, 0, HG_HEADS + b - 2, :], ps(job)[:, 0:L], ACT.Copy))
                    ins = act.activation(by_cols(key[:, 1, HG_HEADS + b - 2, :]), by_rows(ps(job)[:, L:2 * L]), ACT.Copy)
                read_out(act, ins, job)
            for b in range(4):
                job = jobs["hq"] + b
                wait_bank_full(act, job)
                read_out(act, act.activation(qry[:, b, :], ps(job)[:, 0:L], ACT.Copy), job)
            for j in range(4):
                job = jobs["gla_gate"] + j
                wait_bank_full(act, job)
                act.wait_ge(gate_done, 8 + j - 1)
                T = gate_tmp[:, j % 2, 0, :]
                step(act, "act", act.activation(T, ps(job)[:, :], ACT.Abs, bias=bgk[:, j:j + 1]))
                step(act, "act", act.activation(T, T, ACT.Exp, scale=-1.0))
                mark(act, act.activation(T, T, ACT.Ln, bias=ones[:, 0:1]), gate_abs)
            for name, c0 in (("hi", 0), ("gv", WIDE)):
                for i in range(4):
                    job = jobs[name] + i
                    wait_bank_full(act, job)
                    read_out(act, act.activation(val[:, i, c0:c0 + WIDE], ps(job)[:, :], ACT.Copy), job)
            act.wait_ge(masks_ready, 1)
            for name, c0 in (("hg", 0), ("gg", WIDE)):
                for t in range(TT):
                    job = jobs[name] + t
                    wait_bank_full(act, job)
                    read_out(act, act.activation(gate_out[:, t, c0:c0 + WIDE], ps(job)[:, :], ACT.Silu), job)

        def act_states(act):
            act.wait_ge(scans_done, 1)
            for u in range(2 * UNITS):
                ins = act.activation(decay[:, 0, u, :], decay[:, 0, u, :], ACT.Exp, bias=b_end[:, u:u + 1], scale=-1.0)
                if u < 2 * UNITS - 1:
                    step(act, "act", ins)
            mark(act, ins, ctx_exp)
            mark(act, act.activation(q_state, decay[:, 1, :, :], ACT.Exp), q_exp)
            for j in range(6):
                job = jobs["keyT"] + j
                wait_bank_full(act, job)
                g = j % 3
                read_out(act, act.activation(keyT[:, j // 3, 4 * g:4 * g + 4, :],
                                             ps(job)[:, :].rearrange("p (u c) -> p u c", u=4), ACT.Copy), job)
            for j in range(4):
                job = jobs["state"] + j
                d = j % 2
                wait_bank_full(act, job)
                if j < 2:
                    ins = act.activation(state[:, d * UNITS:d * UNITS + 4, :],
                                         ps(job)[:, :].rearrange("p (u c) -> p u c", u=4), ACT.Copy)
                else:
                    s, o = ps(job)[:, :].rearrange("p (k c) -> p k c", k=2), slice(d * UNITS + 4, d * UNITS + 6)
                    step(act, "act", act.activation(state[0:64, o, :], s[0:64, :, 0:P], ACT.Copy))
                    ins = act.activation(state[64:128, o, :], s[64:128, :, P:2 * P], ACT.Copy)
                read_out(act, ins, job)
            for t in range(TT):
                for g in range(3):
                    job = jobs["inter"] + 3 * t + g
                    wait_bank_full(act, job)
                    if g == 0:
                        o, n = o_mix[:, t, 0:WIDE].rearrange("p (h c) -> p h c", h=4), 4
                    else:
                        o, n = o_mix[:, t, WIDE:D].rearrange("p (h e c) -> p h e c", h=2, e=2)[:, :, g - 1, :], 2
                    read_out(act, act.activation(o, ps(job)[:, 0:n * P].rearrange("p (h c) -> p h c", h=n), ACT.Copy), job)

        def act_scores(act):
            def decays(i):
                act.wait_ge(lvl_diff, i + 1)
                mark(act, act.activation(lvlE, lvlE, ACT.Exp), lvl_exp)

            decays(0)
            act_ada_rows(act, 4)
            for name, dst in (("scx", sc_x), ("diag", sc_in)):
                for j in range(4):
                    job = jobs[name] + j
                    wait_bank_full(act, job)
                    read_out(act, act.activation(dst[:, 2 * j:2 * j + 2, :, :],
                                                 ps(job)[:, :].rearrange("p (h b c) -> p h b c", h=2, b=2), ACT.Copy), job)
                if name == "scx":
                    decays(1)
            act_ada_rows(act, 5)
            act_ada_spread(act, 4)
            for lv in range(len(LEVELS)):
                if lv + 2 <= len(LEVELS):
                    decays(lv + 2)
                if lv + 6 < 12:
                    act_ada_rows(act, lv + 6)
                act_ada_spread(act, lv + 5)

        def load_row_pair(act, dst, a, b, s):
            act.dma_start(dst[:, 0, :], a.to_broadcast([P, D])).then_inc(s, 16)
            act.dma_start(dst[:, 1, :], b.to_broadcast([P, D])).then_inc(s, 16)

        def act_experts(act):
            norm_sqrt(act, "head", 1.0 / P)
            for t in range(TT):
                for g in range(2):
                    job = jobs["T_mix"] + 2 * t + g
                    wait_bank_full(act, job)
                    i = ps(job)[:, :].rearrange("p (k t) -> p k t", k=4)
                    if g == 0:
                        ins = act.activation(mixT[:, 0:4, t * P:(t + 1) * P], i, ACT.Copy)
                    else:
                        w = P // ROWS
                        for k in range(4):
                            o = mixT[:, 4 + k, :].rearrange("p (r w) -> p w r", r=ROWS)[:, t * w:(t + 1) * w, :]
                            ins = act.activation(o, i[:, k, :].rearrange("p (w r) -> p w r", r=ROWS), ACT.Copy)
                            if k < 3:
                                step(act, "act", ins)
                    read_out(act, ins, job)
            gamma, beta = A["ln_gamma"][0], A["ln_beta"][0]
            load_row_pair(act, row_a, gamma[0:1, :], beta[0:1, :], load_rows)
            act.dma_start(keys_raw, A["peer_sub_keys"][0].rearrange("s n d -> n s d")).then_inc(load_keys, 16)
            norm_sqrt(act, "post1", 1.0)
            norm_sqrt(act, "mod2", 1.0)
            act_transposed(act, "h2", h2T, 2)
            job = jobs["keys"]
            wait_bank_full(act, job)
            read_out(act, act.activation(keysT, ps(job)[:, 0:2 * P].rearrange("p (a b) -> p a b", a=2), ACT.Copy), job)
            for j in range(8):
                job = jobs["wq"] + j
                wait_bank_full(act, job)
                read_out(act, act.activation(qT[:, 2 * j:2 * j + 2, :],
                                             ps(job)[:, :].rearrange("p (a b) -> p a b", a=2), ACT.Copy), job)
            for t in range(TT):
                for g in range(4):
                    job = jobs["skey"] + 4 * t + g
                    wait_bank_full(act, job)
                    read_out(act, act.activation(s_key[t][:, 4 * g:4 * g + 4, :],
                                                 ps(job)[:, :].rearrange("p (a b) -> p a b", a=4), ACT.Copy), job)
            act_soft(act, 0)
            act_gelu(act, 0)
            act_soft(act, 1)
            load_row_pair(act, row_a, gamma[1:2, :], beta[1:2, :], load_rows)

        def act_soft(act, t):
            act.wait_ge(best_ready, t + 1)
            mark(act, act.activation(gate_w[:, t, :], gate_w[:, t, :], ACT.Exp), soft_ready)

        def act_gelu(act, t):
            act.wait_ge(row_used, GATHERS * (2 * t + 1))
            mark(act, act.activation(act_w[:, t, :], act_w[:, t, :], ACT.Gelu_apprx_tanh), gelu_done)

        def act_rms(act, i):
            norm_sqrt(act, f"rms{i}", 1.0 / D)

        def load_norm_pair(act, k):
            if k:
                act.wait_ge(rows_free, k)
            g = A["norm_g_2"]
            load_row_pair(act, row_b, g[k // 2, 2 * (k % 2):2 * (k % 2) + 1, :],
                          g[k // 2, 2 * (k % 2) + 1:2 * (k % 2) + 2, :], load_norm)

        def act_tail(act, name):
            for n in range(2):
                for t in range(TT):
                    job = jobs[name] + 2 * n + t
                    wait_bank_full(act, job)
                    read_out(act, act.activation(mix2[:, t, n * WIDE:(n + 1) * WIDE], ps(job)[:, :], ACT.Copy), job)

        def blocks(r, g, q, part):
            rows, c = slice(64 * g, 64 * g + 64), slice(32 * q + 16 * g, 32 * q + 16 * g + 16)
            wide = (Bz[:, r] if part == "b" else Cz[r])[rows].rearrange("p (a q) c -> p a q c", q=4)[:, :, q, c]
            if part == "b":
                return wide, bbar[rows, r, :, :].rearrange("p (a q) c -> p a q c", q=4)[:, :, q, :]
            return wide, CT[rows, r, :, c]

        def act_s5_setup(act):
            act.dma_start(s5_raw[0:16, 0, :], A["ssm_lam_re_2"][0].rearrange("(j g) p -> j (g p)", g=2)).then_inc(load_s5, 16)
            act.dma_start(s5_raw[0:16, 1, :], A["ssm_lam_im_2"][0].rearrange("(j g) p -> j (g p)", g=2)).then_inc(load_s5, 16)
            act.dma_start(dt_raw[0:16, :], A["ssm_log_dt_2"][0].rearrange("(j g) -> j g", g=2)).then_inc(load_s5, 16)
            act.dma_start(d_raw[0:4, :], A["ssm_d_2"][0].rearrange("(a g) c -> a (g c)", a=4)).then_inc(load_s5, 16)
            for r, n in enumerate(("ssm_b_re_2", "ssm_b_im_2")):
                act.dma_start(braw[:, r, :, :], A[n][0].rearrange("(j g) p c -> (g p) j c", g=2)).then_inc(load_s5, 16)
            for r, n in enumerate(("ssm_c_re_2", "ssm_c_im_2")):
                for half in range(2):
                    act.dma_start(craw[:, r, :, 64 * half:64 * half + 64],
                                  A[n][0].rearrange("(a g) c p -> (g c) a p", a=4)).then_inc(load_s5, 16)
            wait_read_out(act, jobs["s5p"])
            mark(act, act.activation(S5["dt"], S5["dt"], ACT.Exp), s5_exp)
            act.wait_ge(s5_theta, 1)
            step(act, "act", act.activation(S5["mag"], S5["mag"], ACT.Exp))
            step(act, "act", act.activation(S5["sn"], S5["r"], ACT.Sin))
            mark(act, act.activation(S5["hs"], S5["r"], ACT.Sin, scale=0.5), s5_sin)
            zero = ones[:, 0:P].unsqueeze(1).to_broadcast([P, NSTATE, P])
            for m in (Bz[:, 0], Bz[:, 1], Cz[0], Cz[1]):
                step(act, "act", act.activation(m, zero, ACT.Copy, scale=0.0))
            act_gelu(act, 1)
            act.wait_ge(s5_bbar, 1)
            for r in range(2):
                for g in range(2):
                    for q in range(4):
                        ins = act.activation(*blocks(r, g, q, "b"), ACT.Copy)
                        if (r, g, q) != (1, 1, 3):
                            step(act, "act", ins)
            mark(act, ins, s5_b)
            for r in range(2):
                job = jobs["CT"] + r
                wait_bank_full(act, job)
                read_out(act, act.activation(CT[:, r, :, :], ps(job)[:, :].rearrange("p (a b) -> p a b", a=4), ACT.Copy), job)
            for r in range(2):
                for g in range(2):
                    for q in range(4):
                        ins = act.activation(*blocks(r, g, q, "c"), ACT.Copy, scale=1.0 - 2.0 * r)
                        if (r, g, q) != (1, 1, 3):
                            step(act, "act", ins)
            mark(act, ins, s5_c)
            for r in range(2):
                for g in range(4):
                    job = jobs["BT"] + 4 * r + g
                    wait_bank_full(act, job)
                    read_out(act, act.activation(BT[:, r, 4 * g:4 * g + 4, :],
                                                 ps(job)[:, :].rearrange("p (a b) -> p a b", a=4), ACT.Copy), job)
            act.wait_ge(s5_table, 1)
            load_norm_pair(act, 0)

        def act_s5(act):
            norm_sqrt(act, "post2", 1.0)
            act_rms(act, 0)
            act_transposed(act, "ssm", hT_s, 2)
            for j in range(2):
                job = jobs["ssm_in"] + j
                wait_bank_full(act, job)
                read_out(act, act.activation(uT[:, 2 * j:2 * j + 2, :],
                                             ps(job)[:, :].rearrange("p (a b) -> p a b", a=2), ACT.Copy), job)
            for a in range(4):
                wait_read_out(act, jobs[f"y{a}"])
                mark(act, act.activation(zT[:, a, :], zT[:, a, :], ACT.Gelu_apprx_tanh), z_ready)
            sg = rt.rearrange("p a b t -> p (a b) t")
            for j in range(2):
                job = jobs["glu"] + j
                wait_bank_full(act, job)
                read_out(act, act.activation(sg[:, 2 * j:2 * j + 2, :],
                                             ps(job)[:, :].rearrange("p (a b) -> p a b", a=2), ACT.Sigmoid), job)
            act_tail(act, "ssm_out")
            act_rms(act, 1)
            load_norm_pair(act, 1)

        def act_mlp(act, i):
            act_rms(act, 4 * i + 2)
            act_transposed(act, f"mlp{i}", hT2, 2)
            for j in range(16):
                job = jobs[f"mlp{i}a"] + j
                wait_bank_full(act, job)
                read_out(act, act.activation(ff[:, 2 * j:2 * j + 2, :],
                                             ps(job)[:, :].rearrange("p (a b) -> p a b", a=2), ACT.Relu), job)
            act_tail(act, f"mlp{i}b")
            act_rms(act, 4 * i + 3)

        def act_attention(act):
            load_norm_pair(act, 2)
            act_rms(act, 4)
            act_transposed(act, "att", hT2, 2)
            act.dma_start(rope, A["rope_table"].rearrange("(t p) c d -> p t c d", p=P)).then_inc(load_rope, 16)
            for n in range(5):
                cols = min(WIDE, ATT_COLS - n * WIDE)
                for t in range(TT):
                    job = jobs["att"] + 2 * n + t
                    wait_bank_full(act, job)
                    read_out(act, act.activation(proj[:, t, n * WIDE:n * WIDE + cols], ps(job)[:, 0:cols], ACT.Copy), job)
            for t in range(TT):
                dst = [qTa[:, 0:4], qTa[:, 4:8], qiT[:, 0:4], kTa[:, 0:4], kTa[:, 4:5]]
                for g in range(5):
                    job = jobs["rT"] + 5 * t + g
                    n = 4 if g < 4 else 1
                    wait_bank_full(act, job)
                    read_out(act, act.activation(dst[g][:, :, t * P:(t + 1) * P],
                                                 ps(job)[:, 0:n * P].rearrange("p (a b) -> p a b", a=n), ACT.Copy), job)
            for j in range(8):
                job = jobs["idx"] + j
                wait_bank_full(act, job)
                if j >= 2:
                    act.wait_ge(rel_used, j - 1)
                read_out(act, act.activation(rel[:, j % 2, :, :], ps(job)[:, :].rearrange("p (a b) -> p a b", a=2),
                                             ACT.Relu), job)
            for t in range(TT):
                act.wait_ge(logits_ready, t + 1)
                for h in range(N_HEADS):
                    ins = act.activation(prob[:, t, h, :], prob[:, t, h, :], ACT.Exp, bias=mx16[:, t, h:h + 1],
                                         accum_out=sum16[:, t, h:h + 1])
                    if h < N_HEADS - 1:
                        step(act, "act", ins)
                mark(act, ins, prob_ready)
            for t in range(TT):
                for s in range(t + 1):
                    for g in range(4):
                        job = jobs[f"pT{t}"] + 4 * s + g
                        wait_bank_full(act, job)
                        read_out(act, act.activation(pT[:, s, 4 * g:4 * g + 4, :],
                                                     ps(job)[:, :].rearrange("p (a b) -> p a b", a=4), ACT.Copy), job)
            act_transposed(act, "atto", hT2, 2)
            act_tail(act, "att_out")
            act_rms(act, 5)
            load_norm_pair(act, 3)

        @block.scalar
        def _(act):
            act.dma_start(crow[0:8, 0, :], A["c"][0].rearrange("(k p) -> k p", p=P)).then_inc(load_c, 16)
            act.dma_start(crow[8:16, 0, :], A["c_ctx"].rearrange("(k p) -> k p", p=P)).then_inc(load_c, 16)
            act.dma_start(x_ctx, A["ctx"][0].rearrange("(t p) d -> p t d", p=P)).then_inc(load_x, 16)
            act.dma_start(x_lat, A["x"][0].rearrange("(t p) d -> p t d", p=P)).then_inc(load_x, 16)
            act.dma_start(w_rank, w_in[:, 4096:4128].rearrange("(k p) n -> p k n", p=P)).then_inc(load_gate, 16)
            act.dma_start(gk2[0:RANK, :, :], A["w_gk2"][0].rearrange("d r c -> r d c")).then_inc(load_gate, 16)
            act.dma_start(bgk_raw[0:4, :], A["b_gk"][0].rearrange("d (j p) -> (d j) p", p=P)).then_inc(load_gate, 16)
            act.dma_start(lb_raw[0:8, :], A["hg_lower_bounds"][:, 0, :].rearrange("d (j p) -> (d j) p", p=P)).then_inc(load_gate, 16)
            act.dma_start(gain[:, 0, :], A["hg_norm"].to_broadcast([P, P])).then_inc(load_gain, 16)
            act.dma_start(gain[:, 1, :], A["gla_norm"].to_broadcast([P, P])).then_inc(load_gain, 16)
            act_ada(act)
            act_gates(act)
            act_project(act)
            act_states(act)
            act_scores(act)
            act_experts(act)
            act_s5_setup(act)
            act_s5(act)
            act_mlp(act, 0)
            act_attention(act)
            act_mlp(act, 1)

        @block.vector
        def _(dve):
            def do(ins):
                step(dve, "dve", ins)

            def go(ins):
                counts["dve"] += 1
                ins.then_inc(dve_step, 1)

            def wait_done():
                dve.wait_ge(dve_step, counts["dve"])

            def tt(o, a, b, op):
                return dve.tensor_tensor(o, a, b, op)

            def invert_std(name):
                cols = dict(NORM_USES)[name]
                dve.wait_ge(std_ready, norm_no[name] + 1)
                do(dve.reciprocal(stat[:, 0:cols], stat[:, 0:cols]))

            def layer_stats(tiles):
                for i, x in enumerate(tiles):
                    do(dve.bn_stats(stat[:, 24:30], x[:, 0:512]))
                    do(dve.bn_stats(stat[:, 30:36], x[:, 512:1024]))
                    do(dve.bn_aggr(stat[:, 40 + 2 * i:42 + 2 * i], stat[:, 24:36].rearrange("p (a b) -> p a b", a=2)))
                    ins = dve.tensor_copy(stat[:, i:i + 1], stat[:, 41 + 2 * i:42 + 2 * i])
                    if i < len(tiles) - 1:
                        do(ins)
                mark(dve, ins, var_ready)

            def normalized(o, x, i):
                return dve.tensor_scalar(o, x, stat[:, 40 + 2 * i:41 + 2 * i], stat[:, i:i + 1], ALU.subtract, ALU.mult)

            def square_sums(tiles, junk):
                for t, x in enumerate(tiles):
                    ins = dve.scalar_tensor_tensor(out=junk[:, t, :], in0=x, scalar=1.0, in1=x, op0=ALU.mult,
                                                   op1=ALU.mult, accum_out=stat[:, t:t + 1])
                    if t == 0:
                        do(ins)
                mark(dve, ins, var_ready)

            dve.wait_ge(consts, 7)
            do(tt(it_x, it_t, it_s, ALU.bitwise_xor))
            do(dve.tensor_copy(it_f, it_x))
            for d, op in enumerate((ALU.is_ge, ALU.is_le)):
                do(tt(it_g, it_s, it_t, op))
                do(dve.scalar_tensor_tensor(out=it_g, in0=it_g, scalar=1000.0, in1=it_f, op0=ALU.mult, op1=ALU.add))
                for i, h in enumerate(LEVELS):
                    ins = dve.tensor_scalar(level_mask[:, d, i, :], it_g, float(2 * h), None, ALU.is_lt)
                    if (d, i) != (1, len(LEVELS) - 1):
                        do(ins)
            mark(dve, ins, masks_ready)

            dve.wait_ge(load_x, 32)
            toks = [x_ctx[:, 0, :], x_ctx[:, 1, :], x_lat[:, 0, :], x_lat[:, 1, :]]
            layer_stats(toks)
            invert_std("ln_in")

            def modulated(i):
                w = 1 if i < 2 else 0
                do(normalized(h_in[:, i, :], toks[i], i))
                do(tt(h_in[:, i, :], h_in[:, i, :], mod1[:, 2 + w, :], ALU.mult))
                mark(dve, tt(h_in[:, i, :], h_in[:, i, :], mod1[:, w, :], ALU.add), tok_ready)

            for n in range(4):
                for w in range(2):
                    wait_read_out(dve, jobs[f"adab{n}"] + w)
            for i in range(4):
                modulated(i)

            job = jobs["lb"]
            wait_bank_full(dve, job)
            do(dve.tensor_copy(lb, ps(job)[:, 0:8]))
            read_out(dve, dve.tensor_copy(bgk, ps(job)[:, 8:12]), job)
            mark(dve, tt(lb_t, lb, lb, ALU.subtract), lb_sum)
            dve.wait_ge(lb_exp, 1)
            do(dve.reciprocal(lb, lb_t))
            do(tt(lb_t, lb, lb_t, ALU.mult))
            do(tt(lb, lb_t, lb_t, ALU.subtract))
            do(dve.tensor_scalar(lb, lb, 0.0, 1.0 - 1e-6, ALU.max, ALU.min))
            do(dve.tensor_scalar(one_lb, lb, -1.0, 1.0, ALU.mult, ALU.add))
            mark(dve, dve.tensor_scalar(log_lb, lb, 1e-30, None, ALU.max), lb_sum)
            dve.wait_ge(lb_log, 1)
            do(dve.tensor_scalar(log_lb, log_lb, -50.0 * 0.6931471805599453, None, ALU.add))

            def first(j):
                u = j % 4 + UNITS * (j // 4)
                job = jobs["hff"] + j
                T, S = gate_tmp[:, j % 2, 0, :], gate_tmp[:, j % 2, 1, :]
                wait_bank_full(dve, job)
                dve.wait_ge(gate_abs, j + 1)
                do(dve.scalar_tensor_tensor(out=S, in0=ps(job)[:, :], scalar=0.0, in1=T, op0=ALU.min, op1=ALU.subtract))
                read_out(dve, tt(key[:, :, u, :], S.rearrange("p (s t) -> p s t", s=2),
                                 ps(job)[:, :].rearrange("p (s t) -> p s t", s=2), ALU.subtract), job)
                do(dve.tensor_scalar(S, S, log1m_lb[:, j:j + 1], None, ALU.add))
                mark(dve, dve.tensor_scalar(T, S, log_lb[:, j:j + 1], None, ALU.subtract), gate_diff)

            def second(j):
                u = j % 4 + UNITS * (j // 4)
                T, S = gate_tmp[:, j % 2, 0, :], gate_tmp[:, j % 2, 1, :]
                dve.wait_ge(gate_k, j + 1)
                do(dve.tensor_scalar(key[:, :, u, :], key[:, :, u, :], one_lb[:, j:j + 1], None, ALU.mult))
                dve.wait_ge(gate_log, j + 1)
                mark(dve, dve.scalar_tensor_tensor(out=decay[:, :, u, :], in0=S.rearrange("p (s t) -> p s t", s=2),
                                                   scalar=log_lb[:, j:j + 1], in1=T.rearrange("p (s t) -> p s t", s=2),
                                                   op0=ALU.max, op1=ALU.add), gate_done)

            for j in range(9):
                if j < 8:
                    first(j)
                if j:
                    second(j - 1)
            for j in range(4):
                u = UNITS * (j // 2) + HG_HEADS + j % 2
                job = jobs["gla_gate"] + j
                T, S = gate_tmp[:, j % 2, 0, :], gate_tmp[:, j % 2, 1, :]
                wait_bank_full(dve, job)
                dve.wait_ge(gate_abs, 8 + j + 1)
                read_out(dve, dve.tensor_scalar(S, ps(job)[:, :], bgk[:, j:j + 1], 0.0, ALU.add, ALU.min), job)
                do(tt(S, S, T, ALU.subtract))
                mark(dve, dve.tensor_scalar(decay[:, :, u, :], S.rearrange("p (s t) -> p s t", s=2), 1.0 / 16.0, None,
                                            ALU.mult), gate_done)
            for u in range(2 * UNITS):
                for s in range(2):
                    a = decay[:, s, u, :] if u < UNITS else decay[:, s, u, ::-1]
                    do(dve.tensor_tensor_scan(a, ones[:, :], a, 0.0, ALU.mult, ALU.add))
            do(dve.tensor_copy(b_end[:, 0:UNITS], decay[:, 0, 0:UNITS, L - 1]))
            mark(dve, dve.tensor_copy(b_end[:, UNITS:2 * UNITS], decay[:, 0, UNITS:2 * UNITS, 0]), scans_done)
            for b in (2, 3):
                wait_read_out(dve, jobs["gqk"] + b)
            do(dve.tensor_copy(key[:, :, UNITS + HG_HEADS:2 * UNITS, :], key[:, :, HG_HEADS:UNITS, :]))
            dve.wait_ge(ctx_exp, 1)
            mark(dve, tt(decay[:, 0, :, :], decay[:, 0, :, :], key[:, 0, :, :], ALU.mult), ctx_key)

            bL = decay[:, 1, :, :].rearrange("p u t -> p (u t)")
            kL = key[:, 1, :, :].rearrange("p u t -> p (u t)")
            qL = qry.rearrange("p u t -> p (u t)")
            EL = lvlE.rearrange("p d u t -> p (d u t)")
            WL = lvlW.rearrange("p d u t -> p (d u t)")
            span = UNITS * L

            def halves(flat, d, h):
                return flat[:, d * span:(d + 1) * span].rearrange("p (n c h) -> p n c h", c=2, h=h)

            def exponents(i, h):
                for d in range(2):
                    b, e = halves(bL, d, h), halves(EL, d, h)
                    n = span // (2 * h)
                    seam = (b[:, :, 0, h - 1:h] if d == 0 else b[:, :, 1, 0:1]).to_broadcast([P, n, h])
                    near, far = (0, 1) if d == 0 else (1, 0)
                    do(tt(e[:, :, near, :], seam, b[:, :, near, :], ALU.subtract))
                    ins = tt(e[:, :, far, :], b[:, :, far, :], seam, ALU.subtract)
                    if d == 0:
                        do(ins)
                mark(dve, ins, lvl_diff)

            def decayed(i, h):
                dve.wait_ge(lvl_exp, i + 1)
                for d in range(2):
                    w, e, k, q = halves(WL, d, h), halves(EL, d, h), halves(kL, d, h), halves(qL, 0, h)
                    near, far = (0, 1) if d == 0 else (1, 0)
                    do(tt(w[:, :, near, :], e[:, :, near, :], k[:, :, near, :], ALU.mult))
                    ins = tt(w[:, :, far, :], e[:, :, far, :], q[:, :, far, :], ALU.mult)
                    if d == 0:
                        do(ins)
                mark(dve, ins, lvl_ready)

            levels = [P] + LEVELS
            exponents_after = lambda i: exponents(i + 1, levels[i + 1]) if i + 1 < len(levels) else None
            dve.wait_ge(q_exp, 1)
            for b in range(2):
                wait_read_out(dve, jobs["gqk"] + b)
            for b in range(4):
                wait_read_out(dve, jobs["hq"] + b)
            do(tt(q_state[:, 0:UNITS, :], q_state[:, 0:UNITS, :], qry[:, :, :], ALU.mult))
            mark(dve, tt(q_state[:, UNITS:, :], q_state[:, UNITS:, :], qry[:, :, :], ALU.mult), q_state_ready)
            wait_bank_full(dve, jobs["gg"] + 1)
            exponents(0, P)
            wait_bank_full(dve, jobs["state"] + 3)
            decayed(0, P)
            exponents_after(0)
            for i, h in enumerate(LEVELS):
                if i == 0:
                    wait_bank_full(dve, jobs["scx"] + 3)
                decayed(i + 1, h)
                exponents_after(i + 1)
                if i == 0:
                    for j in range(4):
                        wait_read_out(dve, jobs["diag"] + j)
                for j in range(8):
                    job = jobs[f"lvl{i}"] + j
                    wait_bank_full(dve, job)
                    m = level_mask[:, j // 4, i:i + 1, :].to_broadcast([P, 4, P])
                    dst = sc_in[:, 2 * (j % 4):2 * (j % 4) + 2, :, :].rearrange("p h t c -> p (h t) c")
                    read_out(dve, dve.copy_predicated(dst, m, ps(job)[:, :].rearrange("p (b c) -> p b c", b=4)), job)

            for t in range(TT):
                for g in range(2):
                    job = jobs["o"] + 2 * t + g
                    wait_bank_full(dve, job)
                    o = o_mix[:, t, g * WIDE:(g + 1) * WIDE]
                    if t == 0 and g == 0:
                        for j in range(6):
                            wait_read_out(dve, jobs["inter"] + j)
                    read_out(dve, tt(o, ps(job)[:, :], o, ALU.add), job)
            for t in range(TT):
                do(tt(sq_tmp[:, t, :], o_mix[:, t, :], o_mix[:, t, :], ALU.mult))
                ins = dve.tensor_reduce(stat[:, HEADS * t:HEADS * (t + 1)],
                                        sq_tmp[:, t, :].rearrange("p (h c) -> p h c", h=HEADS), AX_X, ALU.add)
                if t == 0:
                    do(ins)
            mark(dve, ins, var_ready)
            invert_std("head")
            dve.wait_ge(load_gain, 32)
            for name in ("hg", "gg"):
                for j in range(2):
                    wait_read_out(dve, jobs[name] + j)
            for t in range(TT):
                o = o_mix[:, t, :].rearrange("p (h c) -> p h c", h=HEADS)
                do(tt(o, o, stat[:, HEADS * t:HEADS * (t + 1)].unsqueeze(2).to_broadcast([P, HEADS, P]), ALU.mult))
                for g in range(2):
                    do(tt(o[:, 4 * g:4 * g + 4, :], o[:, 4 * g:4 * g + 4, :], gain[:, g:g + 1, :].to_broadcast([P, 4, P]), ALU.mult))
                mark(dve, tt(o_mix[:, t, :], o_mix[:, t, :], gate_out[:, t, :], ALU.mult), tok_ready)

            for n in range(4, 6):
                wait_read_out(dve, jobs[f"adab{n}"])
            for n in range(2):
                c = slice(n * WIDE, (n + 1) * WIDE)
                for t in range(TT):
                    job = jobs["out"] + 2 * n + t
                    wait_bank_full(dve, job)
                    read_out(dve, tt(sq_tmp[:, t, c], ps(job)[:, :], mods[:, 0, c], ALU.mult), job)
                    do(dve.scalar_tensor_tensor(out=x_lat[:, t, c], in0=x_lat[:, t, c], scalar=ALPHA,
                                                in1=sq_tmp[:, t, c], op0=ALU.mult, op1=ALU.add))

            def scaled_norm(name, load_count):
                layer_stats([x_lat[:, t, :] for t in range(TT)])
                invert_std(name)
                dve.wait_ge(load_rows, load_count)
                for t in range(TT):
                    do(normalized(x_lat[:, t, :], x_lat[:, t, :], t))
                    do(tt(x_lat[:, t, :], x_lat[:, t, :], row_a[:, 0, :], ALU.mult))
                    do(tt(x_lat[:, t, :], x_lat[:, t, :], row_a[:, 1, :], ALU.add))

            scaled_norm("post1", 32)
            for n in range(4, 12):
                wait_read_out(dve, jobs[f"adab{n}"])
            layer_stats([x_lat[:, t, :] for t in range(TT)])
            invert_std("mod2")
            for t in range(TT):
                do(normalized(h2[:, t, :], x_lat[:, t, :], t))
                do(tt(h2[:, t, :], h2[:, t, :], mods[:, 2, :], ALU.mult))
                mark(dve, tt(h2[:, t, :], h2[:, t, :], mods[:, 1, :], ALU.add), tok_ready)

            s = S5

            def s5_dt_rows():
                dve.wait_ge(load_s5, 16 * 10)
                mark(dve, dve.tensor_copy(s5_raw[0:16, 2, :].rearrange("p (g n) -> p g n", g=2),
                                          dt_raw[0:16, :].unsqueeze(2).to_broadcast([16, 2, 64])), s5_dt)

            def s5_angles():
                job = jobs["s5p"]
                wait_bank_full(dve, job)
                do(dve.tensor_copy(small[:, 0:48], ps(job)[:, 0:48]))
                do(dve.tensor_copy(d_col, ps(job)[:, 48:52]))
                read_out(dve, dve.tensor_copy(s["t1"], ps(job)[:, 32:48]), job)
                dve.wait_ge(s5_exp, 1)
                do(tt(s["mag"], s["lr"], s["dt"], ALU.mult))
                do(tt(s["th"], s["li"], s["dt"], ALU.mult))
                magic = 12582912.0
                do(dve.tensor_scalar(s["kk"], s["th"], 1.0 / (2 * pi), magic, ALU.mult, ALU.add))
                do(dve.tensor_scalar(s["kk"], s["kk"], magic, None, ALU.subtract))
                do(dve.scalar_tensor_tensor(out=s["r"], in0=s["kk"], scalar=-6.28125, in1=s["th"], op0=ALU.mult, op1=ALU.add))
                do(dve.scalar_tensor_tensor(out=s["r"], in0=s["kk"], scalar=-(2 * pi - 6.28125), in1=s["r"], op0=ALU.mult, op1=ALU.add))
                ins = dve.tensor_scalar(s["r"], s["r"], 3.1415925, -3.1415925, ALU.min, ALU.max)
                mark(dve, ins, s5_theta)

            def s5_factors():
                dve.wait_ge(s5_sin, 1)
                do(tt(s["cs"], s["hs"], s["hs"], ALU.mult))
                do(dve.tensor_scalar(s["cs"], s["cs"], -2.0, 1.0, ALU.mult, ALU.add))
                do(tt(s["t1"], s["cs"], s["cs"], ALU.mult))
                do(tt(s["t2"], s["sn"], s["sn"], ALU.mult))
                do(tt(s["t1"], s["t1"], s["t2"], ALU.add))
                do(dve.tensor_scalar(s["t1"], s["t1"], -0.5, 1.5, ALU.mult, ALU.add))
                do(tt(s["cs"], s["cs"], s["t1"], ALU.mult))
                do(tt(s["sn"], s["sn"], s["t1"], ALU.mult))
                do(tt(s["ar"], s["mag"], s["cs"], ALU.mult))
                do(tt(s["ai"], s["mag"], s["sn"], ALU.mult))
                do(dve.tensor_scalar(s["nr"], s["ar"], -1.0, None, ALU.add))
                do(tt(s["t1"], s["lr"], s["lr"], ALU.mult))
                do(tt(s["t2"], s["li"], s["li"], ALU.mult))
                do(tt(s["den"], s["t1"], s["t2"], ALU.add))
                do(dve.reciprocal(s["den"], s["den"]))
                do(tt(s["t1"], s["nr"], s["lr"], ALU.mult))
                do(tt(s["t2"], s["ai"], s["li"], ALU.mult))
                do(tt(s["fr"], s["t1"], s["t2"], ALU.add))
                do(tt(s["fr"], s["fr"], s["den"], ALU.mult))
                do(tt(s["t1"], s["ai"], s["lr"], ALU.mult))
                do(tt(s["t2"], s["nr"], s["li"], ALU.mult))
                do(tt(s["fi"], s["t1"], s["t2"], ALU.subtract))
                do(tt(s["fi"], s["fi"], s["den"], ALU.mult))

            def s5_inputs():
                wide = [P, NSTATE, 16]
                fr, fi = s["fr"].unsqueeze(2).to_broadcast(wide), s["fi"].unsqueeze(2).to_broadcast(wide)
                tmp = b_tmp
                do(tt(bbar[:, 0, :, :], braw[:, 0, :, :], fr, ALU.mult))
                do(tt(tmp, braw[:, 1, :, :], fi, ALU.mult))
                do(tt(bbar[:, 0, :, :], bbar[:, 0, :, :], tmp, ALU.subtract))
                do(tt(bbar[:, 1, :, :], braw[:, 1, :, :], fr, ALU.mult))
                do(tt(tmp, braw[:, 0, :, :], fi, ALU.mult))
                mark(dve, tt(bbar[:, 1, :, :], bbar[:, 1, :, :], tmp, ALU.add), s5_bbar)

            def s5_powers(first, last, start=False, half=None):
                if start:
                    for j in range(8):
                        wait_read_out(dve, jobs["BT"] + j)
                    dve.wait_ge(s5_c, 1)
                    go(dve.memset(er[:, :, 0:1], 1.0))
                    go(dve.memset(ei[:, :, 0:1], 0.0))
                    go(dve.tensor_copy(s["pr"], s["cs"]))
                    do(dve.tensor_copy(s["pi"], s["sn"]))
                tiles = slice(0, NSTATE) if half is None else slice(8 * half, 8 * half + 8)
                m = tiles.stop - tiles.start
                for level in range(first, last):
                    n = 2 ** level
                    pr, pi_ = [s[x][:, tiles].unsqueeze(2).to_broadcast([P, m, n]) for x in ("pr", "pi")]
                    e0, f0, e1, f1 = er[:, tiles, 0:n], ei[:, tiles, 0:n], er[:, tiles, n:2 * n], ei[:, tiles, n:2 * n]
                    tmp, tmp2 = [e_tmp[:, D * i:D * i + m * n].rearrange("p (j t) -> p j t", j=m) for i in range(2)]
                    go(tt(e1, e0, pr, ALU.mult))
                    go(tt(f1, f0, pr, ALU.mult))
                    go(tt(tmp, f0, pi_, ALU.mult))
                    do(tt(tmp2, e0, pi_, ALU.mult))
                    go(tt(e1, e1, tmp, ALU.subtract))
                    ins = tt(f1, f1, tmp2, ALU.add)
                    if level == 7:
                        if half == 1:
                            mark(dve, ins, s5_table)
                        else:
                            do(ins)
                        continue
                    go(ins)
                    go(tt(s["qr"], s["pr"], s["pr"], ALU.mult))
                    go(tt(s["qi"], s["pi"], s["pi"], ALU.mult))
                    do(tt(s["t1"], s["pr"], s["pi"], ALU.mult))
                    go(tt(s["pr"], s["qr"], s["qi"], ALU.subtract))
                    do(dve.tensor_scalar(s["pi"], s["t1"], 2.0, None, ALU.mult))

            do(tt(iota_f, ones[:, 0:TOPK], ones[:, 0:TOPK], ALU.subtract))
            do(dve.tensor_tensor_scan(iota_f, ones[:, 0:TOPK], ones[:, 0:TOPK], -1.0, ALU.mult, ALU.add))

            def best16(searches):
                for k, (x, work, v, i) in enumerate(searches):
                    go(dve.max(v[:, 0:8], x))
                wait_done()
                for x, work, v, i in searches:
                    go(dve.match_replace(work, v[:, 0:8], x, -3.0e38))
                wait_done()
                for x, work, v, i in searches:
                    go(dve.max_index(i[:, 0:8], v[:, 0:8], x))
                    go(dve.max(v[:, 8:16], work))
                wait_done()
                for x, work, v, i in searches:
                    go(dve.max_index(i[:, 8:16], v[:, 8:16], work))
                wait_done()

            def choose(t, h):
                if h == 0:
                    for g in range(4):
                        wait_read_out(dve, jobs["skey"] + 4 * t + g)
                best16([(s_key[t][:, 2 * h + c, :], s_work[:, c, :], top_v[:, c, :], top_i[:, c, :]) for c in range(2)])
                sq, pair = [P, TOPK, TOPK], [P, 2, TOPK, TOPK]
                go(dve.tensor_copy(top_f, top_i))
                do(tt(cand, top_v[:, 0, :].unsqueeze(2).to_broadcast(sq), top_v[:, 1, :].unsqueeze(1).to_broadcast(sq), ALU.add))
                best16([(cand.rearrange("p i j -> p (i j)"), c_work, best_v[:, h, :], best_p)])
                go(dve.tensor_scalar(part_i[:, 0, :], best_p, 4, None, ALU.logical_shift_right))
                do(dve.tensor_scalar(part_i[:, 1, :], best_p, 15, None, ALU.bitwise_and))
                do(dve.tensor_copy(part_f, part_i))
                do(tt(onehot, part_f.unsqueeze(3).to_broadcast(pair),
                      iota_f.unsqueeze(1).unsqueeze(1).to_broadcast(pair), ALU.is_equal))
                do(tt(onehot, onehot, top_f.unsqueeze(2).to_broadcast(pair), ALU.mult))
                do(dve.tensor_reduce(pick, onehot, AX_X, ALU.add))
                do(dve.scalar_tensor_tensor(out=pick[:, 0, :], in0=pick[:, 0, :], scalar=float(NKEYS), in1=pick[:, 1, :],
                                            op0=ALU.mult, op1=ALU.add))
                mark(dve, dve.tensor_copy(rows_i[:, t, TOPK * h:TOPK * (h + 1)], pick[:, 0, :]), rows_ready)
                if h == PEER_HEADS - 1:
                    gw = by_head(gate_w, t)
                    mark(dve, tt(gw, best_v, best_v[:, :, 0:1].to_broadcast([P, PEER_HEADS, TOPK]), ALU.subtract), best_ready)

            def by_head(x, t):
                return x[:, t, :].rearrange("p (h k) -> p h k", h=PEER_HEADS)

            def soften(t):
                gw = by_head(gate_w, t)
                dve.wait_ge(soft_ready, t + 1)
                do(dve.tensor_reduce(sm8[:, 0, :], gw, AX_X, ALU.add))
                do(dve.reciprocal(sm8[:, 1, :], sm8[:, 0, :]))
                do(tt(gw, gw, sm8[:, 1, :].unsqueeze(2).to_broadcast([P, PEER_HEADS, TOPK]), ALU.mult))

            def weigh(t):
                dve.wait_ge(gelu_done, t + 1)
                do(tt(act_w[:, t, :], act_w[:, t, :], gate_w[:, t, :], ALU.mult))

            def dots(t, first, last):
                base = 2 * t * GATHERS
                with dve.Fori(first, last) as head:
                    i = head * TOPK
                    for s in range(GSLOTS):
                        dve.wait_ge(gathered[s], i + (base + 16))
                        dve.scalar_tensor_tensor(out=gath[s], in0=gath[s], scalar=1.0, in1=h2[:, t, :],
                                                 op0=ALU.mult, op1=ALU.mult,
                                                 accum_out=act_w[:, t, bass.ds(i + s, 1)]).then_inc(row_used, 1)

            def add_rows(t, first, last):
                base = (2 * t + 1) * GATHERS
                with dve.Fori(first, last) as head:
                    i = head * TOPK
                    for s in range(GSLOTS):
                        dve.wait_ge(gathered[s], i + (base + 16))
                        dve.wait_ge(row_used, i + (base + s - 1))
                        dve.scalar_tensor_tensor(out=y_acc[:, s % 2, :], in0=gath[s],
                                                 scalar=act_w[:, t, bass.ds(i + s, 1)], in1=y_acc[:, s % 2, :],
                                                 op0=ALU.mult, op1=ALU.add).then_inc(row_used, 1)

            def add_experts(t):
                dve.wait_ge(row_used, 2 * (t + 1) * GATHERS)
                do(tt(y_acc[:, 0, :], y_acc[:, 0, :], y_acc[:, 1, :], ALU.add))
                do(tt(y_acc[:, 0, :], y_acc[:, 0, :], mods[:, 3, :], ALU.mult))
                do(dve.scalar_tensor_tensor(out=x_lat[:, t, :], in0=x_lat[:, t, :], scalar=ALPHA, in1=y_acc[:, 0, :],
                                            op0=ALU.mult, op1=ALU.add))

            choose(0, 0)
            go(dve.memset(y_acc, 0.0))
            for h in range(PEER_HEADS):
                if h + 1 < PEER_HEADS:
                    choose(0, h + 1)
                else:
                    soften(0)
                dots(0, h, h + 1)
            choose(1, 0)
            weigh(0)
            add_rows(0, 0, 2)
            for h in range(2, PEER_HEADS, 2):
                choose(1, h // 2)
                add_rows(0, h, h + 2)
            choose(1, 4)
            dots(1, 0, 1)
            add_experts(0)
            go(dve.memset(y_acc, 0.0))
            dots(1, 1, 2)
            choose(1, 5)
            dots(1, 2, 3)
            choose(1, 6)
            dots(1, 3, 5)
            choose(1, 7)
            dots(1, 5, 6)
            soften(1)
            s5_dt_rows()
            dots(1, 6, 7)
            s5_angles()
            dots(1, 7, 8)
            s5_factors()
            weigh(1)
            add_rows(1, 0, 1)
            s5_inputs()
            add_rows(1, 1, 3)
            s5_powers(0, 6, True)
            add_rows(1, 3, 5)
            s5_powers(6, 7)
            add_rows(1, 5, 6)
            s5_powers(7, 8, False, 0)
            add_rows(1, 6, 7)
            s5_powers(7, 8, False, 1)
            add_rows(1, 7, 8)
            add_experts(1)
            scaled_norm("post2", 64)

            def pre_norm(i, row, h_tok=h_tok):
                square_sums([x_lat[:, t, :] for t in range(TT)], h_tok)
                invert_std(f"rms{i}")
                dve.wait_ge(load_norm, 32 * (i // 2 + 1))
                for t in range(TT):
                    mark(dve, dve.scalar_tensor_tensor(out=h_tok[:, t, :], in0=x_lat[:, t, :], scalar=stat[:, t:t + 1],
                                                       in1=row_b[:, row, :], op0=ALU.mult, op1=ALU.mult), tok_ready)

            def post_norm(i, row, name, h_tok=h_tok):
                for j in range(4):
                    wait_read_out(dve, jobs[name] + j)
                square_sums([mix2[:, t, :] for t in range(TT)], h_tok)
                invert_std(f"rms{i}")
                for t in range(TT):
                    ins = dve.scalar_tensor_tensor(out=mix2[:, t, :], in0=mix2[:, t, :], scalar=stat[:, t:t + 1],
                                                   in1=row_b[:, row, :], op0=ALU.mult, op1=ALU.mult)
                    if t == 0:
                        do(ins)
                mark(dve, ins, rows_free)
                for t in range(TT):
                    ins = tt(x_lat[:, t, :], x_lat[:, t, :], mix2[:, t, :], ALU.add)
                    if i < 7:
                        do(ins)
                    elif t == 0:
                        do(ins)
                    else:
                        mark(dve, ins, out_ready)

            pre_norm(0, 0, h_tok_s)

            def s5_out(a):
                job = jobs[f"y{a}"]
                wait_bank_full(dve, job)
                ins = dve.scalar_tensor_tensor(out=zT[:, a, :], in0=uT[:, a, :], scalar=d_col[:, a:a + 1],
                                               in1=ps(job)[:, 0:L], op0=ALU.mult, op1=ALU.add)
                read_out(dve, ins, job)

            for j in range(2):
                wait_read_out(dve, jobs["ssm_in"] + j)
            for j in range(NSTATE):
                job = jobs[f"bu{j}"]
                X = xs[:, j % 2, :, :]
                E_ = er[:, j:j + 1, :].to_broadcast([P, 2, L])
                F_ = ei[:, j:j + 1, :].to_broadcast([P, 2, L])
                wait_bank_full(dve, job)
                b = ps(job)[:, :].rearrange("p (r t) -> p r t", r=2)
                do(tt(rt[:, 0, :, :], b, E_, ALU.mult))
                read_out(dve, tt(rt[:, 1, :, :], b, F_, ALU.mult), job)
                if j >= 2:
                    if (j - 2) % 4 == 3:
                        wait_bank_full(dve, jobs[f"y{(j - 2) // 4}"])
                    else:
                        dve.wait_ge(y_used, j - 1 - (j - 2) // 4)
                do(tt(X[:, 0, :], rt[:, 0, 0, :], rt[:, 1, 1, :], ALU.add))
                do(tt(X[:, 1, :], rt[:, 0, 1, :], rt[:, 1, 0, :], ALU.subtract))
                r_ = s["mag"][:, j:j + 1].to_broadcast([P, L])
                for part in range(2):
                    do(dve.tensor_tensor_scan(X[:, part, :], r_, X[:, part, :], 0.0, ALU.mult, ALU.add))
                do(tt(rt[:, 0, :, :], X, E_, ALU.mult))
                do(tt(rt[:, 1, :, :], X, F_, ALU.mult))
                do(tt(X[:, 0, :], rt[:, 0, 0, :], rt[:, 1, 1, :], ALU.subtract))
                mark(dve, tt(X[:, 1, :], rt[:, 0, 1, :], rt[:, 1, 0, :], ALU.add), x_state)
                if j % 4 == 0 and j:
                    s5_out(j // 4 - 1)
            s5_out(3)
            for j in range(2):
                wait_read_out(dve, jobs["glu"] + j)
            mark(dve, tt(zT, zT, rt.rearrange("p a b t -> p (a b) t"), ALU.mult), y_ready)
            post_norm(1, 1, "ssm_out", h_tok_s)

            def mlp(i):
                pre_norm(4 * i + 2, 0)
                for j in range(16):
                    wait_read_out(dve, jobs[f"mlp{i}a"] + j)
                    o = ff[:, 2 * j:2 * j + 2, :]
                    mark(dve, tt(o, o, o, ALU.mult), ff_ready)
                post_norm(4 * i + 3, 1, f"mlp{i}b")

            mlp(0)

            pre_norm(4, 0)
            for j in range(10):
                wait_read_out(dve, jobs["att"] + j)
            dve.wait_ge(load_rope, 16)
            t1 = rope_t[:, 0, :]
            t2 = rope_t[:, 1, :]
            for t in range(TT):
                groups = [(0, 16, [roped[:, t, 0:16, :]]), (1536, 8, [roped[:, t, 16:24, :]]),
                          (1024, 4, [krope[:, t, 0:4, 0:HD], krope[:, t, 0:4, HD:]]),
                          (2048, 1, [krope[:, t, 4:5, 0:HD], krope[:, t, 4:5, HD:]])]
                for c0, nh, dsts in groups:
                    x = proj[:, t, c0:c0 + nh * HD].rearrange("p (h d) -> p h d", h=nh)
                    a = t1[:, 0:nh * HD].rearrange("p (h d) -> p h d", h=nh)
                    b = t2[:, 0:nh * HD].rearrange("p (h d) -> p h d", h=nh)
                    cos, sin = rope[:, t, 0:1, :], rope[:, t, 1:2, :]
                    do(tt(a, x, cos.to_broadcast([P, nh, HD]), ALU.mult))
                    do(tt(b[:, :, 0:32], x[:, :, 32:64], sin[:, :, 0:32].to_broadcast([P, nh, 32]), ALU.mult))
                    do(tt(b[:, :, 32:64], x[:, :, 0:32], sin[:, :, 32:64].to_broadcast([P, nh, 32]), ALU.mult))
                    for k, o in enumerate(dsts):
                        ins = tt(o, a, b, ALU.add)
                        if not (c0 == 2048 and k == 1):
                            do(ins)
                mark(dve, ins, roped_ready)
            scale_w = IDX_HEADS ** -0.5 * HD ** -0.5
            do(dve.tensor_scalar(wi_col, proj[:, :, 2112:2120], scale_w, None, ALU.mult))
            for t in range(TT):
                for g in range(4):
                    wait_read_out(dve, jobs["idx"] + 4 * t + g)
                    for b in range(2):
                        h = 4 * (g // 2) + 2 * b + g % 2
                        w = wi_col[:, t, h:h + 1]
                        x = rel[:, g % 2, b, :]
                        if g == 0 and b == 0:
                            ins = dve.tensor_scalar(idx_s[:, t, :], x, w, None, ALU.mult)
                        else:
                            ins = dve.scalar_tensor_tensor(out=idx_s[:, t, :], in0=x, scalar=w, in1=idx_s[:, t, :],
                                                           op0=ALU.mult, op1=ALU.add)
                        if b == 0:
                            do(ins)
                    mark(dve, ins, rel_used)
            for t in range(TT):
                dve.wait_ge(idx_causal, t + 1)
                src = idx_s
                for r in range(K_SEL // 8):
                    do(dve.max(m8, src[:, t, :]))
                    do(dve.match_replace(idx_w[:, t, :], m8, src[:, t, :], -3.0e38))
                    src = idx_w
                do(dve.tensor_scalar(keep[:, t, :], idx_w[:, t, :], -2.0e38, 1.0, ALU.is_le, ALU.subtract))
                mark(dve, dve.tensor_scalar(keep[:, t, :], keep[:, t, :], -NEG, None, ALU.mult), keep_ready)
            for t in range(TT):
                dve.wait_ge(keep_causal, t + 1)
                for g in range(8):
                    job = jobs[f"att_s{t}"] + g
                    wait_bank_full(dve, job)
                    read_out(dve, dve.scalar_tensor_tensor(
                        out=prob[:, t, 4 * (g // 2):4 * (g // 2) + 4, :].rearrange("p (b e) s -> p b e s", e=2)[:, :, g % 2, :], in0=ps(job)[:, :].rearrange("p (a b) -> p a b", a=2),
                        scalar=HD ** -0.5, in1=keep[:, t:t + 1, :].to_broadcast([P, 2, L]), op0=ALU.mult, op1=ALU.add), job)
                do(dve.tensor_reduce(mx16[:, t, :], prob[:, t, :, :], AX_X, ALU.max))
                mark(dve, dve.tensor_scalar(mx16[:, t, :], mx16[:, t, :], -1.0, None, ALU.mult), logits_ready)
            for t in range(TT):
                dve.wait_ge(prob_ready, t + 1)
                do(dve.reciprocal(sum16[:, t, :], sum16[:, t, :]))
                for g in range(2):
                    job = jobs[f"pv{t}"] + g
                    wait_bank_full(dve, job)
                    read_out(dve, tt(o_att[:, t, 512 * g:512 * g + 512].rearrange("p (h d) -> p h d", h=8),
                                     ps(job)[:, :].rearrange("p (h d) -> p h d", h=8),
                                     sum16[:, t, 8 * g:8 * g + 8].unsqueeze(2).to_broadcast([P, 8, HD]), ALU.mult), job)
            post_norm(5, 1, "att_out")
            mlp(1)


_INS = ['x', 'c', 'ctx', 'c_ctx', 'w_ada', 'b_ada', 'w_in', 'w_gk2', 'b_gk', 'hg_lower_bounds', 'hg_norm', 'gla_norm',
        'w_out', 'ln_gamma', 'ln_beta', 'peer_w_query', 'peer_sub_keys', 'peer_u', 'peer_v', 'norm_g_2', 'mlp_w1_2',
        'mlp_w2_2', 'ssm_w_in_2', 'ssm_lam_re_2', 'ssm_lam_im_2', 'ssm_log_dt_2', 'ssm_b_re_2', 'ssm_b_im_2',
        'ssm_c_re_2', 'ssm_c_im_2', 'ssm_d_2', 'ssm_w_glu_2', 'ssm_w_out_2', 'att_w_in_2', 'att_w_out_2']


def kernel(**inputs):
    import numpy as _np
    import concourse.bacc as _bacc
    from concourse.bass_utils import run_bass_kernel_spmd as _run

    nc = _bacc.Bacc("TRN2", target_bir_lowering=False, num_devices=1)
    arrays, aps = {}, {}

    def give(name, a):
        arrays[f"in_{name}"] = a
        aps[name] = nc.dram_tensor(f"in_{name}", a.shape, mybir.dt.from_np(a.dtype), kind="ExternalInput").ap()

    for name in _INS:
        give(name, _np.ascontiguousarray(inputs[name]))
    half = HD // 2
    freq = _np.float32(10000.0) ** (-_np.arange(half, dtype=_np.float32) * _np.float32(2.0) / _np.float32(HD))
    ang = _np.arange(L, dtype=_np.float32)[:, None] * freq[None, :].astype(_np.float32)
    cos, sin = _np.cos(ang), _np.sin(ang)
    give("rope_table", _np.ascontiguousarray(
        _np.stack([_np.concatenate([cos, cos], 1), _np.concatenate([-sin, sin], 1)], 1).astype(_np.float32)))
    out = nc.dram_tensor("out_0", (1, L, D), F32, kind="ExternalOutput").ap()
    build(nc, aps, out)
    r = _run(nc, [arrays], core_ids=[0])
    return r.results[0]["out_0"]
```

```python
from contextlib import ExitStack
from math import pi

import concourse.bass as bass
from concourse import mybir

F32 = mybir.dt.float32
F32R = mybir.dt.float32r
U32 = mybir.dt.uint32
I32 = mybir.dt.int32
U8 = mybir.dt.uint8
ALU = mybir.AluOpType
ACT = mybir.ActivationFunctionType
AX_X = mybir.AxisListType.X

P = 128
D = 1024
KC = D // P
L = 256
TT = L // P
HALF = 4
WIDE = 512
SLOTS = 6
RAW_SLOTS = 4
SPLIT_SLOTS = 3
EPS = 1e-6
ALPHA = 2.0 ** 0.25
BANKS = 8

HG_HEADS, GLA_HEADS = 4, 4
HEADS = HG_HEADS + GLA_HEADS
UNITS = 6
GRID_W = 64
ROWS = L // GRID_W
RANK = 16
LEVELS = [64, 32, 16, 8, 4, 2, 1]

PEER_HEADS = 8
NKEYS = 128
TOPK = 16
GATHERS = PEER_HEADS * TOPK
GSLOTS = TOPK

D_FF = 4096
SSM = 512
NSTATE = 16
N_HEADS, N_KV, HD = 16, 4, 64
IDX_HEADS = 8
K_SEL = 64
ATT_COLS = 2120
ROPED = 1024 + 256 + 512 + 64
NEG = -1.0e30


def build(nc, A, out):
    with ExitStack() as ctx:
        def sb(name, shape, dt=F32):
            return ctx.enter_context(nc.sbuf_tensor(name, shape, dt))

        def sem(name):
            return ctx.enter_context(nc.semaphore(name))

        bank = [ctx.enter_context(nc.psum_tensor(f"bank{b}", [P, WIDE], F32)) for b in range(BANKS)]
        bank_full = [sem(f"bank_full{b}") for b in range(BANKS)]
        bank_free = [sem(f"bank_free{b}") for b in range(BANKS)]
        jobs = {}
        njobs = [0]

        def alloc(name, n):
            jobs[name] = njobs[0]
            njobs[0] += n

        def ps(job):
            return bank[job % BANKS]

        def wait_bank_free(pe, job):
            if job >= BANKS:
                pe.wait_ge(bank_free[job % BANKS], job // BANKS)

        def wait_bank_full(eng, job):
            eng.wait_ge(bank_full[job % BANKS], job // BANKS + 1)

        def full(job):
            return bank_full[job % BANKS]

        def free(job):
            return bank_free[job % BANKS]

        arena = sb("arena", [P, 38400])
        arena_at = nc.sbuf_base - 4 * 38400

        def carve(off, *shape, dt=None):
            n = 1
            for s in shape:
                n *= s
            ap = arena[:, off:off + n]
            if dt is not None:
                ap = ap.bitcast(dt)
            if len(shape) == 2:
                ap = ap.rearrange("p (a b) -> p a b", a=shape[0])
            if len(shape) == 3:
                ap = ap.rearrange("p (a b c) -> p a b c", a=shape[0], b=shape[1])
            if len(shape) == 4:
                ap = ap.rearrange("p (a b c d) -> p a b c d", a=shape[0], b=shape[1], c=shape[2])
            return ap

        ring = sb("ring", [P, SLOTS, HALF * WIDE])
        ring_at = nc.sbuf_base - 4 * SLOTS * HALF * WIDE

        def overlay(name, at, *shape):
            return nc.alloc_sbuf_tensor_at(name, [P, *shape], F32R, offset=at)

        w_split = [overlay("w_split0", arena_at + 4 * 28672, 2, HALF, WIDE),
                   overlay("w_split1", arena_at + 4 * 32768, 2, HALF, WIDE),
                   overlay("w_split2", ring_at + 4 * RAW_SLOTS * HALF * WIDE, 2, HALF, WIDE)]
        x_split = [overlay("x_high", arena_at + 4 * 2048, KC, L), overlay("x_low", arena_at + 4 * 26624, KC, L)]
        ff_split = overlay("ff_split", arena_at + 4 * 10240, 2, D_FF // P, L)
        ident = sb("ident", [P, P])
        ones = sb("ones", [P, L])
        select = sb("select", [P, 2, P])
        eps = sb("eps", [P, 1])
        level_mask = sb("level_mask", [P, 2, len(LEVELS), P], U8)
        stat = sb("stat", [P, 64])
        small = sb("small", [P, 1024])

        x_lat = carve(0, TT, D)
        mods = carve(2048, 4, D)
        mod1 = carve(6144, 4, D)
        val = carve(6144, 4, D)
        m_rows = [carve(10240, 2, WIDE), carve(16384, 2, WIDE)]
        b_rows = [arena[0:1, 11264:11264 + 2048].rearrange("p (a b) -> p a b", a=4),
                  arena[0:1, 17408:17408 + 2048].rearrange("p (a b) -> p a b", a=4)]
        decay = carve(10240, 2, 2 * UNITS, L)
        key = carve(16384, 2, 2 * UNITS, L)
        h_in = carve(16384, 4, D)
        qry = carve(22528, UNITS, L)
        gate_tmp = carve(24064, 2, 2, WIDE)
        state = carve(24064, 2 * UNITS, P)
        PB = 26112
        x_ctx = carve(PB, TT, D)
        hT = carve(PB + 2048, KC, 2 * L)
        hT_col = carve(PB, KC, L)
        rank_act = carve(PB + 6144, 2 * L)
        gk2 = carve(PB + 7168, 2, L)
        w_rank = carve(PB + 8704, KC, 32)
        crow = carve(PB + 9216, 1, P)
        keyT = carve(PB, TT, 2 * UNITS, P)
        lvlW = carve(PB, 2, UNITS, L)
        q_state = carve(PB + 3072, 2 * UNITS, L)
        sc_in = carve(PB + 3072, HEADS, TT, P)
        sc_x = carve(PB + 5120, HEADS, 2, P)
        lvlE = carve(PB + 7168, 2, UNITS, L)
        o_mix = carve(10240, TT, D)
        gate_out = carve(36352, TT, D)
        mixT = carve(PB + 7168, KC, L)
        sq_tmp = carve(PB, 2, D)
        row_a = carve(22528, 2, D)
        h2 = carve(6144, TT, D)
        h2T = carve(8192, KC, L)
        qT = carve(10240, 16, L)
        keys_raw = carve(14336, 2, P)
        keysT = carve(14592, 2, P)
        s_key = [carve(16384, 16, P), carve(19712, 16, P)]
        s_work = carve(18432, 2, P)
        cand = carve(18688, TOPK, TOPK)
        c_work = carve(18944, L)
        onehot = carve(19200, 2, TOPK, TOPK)
        top_v = carve(24576, 2, TOPK)
        top_i = carve(24608, 2, TOPK, dt=U32)
        top_f = carve(24640, 2, TOPK)
        best_v = carve(24672, PEER_HEADS, TOPK)
        best_p = carve(24800, TOPK, dt=U32)
        part_i = carve(24816, 2, TOPK, dt=U32)
        part_f = carve(24848, 2, TOPK)
        pick = carve(24880, 2, TOPK)
        iota_f = carve(26128, TOPK)
        gate_w = carve(26144, TT, GATHERS)
        act_w = carve(26400, TT, GATHERS)
        rows_i = carve(26656, TT, GATHERS, dt=U32)
        sm8 = carve(26912, 2, PEER_HEADS)
        now_i = carve(26928, GSLOTS, dt=U32)
        y_acc = carve(35328, 2, D)

        mix2 = carve(4096, TT, D)
        row_b = carve(6144, 2, D)
        h_tok = carve(8192, TT, D)
        ff_tmp = carve(36864, 3, 2, L)
        er = carve(8192, NSTATE, L)
        ei = carve(12288, NSTATE, L)
        Bz = carve(8192, NSTATE * 2, P).rearrange("p (r j) c -> p r j c", r=2)
        BT = carve(16384, 2, NSTATE, P)
        Cz = [carve(20480, NSTATE, P), carve(2048, NSTATE, P)]
        braw = carve(24576, 2, NSTATE, 16)
        bbar = carve(25088, 2, NSTATE, 16)
        craw = carve(4096, 2, 4, P)
        CT = carve(6144, 2, 4, P)
        e_tmp = carve(6144, 2 * D)
        b_tmp = carve(12288, NSTATE, 16)
        hT_s = carve(27136, KC, L)
        h_tok_s = carve(31232, TT, D)
        uT = carve(33792, 4, L)
        zT = carve(34816, 4, L)
        xs = carve(35840, 2, L)
        turned = [carve(27136, 2, 2, L), carve(28160, 2, 2, L)]
        rt = carve(36864, 2, 2, L)
        proj = carve(10240, TT, ATT_COLS)
        roped = carve(14592, TT, 24, 64)
        krope = carve(17664, TT, 5, P)
        qTa = carve(18944, 8, L)
        qiT = carve(20992, 4, L)
        kTa = carve(22016, 5, L)
        rope = carve(23296, TT, 2, HD)
        rope_t = carve(23552, TT, 29 * HD)
        idx_s = carve(27264, TT, L)
        idx_w = carve(27776, TT, L)
        keep = carve(28288, TT, L)
        rel = carve(28800, 2, 2, L)
        prob = carve(29824, 2, N_HEADS, L)
        pT = carve(14592, 2, N_HEADS, P)
        o_att = carve(8192, TT, D)

        def seen(t):
            return slice(0, P * (t + 1))

        w_full = [sem(f"w_full{s}") for s in range(SLOTS)]
        w_used = sem("w_used")
        w_high = sem("w_high")
        w_low = sem("w_low")
        x_high = sem("x_high")
        dve_step = sem("dve_step")
        act_step = sem("act_step")
        pool_step = sem("pool_step")
        load_c, load_x, load_gate, load_gain, load_rows, load_keys, load_norm, load_s5, \
            load_rope = [sem(f"load_{n}") for n in "c x gate gain rows keys norm s5 rope".split()]
        load_b = [sem(f"load_b{i}") for i in range(4)]
        consts = sem("consts")
        gk2_zero = sem("gk2_zero")
        c_silu = sem("c_silu")
        var_ready = sem("var_ready")
        x_ready = sem("x_ready")
        std_ready = sem("std_ready")
        tok_ready = sem("tok_ready")
        masks_ready = sem("masks_ready")
        hT_col_ready = sem("hT_col_ready")
        lb_exp = sem("lb_exp")
        lb_sum = sem("lb_sum")
        lb_log = sem("lb_log")
        gate_abs = sem("gate_abs")
        gate_diff = sem("gate_diff")
        gate_k = sem("gate_k")
        gate_log = sem("gate_log")
        gate_done = sem("gate_done")
        scans_done = sem("scans_done")
        ctx_exp = sem("ctx_exp")
        ctx_key = sem("ctx_key")
        q_exp = sem("q_exp")
        q_state_ready = sem("q_state_ready")
        lvl_diff = sem("lvl_diff")
        lvl_exp = sem("lvl_exp")
        lvl_ready = sem("lvl_ready")
        mixed = sem("mixed")
        best_ready = sem("best_ready")
        soft_ready = sem("soft_ready")
        rows_ready = sem("rows_ready")
        gathered = [sem(f"gathered{s}") for s in range(GSLOTS)]
        row_used = sem("row_used")
        gelu_done = sem("gelu_done")
        index_ready = sem("index_ready")
        rows_free = sem("rows_free")
        s5_exp = sem("s5_exp")
        s5_theta = sem("s5_theta")
        s5_sin = sem("s5_sin")
        s5_bbar = sem("s5_bbar")
        s5_b = sem("s5_b")
        s5_c = sem("s5_c")
        s5_table = sem("s5_table")
        s5_dt = sem("s5_dt")
        x_state = sem("x_state")
        y_used = sem("y_used")
        y_ready = sem("y_ready")
        z_ready = sem("z_ready")
        glu_sig = sem("glu_sig")
        ff_ready = sem("ff_ready")
        roped_ready = sem("roped_ready")
        rel_used = sem("rel_used")
        idx_causal = sem("idx_causal")
        keep_ready = sem("keep_ready")
        keep_causal = sem("keep_causal")
        logits_ready = sem("logits_ready")
        prob_ready = sem("prob_ready")
        out_ready = sem("out_ready")
        stored = sem("stored")

        NORM_USES = [("ln_in", 4), ("head", 16), ("post1", 2), ("mod2", 2), ("post2", 2)] + [
            (f"rms{i}", 2) for i in range(8)]
        norm_no = {n: i for i, (n, _) in enumerate(NORM_USES)}
        var_no = {n: i for i, n in enumerate(n for n, _ in NORM_USES if n not in ("rms0", "rms2", "rms4", "rms6"))}
        tok_no, at = {}, 0
        for n, c in [("in", 4), ("mix", 2), ("h2", 2), ("ssm", 2), ("mlp0", 2), ("att", 2), ("mlp1", 2)]:
            tok_no[n] = at
            at += c

        alloc("cT", 1)
        for n in range(4):
            alloc(f"ada{n}", 1)
            if n:
                alloc(f"adab{n - 1}", 2)
        alloc("adab3", 2)
        alloc("T_in", 8)
        for name, n in [("lb", 1), ("hff", 4), ("hfb", 4), ("rank", 1), ("gqk", 4), ("hq", 4), ("gla_gate", 4),
                        ("hi", 4), ("gv", 4), ("hg", 2), ("gg", 2), ("keyT", 6), ("state", 4), ("inter", 6),
                        ("ada4", 1), ("scx", 4), ("diag", 4), ("ada5", 1), ("adab4", 1)]:
            alloc(name, n)
        for lv in range(len(LEVELS)):
            alloc(f"lvl{lv}", 4)
            if lv + 6 < 12:
                alloc(f"ada{lv + 6}", 1)
            alloc(f"adab{lv + 5}", 1)
        for name, n in [("o", 4), ("T_mix", 4), ("out", 4), ("T_h2", 4), ("keys", 1)] + [
                        x for n in range(4) for x in ((f"wq{n}", 2), (f"skey{n}", 2))] + [("s5p", 1), ("CT", 2), ("BT", 8), ("T_ssm", 4), ("ssm_in", 2)]:
            alloc(name, n)
        for j in range(NSTATE):
            if j % 4 == 0:
                alloc(f"y{j // 4}", 1)
            alloc(f"bu{j}", 1)
        for name, n in [("glu", 2), ("ssm_out", 4), ("T_mlp0", 4), ("mlp0a", 32), ("mlp0b", 4), ("T_att", 4),
                        ("att", 10), ("rT", 10), ("idx", 8), ("att_s0", 8), ("att_s1", 8), ("pT0", 4), ("pv0", 2),
                        ("pT1", 8), ("pv1", 2), ("T_atto", 4), ("att_out", 4), ("T_mlp1", 4), ("mlp1a", 32),
                        ("mlp1b", 4)]:
            alloc(name, n)

        stream, tile_no, given_back = [], {}, {}
        slot_of, turn_of, former = [], [], []
        split_no, split_back = {}, []

        def weights(name, w, col0, cols, job, split=None):
            tile_no[name] = len(stream)
            for k, r in enumerate(range(0, w.shape[0], HALF * P)):
                n = len(stream)
                if split is None:
                    given_back[n] = job
                else:
                    split_no[n] = len(split_back)
                    split_back.append(job if k % split == split - 1 else None)
                raw = SLOTS if n < tile_no.get("mlp0a0", n + 1) else RAW_SLOTS
                slot = n % SLOTS if raw == SLOTS else (n - tile_no["mlp0a0"]) % RAW_SLOTS
                slot_of.append(slot)
                turn_of.append(slot_of.count(slot))
                former.append(max([m for m in range(n) if slot_of[m] == slot], default=None))
                stream.append(w[r:r + HALF * P, col0:col0 + cols].rearrange("(k p) n -> p k n", p=P))

        def wtile(n, cols=WIDE):
            return ring[:, slot_of[n], 0:HALF * cols].rearrange("p (k n) -> p k n", k=HALF)

        def wait_weights(pe, n):
            pe.wait_ge(w_full[slot_of[n]], 16 * turn_of[n])

        w_in = A["w_in"][0]
        for n in range(4):
            weights(f"ada{n}", A["w_ada"][0], n * WIDE, WIDE, jobs[f"ada{n}"])
        for name, c0, n in [("hff", 512, 4), ("hfb", 1024, 4), ("gqk", 2560, 4), ("hq", 0, 4), ("hi", 1536, 4),
                            ("gv", 3072, 4), ("hg", 2048, 2), ("gg", 3584, 2)]:
            weights(name, w_in, c0, WIDE, jobs[name] + n - 1)
        for n in range(4, 12):
            weights(f"ada{n}", A["w_ada"][0], n * WIDE, WIDE, jobs[f"ada{n}"])
        for n in range(2):
            weights(f"out{n}", A["w_out"][0], n * WIDE, WIDE, jobs["out"] + 2 * n + 1)
        for n in range(4):
            weights(f"wq{n}", A["peer_w_query"][0], n * WIDE, WIDE, jobs[f"wq{n}"] + 1)
        weights("ssm_in", A["ssm_w_in_2"][0], 0, WIDE, jobs["ssm_in"] + 1)
        weights("glu", A["ssm_w_glu_2"][0], 0, WIDE, jobs["glu"] + 1)
        for n in range(2):
            weights(f"ssm_out{n}", A["ssm_w_out_2"][0], n * WIDE, WIDE, jobs["ssm_out"] + 2 * n + 1)
        for i in range(2):
            for n in range(8):
                weights(f"mlp{i}a{n}", A["mlp_w1_2"][i], n * WIDE, WIDE, jobs[f"mlp{i}a"] + 4 * n + 3, split=2)
            for n in range(2):
                weights(f"mlp{i}b{n}", A["mlp_w2_2"][i], n * WIDE, WIDE, jobs[f"mlp{i}b"] + 2 * n + 1, split=8)
            if i == 0:
                for n in range(5):
                    weights(f"att{n}", A["att_w_in_2"][0], n * WIDE, min(WIDE, ATT_COLS - n * WIDE),
                            jobs["att"] + 2 * n + 1, split=2)
                for n in range(2):
                    weights(f"att_out{n}", A["att_w_out_2"][0], n * WIDE, WIDE, jobs["att_out"] + 2 * n + 1, split=2)

        gath = [arena[:, 27136 + D * i:27136 + D * (i + 1)] for i in range(8)] + [
            ring[:, slot_of[tile_no["wq1"] + i // 2], D * (i % 2):D * (i % 2 + 1)] for i in range(8)]

        bgk_raw = small[:, 0:128]
        lb_raw = small[:, 128:256]
        gain = small[:, 256:512].rearrange("p (a b) -> p a b", a=2)
        bgk = small[:, 512:516]
        one_lb = small[:, 516:524]
        log_lb = small[:, 524:532]
        log1m_lb = small[:, 532:540]
        lb = small[:, 540:548]
        cT = small[:, 592:848].rearrange("p (k w) -> p k w", w=32)
        b_end = small[:, 564:576]
        lb_t = small[:, 576:584]
        S5 = {n: small[:, 16 * i:16 * i + 16] for i, n in enumerate(
            "lr li dt mag th kk r sn hs cs ar ai den nr fr fi t1 t2 pr pi qr qi".split())}
        d_col = small[:, 360:364]
        s5_raw = carve(25600, 3, P)
        d_raw = carve(25984, P)
        dt_raw = carve(26112, 2)
        wi_col = small[:, 0:16].rearrange("p (t h) -> p t h", t=2)
        m8 = small[:, 16:24]
        mx16 = small[:, 24:56].rearrange("p (t h) -> p t h", t=2)
        sum16 = small[:, 56:88].rearrange("p (t h) -> p t h", t=2)
        it_t = gate_out[:, 0, 0:P].bitcast(I32)
        it_s = gate_out[:, 0, P:2 * P].bitcast(I32)
        it_x = gate_out[:, 0, 2 * P:3 * P].bitcast(I32)
        it_f = gate_out[:, 0, 3 * P:4 * P]
        it_g = gate_out[:, 0, 4 * P:5 * P]

        HEAD_AT = [0, 1, 2, 3, 4, 6, 5, 7]

        def unit_rows(place):
            head = HEAD_AT[place]
            if head < HG_HEADS:
                return head, slice(0, P)
            g = head - HG_HEADS
            return HG_HEADS + g // 2, slice(64 * (g % 2), 64 * (g % 2) + 64)

        def far_half(ap, d, h):
            c = 1 - d
            if len(ap.shape) == 2:
                return ap.rearrange("p (n c h) -> p n c h", c=2, h=h)[:, :, c, :]
            return ap.rearrange("p b (n c h) -> p b n c h", c=2, h=h)[:, :, :, c, :]

        LEVEL_BLOCKS = [[(d, p, t) for p in range(4) for t in range(TT)] for d in range(2)] + [
            [(d, p, t) for d in range(2) for p in pair for t in range(TT)] for pair in ((4, 5), (6, 7))]

        counts = {}

        def step(eng, name, ins):
            counts[name] = counts.get(name, 0) + 1
            ins.then_inc({"dve": dve_step, "act": act_step, "pool": pool_step}[name], 1)
            eng.wait_ge({"dve": dve_step, "act": act_step, "pool": pool_step}[name], counts[name])

        def mark(eng, ins, s):
            counts[s.name] = counts.get(s.name, 0) + 1
            ins.then_inc(s, 1)
            eng.wait_ge(s, counts[s.name])

        def read_out(eng, ins, job):
            ins.then_inc(free(job), 1)
            eng.wait_ge(free(job), job // BANKS + 1)

        def wait_read_out(eng, job):
            eng.wait_ge(free(job), job // BANKS + 1)

        def by_cols(ap):
            return ap.rearrange("p (w r) -> p r w", r=ROWS)

        def by_rows(ap):
            return ap.rearrange("p (r w) -> p r w", r=ROWS)

        block = ctx.enter_context(nc.Block())

        @block.sync
        def _(sp):
            ada_at = {tile_no[f"ada{n}"]: n for n in range(12)}
            for n, src in enumerate(stream):
                if n in ada_at:
                    b = ada_at[n]
                    if b >= 4:
                        wait_bank_full(sp, jobs[f"adab{b - 4}"] + (1 if b - 4 < 4 else 0))
                    if b == 4:
                        sp.wait_ge(ctx_key, 1)
                    sp.dma_start(b_rows[b >= 4][:, b % 4, :], A["b_ada"][:, b * WIDE:(b + 1) * WIDE]).then_inc(load_b[b % 4], 16)
                if n == tile_no["ssm_in"]:
                    sp.wait_ge(row_used, 2 * TT * GATHERS)
                old = former[n]
                if old in split_no:
                    sp.wait_ge(w_low, split_no[old] + 1)
                elif old is not None:
                    wait_bank_full(sp, given_back[old])
                sp.dma_start(wtile(n, src.shape[2]), src).then_inc(w_full[slot_of[n]], 16)
            sp.wait_ge(out_ready, 1)
            sp.dma_start(out[0].rearrange("(t p) d -> p t d", p=P), x_lat).then_inc(stored, 16)
            sp.wait_ge(stored, 16)

        @block.gpsimd
        def _(pool):
            def do(ins):
                step(pool, "pool", ins)

            pool.memset(gk2[0:2 * RANK, :, :], 0.0).then_inc(gk2_zero, 1)
            pool.memset(cT, 0.0).then_inc(consts, 1)
            pool.memset(ones[:], 1.0).then_inc(consts, 1)
            pool.memset(eps[:], EPS).then_inc(consts, 1)
            pool.iota(it_t, [[1, P]], base=0, channel_multiplier=0).then_inc(consts, 1)
            pool.iota(it_s, [[0, P]], base=0, channel_multiplier=1).then_inc(consts, 1)
            do(pool.memset(ident[:], 0.0))
            pool.affine_select(out=ident[:], in_=ident[:], compare_op=ALU.not_equal, fill=1.0, base=0,
                               pattern=[[-1, P]], channel_multiplier=1).then_inc(consts, 1)
            do(pool.memset(select[:], 0.0))
            for i in range(4):
                ins = pool.affine_select(out=select[:], in_=select[:], compare_op=ALU.not_equal, fill=1.0, base=-32 * i,
                                         pattern=[[-1, 2], [0, P]], channel_multiplier=1)
                if i < 3:
                    do(ins)
            ins.then_inc(consts, 1)

            for j in range(4, 8):
                wait_read_out(pool, jobs["T_in"] + j)
            for k in range(KC):
                ins = pool.tensor_copy(by_cols(hT_col[:, k, :]), by_rows(hT[:, k, L:2 * L]))
                if k < KC - 1:
                    do(ins)
            mark(pool, ins, hT_col_ready)

            loop = 0
            for t in range(TT):
                for table in (A["peer_u"][0], A["peer_v"][0]):
                    base = loop * GATHERS

                    def gather(s):
                        pool.indirect_dma_start(
                            out=gath[s], out_offset=None, in_=table,
                            in_offset=bass.IndirectOffsetOnAxis(ap=now_i[:, s:s + 1], axis=0),
                        ).then_inc(gathered[s], 16)

                    if loop == 0:
                        pool.wait_ge(rows_ready, 1)
                        for s in range(GSLOTS):
                            if s in (8, 12):
                                wait_bank_full(pool, jobs[f"wq{s // 4 - 1}"] + 1)
                            do(pool.tensor_copy(now_i[:, s:s + 1], rows_i[:, t, s:s + 1]))
                            gather(s)
                    head0 = 1 if loop == 0 else 0
                    first = counts["pool"] - head0 * TOPK
                    with pool.Fori(head0, PEER_HEADS) as head:
                        if loop % 2 == 0:
                            pool.wait_ge(rows_ready, head + (PEER_HEADS * t + 1))
                        i = head * TOPK
                        for s in range(GSLOTS):
                            pool.wait_ge(row_used, i + (base + s + 1 - GSLOTS))
                            pool.tensor_copy(now_i[:, s:s + 1], rows_i[:, t, bass.ds(i + s, 1)]).then_inc(pool_step, 1)
                            pool.wait_ge(pool_step, i + (first + s + 1))
                            pool.sem_inc(index_ready, 1)
                            gather(s)
                    counts["pool"] = first + GATHERS
                    loop += 1

            for t in range(TT):
                pool.wait_ge(rel_used, 4 * t + 4)
                pool.affine_select(out=idx_s[:, t, seen(t)], in_=idx_s[:, t, seen(t)], compare_op=ALU.is_ge, fill=-1.0e38,
                                   base=t * P, pattern=[[-1, P * (t + 1)]], channel_multiplier=1).then_inc(idx_causal, 1)
            for t in range(TT):
                pool.wait_ge(keep_ready, t + 1)
                pool.affine_select(out=keep[:, t, seen(t)], in_=keep[:, t, seen(t)], compare_op=ALU.is_ge, fill=NEG,
                                   base=t * P, pattern=[[-1, P * (t + 1)]], channel_multiplier=1).then_inc(keep_causal, 1)

        def mm(o, lhsT, rhs, first, last):
            return nc.tensor.matmul(o, lhsT, rhs, start=first, stop=last)

        def pe_feature(pe, job0, tile, kc, n_blocks, cols, x, per_job):
            for m in range((kc + HALF - 1) // HALF):
                wait_weights(pe, tile + m)
            for b in range(n_blocks):
                job = job0 + b // per_job
                c0 = (b % per_job) * cols
                if b % per_job == 0:
                    wait_bank_free(pe, job)
                for k in range(kc):
                    last = mm(ps(job)[:, c0:c0 + cols], wtile(tile + k // HALF)[:, k % HALF, b * P:(b + 1) * P],
                              x(k), k == 0, k == kc - 1)
                if b % per_job == per_job - 1:
                    last.then_inc(full(job), 1)

        def pe_token(pe, job0, tile, kc, xs_of_tile, cols=WIDE):
            for m in range((kc + HALF - 1) // HALF):
                wait_weights(pe, tile + m)
            for i, x in enumerate(xs_of_tile):
                wait_bank_free(pe, job0 + i)
                for k in range(kc):
                    last = mm(ps(job0 + i)[:, 0:cols], x(k), wtile(tile + k // HALF, cols)[:, k % HALF, :],
                              k == 0, k == kc - 1)
                last.then_inc(full(job0 + i), 1)

        def pe_transpose(pe, name, tiles, n_tiles):
            for t in range(n_tiles):
                if name == "atto":
                    for g in range(2):
                        wait_read_out(pe, jobs[f"pv{t}"] + g)
                else:
                    pe.wait_ge(tok_ready, tok_no[name] + t + 1)
                for g in range(2):
                    job = jobs["T_" + name] + 2 * t + g
                    wait_bank_free(pe, job)
                    for b in range(4):
                        last = nc.tensor.transpose(ps(job)[:, b * P:(b + 1) * P],
                                                   tiles[:, t, (4 * g + b) * P:(4 * g + b + 1) * P], ident[:])
                    last.then_inc(full(job), 1)

        def wait_transposed(pe, name, t0, n_tiles):
            for j in range(2 * t0, 2 * (t0 + n_tiles)):
                wait_read_out(pe, jobs["T_" + name] + j)

        def tile_of(xT, t):
            return lambda k: xT[:, k, t * P:(t + 1) * P]

        def pe_ada(pe):
            pe.wait_ge(consts, 7)
            pe.wait_ge(c_silu, 1)
            nc.tensor.transpose(ps(jobs["cT"])[:, 0:16], crow[0:16, 0, :], ident[0:16, 0:16]).then_inc(full(jobs["cT"]), 1)
            wait_read_out(pe, jobs["cT"])
            for n in range(5):
                if n < 4:
                    pe_ada_rows(pe, n)
                if n:
                    pe_ada_spread(pe, n - 1)

        def pe_ada_rows(pe, n):
            job = jobs[f"ada{n}"]
            wait_weights(pe, tile_no[f"ada{n}"])
            wait_weights(pe, tile_no[f"ada{n}"] + 1)
            wait_bank_free(pe, job)
            for k in range(KC):
                c = k % 4
                last = nc.tensor.matmul(ps(job)[32 * c:32 * c + 32, :], cT[:, k, :],
                                        wtile(tile_no[f"ada{n}"] + k // HALF)[:, k % HALF, :],
                                        start=k < 4, stop=k >= 4, tile_position=(0, 32 * c))
            last.then_inc(full(job), 1)

        def pe_ada_spread(pe, n):
            wait_read_out(pe, jobs[f"ada{n}"])
            pe.wait_ge(load_b[n % 4], 16 * (n // 4 + 1))
            for w in range(2 if n < 4 else 1):
                job = jobs[f"adab{n}"] + w
                wait_bank_free(pe, job)
                mm(ps(job)[:, :], select[:, w, :], m_rows[n >= 4][:, n % 2, :], True, False)
                mm(ps(job)[:, :], ones[0:1, 0:P], b_rows[n >= 4][:, n % 4, :], False, True).then_inc(full(job), 1)

        def pe_project(pe):
            pe_transpose(pe, "in", h_in, 4)
            job = jobs["lb"]
            wait_bank_free(pe, job)
            pe.wait_ge(load_gate, 80)
            nc.tensor.transpose(ps(job)[:, 0:8], lb_raw[0:8, :], ident[0:8, 0:8])
            nc.tensor.transpose(ps(job)[:, 8:12], bgk_raw[0:4, :], ident[0:4, 0:4]).then_inc(full(job), 1)
            wait_transposed(pe, "in", 0, 4)
            every = lambda k: hT[:, k, :]
            latent = lambda k: hT[:, k, L:2 * L]
            for name in ("hff", "hfb"):
                pe_feature(pe, jobs[name], tile_no[name], KC, 4, 2 * L, every, 1)
            job = jobs["rank"]
            wait_bank_free(pe, job)
            for k in range(KC):
                last = mm(ps(job)[0:2 * RANK, :], w_rank[:, k, :], hT[:, k, :], k == 0, k == KC - 1)
            last.then_inc(full(job), 1)
            for m in range(2):
                wait_weights(pe, tile_no["gqk"] + m)
            for b in range(4):
                job = jobs["gqk"] + b
                wait_bank_free(pe, job)
                cols = 2 * L if b >= 2 else L
                for k in range(KC):
                    last = mm(ps(job)[:, 0:cols], wtile(tile_no["gqk"] + k // HALF)[:, k % HALF, b * P:(b + 1) * P],
                              hT[:, k, 2 * L - cols:2 * L], k == 0, k == KC - 1)
                last.then_inc(full(job), 1)
            pe_feature(pe, jobs["hq"], tile_no["hq"], KC, 4, L, latent, 1)
            for j in range(4):
                job = jobs["gla_gate"] + j
                wait_read_out(pe, jobs["rank"])
                wait_bank_free(pe, job)
                mm(ps(job)[:, :], gk2[0:2 * RANK, j // 2, (j % 2) * P:(j % 2 + 1) * P], rank_act[0:2 * RANK, :],
                   True, True).then_inc(full(job), 1)

            def row_major(tok):
                return lambda k: hT[:, k, tok * P:(tok + 1) * P]

            def col_major(t):
                return lambda k: hT_col[:, k, t * P:(t + 1) * P]

            pe_token(pe, jobs["hi"], tile_no["hi"], KC, [row_major(i) for i in range(4)])
            pe.wait_ge(hT_col_ready, 1)
            pe_token(pe, jobs["gv"], tile_no["gv"], KC, [row_major(0), row_major(1), col_major(0), col_major(1)])
            pe_token(pe, jobs["hg"], tile_no["hg"], KC, [row_major(2), row_major(3)])
            pe_token(pe, jobs["gg"], tile_no["gg"], KC, [col_major(0), col_major(1)])

        def pe_states(pe):
            pe.wait_ge(ctx_key, 1)
            for t in range(TT):
                for g in range(3):
                    job = jobs["keyT"] + 3 * t + g
                    wait_bank_free(pe, job)
                    for b in range(4):
                        last = nc.tensor.transpose(ps(job)[:, b * P:(b + 1) * P],
                                                   decay[:, 0, 4 * g + b, t * P:(t + 1) * P], ident[:])
                    last.then_inc(full(job), 1)
            for j in range(6):
                wait_read_out(pe, jobs["keyT"] + j)
            for name in ("hi", "gv"):
                for j in range(4):
                    wait_read_out(pe, jobs[name] + j)
            for j in range(4):
                d, gla = j % 2, j // 2
                job = jobs["state"] + j
                wait_bank_free(pe, job)
                for b in range(2 if gla else 4):
                    w = 2 * P if gla else P
                    for t in range(TT):
                        last = mm(ps(job)[:, b * w:(b + 1) * w], keyT[:, t, d * UNITS + 4 * gla + b, :],
                                  val[:, t, 512 * gla + b * w:512 * gla + (b + 1) * w], t == 0, t == TT - 1)
                last.then_inc(full(job), 1)
            pe.wait_ge(q_state_ready, 1)
            for j in range(4):
                wait_read_out(pe, jobs["state"] + j)
            for t in range(TT):
                for g, (p0, p1) in enumerate(((0, 4), (4, 6), (6, 8))):
                    job = jobs["inter"] + 3 * t + g
                    wait_bank_free(pe, job)
                    for b in range(p1 - p0):
                        u, rows = unit_rows(p0 + b)
                        for d in range(2):
                            last = mm(ps(job)[:, b * P:(b + 1) * P], q_state[rows, d * UNITS + u, t * P:(t + 1) * P],
                                      state[rows, d * UNITS + u, :], d == 0, d == 1)
                    last.then_inc(full(job), 1)

        def pe_scores(pe):
            pe_ada_rows(pe, 4)
            pe.wait_ge(lvl_ready, 1)
            first, second = slice(0, P), slice(P, 2 * P)
            for j in range(4):
                job = jobs["scx"] + j
                wait_bank_free(pe, job)
                for b in range(4):
                    u, rows = unit_rows(2 * j + b // 2)
                    d = b % 2
                    ks, qs = (first, second) if d == 0 else (second, first)
                    last = mm(ps(job)[:, b * P:(b + 1) * P], lvlW[rows, d, u, ks], lvlW[rows, d, u, qs], True, True)
                last.then_inc(full(job), 1)
            for j in range(4):
                job = jobs["diag"] + j
                wait_bank_free(pe, job)
                for b in range(4):
                    u, rows = unit_rows(2 * j + b // 2)
                    t = b % 2
                    for d in range(2):
                        last = mm(ps(job)[:, b * P:(b + 1) * P], key[rows, 1, d * UNITS + u, t * P:(t + 1) * P],
                                  qry[rows, u, t * P:(t + 1) * P], d == 0, d == 1)
                last.then_inc(full(job), 1)
            pe_ada_rows(pe, 5)
            pe_ada_spread(pe, 4)
            for lv, h in enumerate(LEVELS):
                pe.wait_ge(lvl_ready, lv + 2)
                for j, blocks in enumerate(LEVEL_BLOCKS):
                    job = jobs[f"lvl{lv}"] + j
                    wait_bank_free(pe, job)
                    for b, (d, p, t) in enumerate(blocks):
                        u, rows = unit_rows(p)
                        w = lvlW[rows, d, u, t * P:(t + 1) * P]
                        o = ps(job)[:, 64 * b:64 * (b + 1)].rearrange("p (n h) -> p n h", h=h)
                        last = mm(o, w, far_half(w, d, h), True, True)
                    last.then_inc(full(job), 1)
                if lv + 6 < 12:
                    pe_ada_rows(pe, lv + 6)
                pe_ada_spread(pe, lv + 5)
            for j in range(4):
                wait_read_out(pe, jobs[f"lvl{len(LEVELS) - 1}"] + j)
            for t in range(TT):
                for g in range(2):
                    job = jobs["o"] + 2 * t + g
                    wait_bank_free(pe, job)
                    for b in range(4):
                        h = HEAD_AT.index(4 * g + b)
                        v = slice((4 * g + b) * P, (4 * g + b + 1) * P)
                        mm(ps(job)[:, b * P:(b + 1) * P], sc_in[:, h, t, :], val[:, 2 + t, v], True, False)
                        last = mm(ps(job)[:, b * P:(b + 1) * P], sc_x[:, h, 1 - t, :], val[:, 3 - t, v], False, True)
                    last.then_inc(full(job), 1)

        def pe_experts(pe):
            pe_transpose(pe, "mix", o_mix, 2)
            wait_transposed(pe, "mix", 0, 2)
            for n in range(2):
                pe_token(pe, jobs["out"] + 2 * n, tile_no[f"out{n}"], KC, [tile_of(mixT, t) for t in range(TT)])
            pe_transpose(pe, "h2", h2, 2)
            job = jobs["keys"]
            wait_bank_free(pe, job)
            pe.wait_ge(load_keys, 16)
            nc.tensor.transpose(ps(job)[:, 0:P], keys_raw[:, 0, :], ident[:])
            nc.tensor.transpose(ps(job)[:, P:2 * P], keys_raw[:, 1, :], ident[:]).then_inc(full(job), 1)
            wait_transposed(pe, "h2", 0, 2)
            wait_read_out(pe, jobs["keys"])
            for n in range(4):
                pe_feature(pe, jobs[f"wq{n}"], tile_no[f"wq{n}"], KC, 4, L, lambda k: h2T[:, k, :], 2)
                for j in range(2):
                    wait_read_out(pe, jobs[f"wq{n}"] + j)
                for t in range(TT):
                    job = jobs[f"skey{n}"] + t
                    wait_bank_free(pe, job)
                    for b in range(4):
                        last = mm(ps(job)[:, b * P:(b + 1) * P], qT[:, 4 * n + b, t * P:(t + 1) * P],
                                  keysT[:, b % 2, :], True, True)
                    last.then_inc(full(job), 1)

        def pe_s5(pe):
            job = jobs["s5p"]
            wait_bank_free(pe, job)
            pe.wait_ge(load_s5, 16 * 10)
            pe.wait_ge(s5_dt, 1)
            for i in range(3):
                nc.tensor.transpose(ps(job)[:, 16 * i:16 * i + 16], s5_raw[0:16, i, :], ident[0:16, 0:16])
            nc.tensor.transpose(ps(job)[:, 48:52], d_raw[0:4, :], ident[0:4, 0:4]).then_inc(full(job), 1)
            for r in range(2):
                job = jobs["CT"] + r
                wait_bank_free(pe, job)
                for b in range(4):
                    last = nc.tensor.transpose(ps(job)[:, b * P:(b + 1) * P], craw[:, r, b, :], ident[:])
                last.then_inc(full(job), 1)
            pe.wait_ge(s5_b, 1)
            for r in range(2):
                for g in range(4):
                    job = jobs["BT"] + 4 * r + g
                    wait_bank_free(pe, job)
                    for b in range(4):
                        last = nc.tensor.transpose(ps(job)[:, b * P:(b + 1) * P], Bz[:, r, 4 * g + b, :], ident[:])
                    last.then_inc(full(job), 1)
            pe_transpose(pe, "ssm", h_tok_s, 2)
            wait_transposed(pe, "ssm", 0, 2)
            pe_feature(pe, jobs["ssm_in"], tile_no["ssm_in"], KC, 4, L, lambda k: hT_s[:, k, :], 2)
            for j in range(2):
                wait_read_out(pe, jobs["ssm_in"] + j)
            for j in range(8):
                wait_read_out(pe, jobs["BT"] + j)
            pe.wait_ge(s5_c, 1)

            def output(j):
                a = j // 4
                if j % 4 == 0:
                    wait_bank_free(pe, jobs[f"y{a}"])
                pe.wait_ge(x_state, j + 1)
                for c in range(2):
                    for part in range(2):
                        last = mm(ps(jobs[f"y{a}"])[:, 0:L], Cz[part][:, j, :], turned[j % 2][:, c, part, :],
                                  (j % 4, c, part) == (0, 0, 0), (j % 4, c, part) == (3, 1, 1))
                last.then_inc(*((full(jobs[f"y{a}"]), 1) if j % 4 == 3 else (y_used, 1)))

            for j in range(NSTATE):
                job = jobs[f"bu{j}"]
                wait_bank_free(pe, job)
                for r in range(2):
                    last = mm(ps(job)[:, r * L:(r + 1) * L], BT[:, r, j, :], uT[:, j // 4, :], True, True)
                last.then_inc(full(job), 1)
                if j:
                    output(j - 1)
            output(NSTATE - 1)
            for j in range(4):
                pe.wait_ge(z_ready, j + 1)
            pe_feature(pe, jobs["glu"], tile_no["glu"], HALF, 4, L, lambda k: zT[:, k, :], 2)
            pe.wait_ge(y_ready, 1)
            for n in range(2):
                pe_token(pe, jobs["ssm_out"] + 2 * n, tile_no[f"ssm_out{n}"], HALF, [tile_of(zT, t) for t in range(TT)])

        PASSES = ((0, 0), (0, 1), (1, 0))

        def pe_token_split(pe, job0, tile, cols=WIDE):
            for m in range(2):
                q = split_no[tile + m]
                w = w_split[q % SPLIT_SLOTS]
                pe.wait_ge(w_low, q + 1)
                for t in range(TT):
                    if m == 0:
                        wait_bank_free(pe, job0 + t)
                    for k in range(HALF):
                        for c, (xs_, ws) in enumerate(PASSES):
                            last = mm(ps(job0 + t)[:, 0:cols], x_split[xs_][:, HALF * m + k, t * P:(t + 1) * P],
                                      w[:, ws, k, 0:cols], (m, k, c) == (0, 0, 0), (m, k, c) == (1, HALF - 1, 2))
                    if m == 1:
                        last.then_inc(full(job0 + t), 1)
                if m == 0:
                    last.then_inc(w_used, 1)

        def pe_mlp(pe, i):
            pe_transpose(pe, f"mlp{i}", h_tok, 2)
            wait_transposed(pe, f"mlp{i}", 0, 2)
            for n in range(8):
                for m in range(2):
                    q = split_no[tile_no[f"mlp{i}a{n}"] + m]
                    w = w_split[q % SPLIT_SLOTS]
                    pe.wait_ge(w_low, q + 1)
                    for b in range(4):
                        job = jobs[f"mlp{i}a"] + 4 * n + b
                        if m == 0:
                            wait_bank_free(pe, job)
                        for k in range(HALF):
                            for c, (ws, xs_) in enumerate(PASSES):
                                last = mm(ps(job)[:, 0:L], w[:, ws, k, b * P:(b + 1) * P], x_split[xs_][:, HALF * m + k, :],
                                          (m, k, c) == (0, 0, 0), (m, k, c) == (1, HALF - 1, 2))
                        if m == 1:
                            last.then_inc(full(job), 1)
                    if m == 0:
                        last.then_inc(w_used, 1)
            for n in range(2):
                for t in range(TT):
                    wait_bank_free(pe, jobs[f"mlp{i}b"] + 2 * n + t)
                for kh in range(8):
                    q = split_no[tile_no[f"mlp{i}b{n}"] + kh]
                    w = w_split[q % SPLIT_SLOTS]
                    pe.wait_ge(w_low, q + 1)
                    if n == 0:
                        pe.wait_ge(ff_ready, 16 * i + 2 * kh + 2)
                    for t in range(TT):
                        job = jobs[f"mlp{i}b"] + 2 * n + t
                        for k in range(HALF):
                            for c, (fs, ws) in enumerate(PASSES):
                                last = mm(ps(job)[:, :], ff_split[:, fs, HALF * kh + k, t * P:(t + 1) * P], w[:, ws, k, :],
                                          (kh, k, c) == (0, 0, 0), (kh, k, c) == (7, HALF - 1, 2))
                        if kh == 7:
                            last.then_inc(full(job), 1)
                    if kh < 7:
                        last.then_inc(w_used, 1)

        def pe_attention(pe):
            pe_transpose(pe, "att", h_tok, 2)
            wait_transposed(pe, "att", 0, 2)
            for n in range(5):
                pe_token_split(pe, jobs["att"] + 2 * n, tile_no[f"att{n}"], min(WIDE, ATT_COLS - n * WIDE))
            for t in range(TT):
                pe.wait_ge(roped_ready, t + 1)
                blocks = [roped[:, t, 2 * i:2 * i + 2, :] for i in range(12)] + [krope[:, t, i, :] for i in range(5)]
                for g in range(5):
                    job = jobs["rT"] + 5 * t + g
                    wait_bank_free(pe, job)
                    for b, x in enumerate(blocks[4 * g:4 * g + 4]):
                        last = nc.tensor.transpose(ps(job)[:, b * P:(b + 1) * P], x, ident[:])
                    last.then_inc(full(job), 1)
            for j in range(10):
                wait_read_out(pe, jobs["rT"] + j)
            for t in range(TT):
                for g in range(4):
                    job = jobs["idx"] + 4 * t + g
                    wait_bank_free(pe, job)
                    rows = slice(64 * (g % 2), 64 * (g % 2) + 64)
                    for b in range(2):
                        last = mm(ps(job)[:, b * L:b * L + P * (t + 1)], qiT[rows, 2 * (g // 2) + b, t * P:(t + 1) * P],
                                  kTa[rows, 4, seen(t)], True, True)
                    last.then_inc(full(job), 1)
            for t in range(TT):
                for g in range(8):
                    job = jobs[f"att_s{t}"] + g
                    wait_bank_free(pe, job)
                    rows = slice(64 * (g % 2), 64 * (g % 2) + 64)
                    for b in range(2):
                        last = mm(ps(job)[:, b * L:b * L + P * (t + 1)], qTa[rows, 2 * (g // 2) + b, t * P:(t + 1) * P],
                                  kTa[rows, g // 2, seen(t)], True, True)
                    last.then_inc(full(job), 1)
            for t in range(TT):
                pe.wait_ge(prob_ready, t + 1)
                for s in range(t + 1):
                    for g in range(4):
                        job = jobs[f"pT{t}"] + 4 * s + g
                        wait_bank_free(pe, job)
                        for b in range(4):
                            last = nc.tensor.transpose(ps(job)[:, b * P:(b + 1) * P],
                                                       prob[:, t, 4 * g + b, s * P:(s + 1) * P], ident[:])
                        last.then_inc(full(job), 1)
                for j in range(4 * (t + 1)):
                    wait_read_out(pe, jobs[f"pT{t}"] + j)
                for g in range(2):
                    job = jobs[f"pv{t}"] + g
                    wait_bank_free(pe, job)
                    for b in range(8):
                        h = 8 * g + b
                        c = 1280 + HD * (h // 4)
                        for s in range(t + 1):
                            last = mm(ps(job)[:, b * HD:(b + 1) * HD], pT[:, s, h, :], proj[:, s, c:c + HD], s == 0, s == t)
                    last.then_inc(full(job), 1)
            pe_transpose(pe, "atto", o_att, 2)
            wait_transposed(pe, "atto", 0, 2)
            for n in range(2):
                pe_token_split(pe, jobs["att_out"] + 2 * n, tile_no[f"att_out{n}"])

        @block.tensor
        def _(pe):
            pe_ada(pe)
            pe_project(pe)
            pe_states(pe)
            pe_scores(pe)
            pe_experts(pe)
            pe_s5(pe)
            pe_mlp(pe, 0)
            pe_attention(pe)
            pe_mlp(pe, 1)

        def act_transposed(act, name, xT, n_tiles):
            for t in range(n_tiles):
                for g in range(2):
                    job = jobs["T_" + name] + 2 * t + g
                    wait_bank_full(act, job)
                    read_out(act, act.activation(xT[:, 4 * g:4 * g + 4, t * P:(t + 1) * P],
                                                 ps(job)[:, :].rearrange("p (k t) -> p k t", k=4), ACT.Copy), job)

        def norm_sqrt(act, name, scale):
            cols = dict(NORM_USES)[name]
            if name in var_no:
                act.wait_ge(var_ready, var_no[name] + 1)
            mark(act, act.activation(stat[:, 0:cols], stat[:, 0:cols], ACT.Sqrt, bias=eps[:, 0:1], scale=scale), std_ready)

        def act_ada_rows(act, n):
            job = jobs[f"ada{n}"]
            wait_bank_full(act, job)
            if n >= 2 and n != 4 and n != 5:
                wait_bank_full(act, jobs[f"adab{n - 2}"] + (1 if n - 2 < 4 else 0))
            read_out(act, act.activation(m_rows[n >= 4][:, n % 2, :], ps(job)[:, :], ACT.Copy), job)

        def act_ada_spread(act, n):
            s, c = n // 2, slice((n % 2) * WIDE, (n % 2 + 1) * WIDE)
            for w in range(2 if n < 4 else 1):
                job = jobs[f"adab{n}"] + w
                wait_bank_full(act, job)
                dst = mod1[:, 2 * s + w, c] if n < 4 else mods[:, s - 2, c]
                if s in (1, 4):
                    ins = act.activation(dst, ps(job)[:, :], ACT.Identity, bias=ones[:, 0:1])
                else:
                    ins = act.activation(dst, ps(job)[:, :], ACT.Copy)
                read_out(act, ins, job)

        def act_ada(act):
            act.wait_ge(load_c, 32)
            mark(act, act.activation(crow[0:16, 0, :], crow[0:16, 0, :], ACT.Silu), c_silu)
            wait_bank_full(act, jobs["cT"])
            act.wait_ge(consts, 7)
            read_out(act, act.activation(cT[:, :, 0:2], ps(jobs["cT"])[:, 0:16].rearrange("p (w k) -> p k w", w=2), ACT.Copy), jobs["cT"])
            norm_sqrt(act, "ln_in", 1.0)
            for n in range(5):
                if n < 4:
                    act_ada_rows(act, n)
                if n:
                    act_ada_spread(act, n - 1)
            act_transposed(act, "in", hT, 4)

        def act_gates(act):
            act.wait_ge(lb_sum, 1)
            mark(act, act.activation(lb_t, lb_t, ACT.Exp), lb_exp)
            act.wait_ge(lb_sum, 2)
            step(act, "act", act.activation(log_lb, log_lb, ACT.Ln, scale=2.0 ** 50))
            mark(act, act.activation(log1m_lb, one_lb, ACT.Ln), lb_log)

            def first(j):
                job = jobs["hff"] + j
                wait_bank_full(act, job)
                if j >= 2:
                    act.wait_ge(gate_done, j - 1)
                T = gate_tmp[:, j % 2, 0, :]
                step(act, "act", act.activation(T, ps(job)[:, :], ACT.Abs))
                step(act, "act", act.activation(T, T, ACT.Exp, scale=-1.0))
                mark(act, act.activation(T, T, ACT.Ln, bias=ones[:, 0:1]), gate_abs)

            def second(j):
                u = j % 4 + UNITS * (j // 4)
                wait_read_out(act, jobs["hff"] + j)
                mark(act, act.activation(key[:, :, u, :], key[:, :, u, :], ACT.Exp), gate_k)
                act.wait_ge(gate_diff, j + 1)
                T = gate_tmp[:, j % 2, 0, :]
                step(act, "act", act.activation(T, T, ACT.Abs))
                step(act, "act", act.activation(T, T, ACT.Exp, scale=-1.0))
                mark(act, act.activation(T, T, ACT.Ln, bias=ones[:, 0:1]), gate_log)

            for j in range(9):
                if j < 8:
                    first(j)
                if j:
                    second(j - 1)
            job = jobs["rank"]
            wait_bank_full(act, job)
            step(act, "act", act.activation(rank_act[0:2 * RANK, 0:L], ps(job)[0:2 * RANK, 0:L], ACT.Copy))
            read_out(act, act.activation(by_cols(rank_act[0:2 * RANK, L:2 * L]), by_rows(ps(job)[0:2 * RANK, L:2 * L]),
                                         ACT.Copy), job)

        def act_project(act):
            for b in range(4):
                job = jobs["gqk"] + b
                wait_bank_full(act, job)
                if b < 2:
                    ins = act.activation(by_cols(qry[:, HG_HEADS + b, :]), by_rows(ps(job)[:, 0:L]), ACT.Copy, scale=0.125)
                else:
                    step(act, "act", act.activation(key[:, 0, HG_HEADS + b - 2, :], ps(job)[:, 0:L], ACT.Copy))
                    ins = act.activation(by_cols(key[:, 1, HG_HEADS + b - 2, :]), by_rows(ps(job)[:, L:2 * L]), ACT.Copy)
                read_out(act, ins, job)
            for b in range(4):
                job = jobs["hq"] + b
                wait_bank_full(act, job)
                read_out(act, act.activation(qry[:, b, :], ps(job)[:, 0:L], ACT.Copy), job)
            for j in range(4):
                job = jobs["gla_gate"] + j
                wait_bank_full(act, job)
                act.wait_ge(gate_done, 8 + j - 1)
                T = gate_tmp[:, j % 2, 0, :]
                step(act, "act", act.activation(T, ps(job)[:, :], ACT.Abs, bias=bgk[:, j:j + 1]))
                step(act, "act", act.activation(T, T, ACT.Exp, scale=-1.0))
                mark(act, act.activation(T, T, ACT.Ln, bias=ones[:, 0:1]), gate_abs)
            for name, c0 in (("hi", 0), ("gv", WIDE)):
                for i in range(4):
                    job = jobs[name] + i
                    wait_bank_full(act, job)
                    read_out(act, act.activation(val[:, i, c0:c0 + WIDE], ps(job)[:, :], ACT.Copy), job)
                if name == "hi":
                    act.wait_ge(scans_done, 1)
                    for u in range(2 * UNITS):
                        ins = act.activation(decay[:, 0, u, :], decay[:, 0, u, :], ACT.Exp, bias=b_end[:, u:u + 1], scale=-1.0)
                        if u < 2 * UNITS - 1:
                            step(act, "act", ins)
                    mark(act, ins, ctx_exp)
            act.wait_ge(masks_ready, 1)
            for name, c0 in (("hg", 0), ("gg", WIDE)):
                for t in range(TT):
                    job = jobs[name] + t
                    wait_bank_full(act, job)
                    read_out(act, act.activation(gate_out[:, t, c0:c0 + WIDE], ps(job)[:, :], ACT.Silu), job)

        def act_states(act):
            mark(act, act.activation(q_state, decay[:, 1, :, :], ACT.Exp), q_exp)
            for j in range(6):
                job = jobs["keyT"] + j
                wait_bank_full(act, job)
                g = j % 3
                read_out(act, act.activation(keyT[:, j // 3, 4 * g:4 * g + 4, :],
                                             ps(job)[:, :].rearrange("p (u c) -> p u c", u=4), ACT.Copy), job)
            decays(act, 0)
            for j in range(4):
                job = jobs["state"] + j
                d = j % 2
                wait_bank_full(act, job)
                if j < 2:
                    ins = act.activation(state[:, d * UNITS:d * UNITS + 4, :],
                                         ps(job)[:, :].rearrange("p (u c) -> p u c", u=4), ACT.Copy)
                else:
                    s, o = ps(job)[:, :].rearrange("p (k c) -> p k c", k=2), slice(d * UNITS + 4, d * UNITS + 6)
                    step(act, "act", act.activation(state[0:64, o, :], s[0:64, :, 0:P], ACT.Copy))
                    ins = act.activation(state[64:128, o, :], s[64:128, :, P:2 * P], ACT.Copy)
                read_out(act, ins, job)
            for t in range(TT):
                for g in range(3):
                    job = jobs["inter"] + 3 * t + g
                    wait_bank_full(act, job)
                    if g == 0:
                        o, n = o_mix[:, t, 0:WIDE].rearrange("p (h c) -> p h c", h=4), 4
                    else:
                        o, n = o_mix[:, t, WIDE:D].rearrange("p (h e c) -> p h e c", h=2, e=2)[:, :, g - 1, :], 2
                    read_out(act, act.activation(o, ps(job)[:, 0:n * P].rearrange("p (h c) -> p h c", h=n), ACT.Copy), job)

        def decays(act, i):
            act.wait_ge(lvl_diff, i + 1)
            mark(act, act.activation(lvlE, lvlE, ACT.Exp), lvl_exp)

        def act_scores(act):
            act_ada_rows(act, 4)
            for name, dst in (("scx", sc_x), ("diag", sc_in)):
                for j in range(4):
                    job = jobs[name] + j
                    wait_bank_full(act, job)
                    read_out(act, act.activation(dst[:, 2 * j:2 * j + 2, :, :],
                                                 ps(job)[:, :].rearrange("p (h b c) -> p h b c", h=2, b=2), ACT.Copy), job)
                if name == "scx":
                    decays(act, 1)
            act_ada_rows(act, 5)
            act_ada_spread(act, 4)
            for lv in range(len(LEVELS)):
                if lv + 2 <= len(LEVELS):
                    decays(act, lv + 2)
                if lv + 6 < 12:
                    act_ada_rows(act, lv + 6)
                act_ada_spread(act, lv + 5)

        def load_row_pair(act, dst, a, b, s):
            act.dma_start(dst[:, 0, :], a.to_broadcast([P, D])).then_inc(s, 16)
            act.dma_start(dst[:, 1, :], b.to_broadcast([P, D])).then_inc(s, 16)

        def act_experts(act):
            norm_sqrt(act, "head", 1.0 / P)
            for t in range(TT):
                for g in range(2):
                    job = jobs["T_mix"] + 2 * t + g
                    wait_bank_full(act, job)
                    i = ps(job)[:, :].rearrange("p (k t) -> p k t", k=4)
                    if g == 0:
                        ins = act.activation(mixT[:, 0:4, t * P:(t + 1) * P], i, ACT.Copy)
                    else:
                        w = P // ROWS
                        for k in range(4):
                            o = mixT[:, 4 + k, :].rearrange("p (r w) -> p w r", r=ROWS)[:, t * w:(t + 1) * w, :]
                            ins = act.activation(o, i[:, k, :].rearrange("p (w r) -> p w r", r=ROWS), ACT.Copy)
                            if k < 3:
                                step(act, "act", ins)
                    read_out(act, ins, job)
            gamma, beta = A["ln_gamma"][0], A["ln_beta"][0]
            load_row_pair(act, row_a, gamma[0:1, :], beta[0:1, :], load_rows)
            act.dma_start(keys_raw, A["peer_sub_keys"][0].rearrange("s n d -> n s d")).then_inc(load_keys, 16)
            norm_sqrt(act, "post1", 1.0)
            norm_sqrt(act, "mod2", 1.0)
            act_transposed(act, "h2", h2T, 2)
            job = jobs["keys"]
            wait_bank_full(act, job)
            read_out(act, act.activation(keysT, ps(job)[:, 0:2 * P].rearrange("p (a b) -> p a b", a=2), ACT.Copy), job)
            for n in range(4):
                for j in range(2):
                    job = jobs[f"wq{n}"] + j
                    wait_bank_full(act, job)
                    read_out(act, act.activation(qT[:, 4 * n + 2 * j:4 * n + 2 * j + 2, :],
                                                 ps(job)[:, :].rearrange("p (a b) -> p a b", a=2), ACT.Copy), job)
                for t in range(TT):
                    job = jobs[f"skey{n}"] + t
                    wait_bank_full(act, job)
                    read_out(act, act.activation(s_key[t][:, 4 * n:4 * n + 4, :],
                                                 ps(job)[:, :].rearrange("p (a b) -> p a b", a=4), ACT.Copy), job)
            act_soft(act, 0)
            act_gelu(act, 0)
            act_soft(act, 1)
            load_row_pair(act, row_a, gamma[1:2, :], beta[1:2, :], load_rows)

        def act_soft(act, t):
            act.wait_ge(best_ready, t + 1)
            mark(act, act.activation(gate_w[:, t, :], gate_w[:, t, :], ACT.Exp), soft_ready)

        def act_gelu(act, t):
            act.wait_ge(row_used, GATHERS * (2 * t + 1))
            mark(act, act.activation(act_w[:, t, :], act_w[:, t, :], ACT.Gelu_apprx_tanh), gelu_done)

        def act_rms(act, i):
            if i % 2 == 0:
                junk = h_tok_s if i == 0 else h_tok
                for t in range(TT):
                    act.wait_ge(x_ready, TT * (i // 2) + t + 1)
                    step(act, "act", act.activation(junk[:, t, :], x_lat[:, t, :], ACT.Square, accum_out=stat[:, t:t + 1]))
            norm_sqrt(act, f"rms{i}", 1.0 / D)

        def load_norm_pair(act, k):
            if k:
                act.wait_ge(rows_free, k)
            g = A["norm_g_2"]
            load_row_pair(act, row_b, g[k // 2, 2 * (k % 2):2 * (k % 2) + 1, :],
                          g[k // 2, 2 * (k % 2) + 1:2 * (k % 2) + 2, :], load_norm)

        def act_tail(act, name):
            for n in range(2):
                act_tail_block(act, name, n)

        def act_tail_block(act, name, n):
            for t in range(TT):
                job = jobs[name] + 2 * n + t
                wait_bank_full(act, job)
                read_out(act, act.activation(mix2[:, t, n * WIDE:(n + 1) * WIDE], ps(job)[:, :], ACT.Copy), job)

        def blocks(r, g, q, part):
            rows, c = slice(64 * g, 64 * g + 64), slice(32 * q + 16 * g, 32 * q + 16 * g + 16)
            wide = (Bz[:, r] if part == "b" else Cz[r])[rows].rearrange("p (a q) c -> p a q c", q=4)[:, :, q, c]
            if part == "b":
                return wide, bbar[rows, r, :, :].rearrange("p (a q) c -> p a q c", q=4)[:, :, q, :]
            return wide, CT[rows, r, :, c]

        def act_s5_setup(act):
            act.dma_start(s5_raw[0:16, 0, :], A["ssm_lam_re_2"][0].rearrange("(j g) p -> j (g p)", g=2)).then_inc(load_s5, 16)
            act.dma_start(s5_raw[0:16, 1, :], A["ssm_lam_im_2"][0].rearrange("(j g) p -> j (g p)", g=2)).then_inc(load_s5, 16)
            act.dma_start(dt_raw[0:16, :], A["ssm_log_dt_2"][0].rearrange("(j g) -> j g", g=2)).then_inc(load_s5, 16)
            act.dma_start(d_raw[0:4, :], A["ssm_d_2"][0].rearrange("(a g) c -> a (g c)", a=4)).then_inc(load_s5, 16)
            for r, n in enumerate(("ssm_b_re_2", "ssm_b_im_2")):
                act.dma_start(braw[:, r, :, :], A[n][0].rearrange("(j g) p c -> (g p) j c", g=2)).then_inc(load_s5, 16)
            for r, n in enumerate(("ssm_c_re_2", "ssm_c_im_2")):
                for half in range(2):
                    act.dma_start(craw[:, r, :, 64 * half:64 * half + 64],
                                  A[n][0].rearrange("(a g) c p -> (g c) a p", a=4)).then_inc(load_s5, 16)
            wait_read_out(act, jobs["s5p"])
            mark(act, act.activation(S5["dt"], S5["dt"], ACT.Exp), s5_exp)
            act.wait_ge(s5_theta, 1)
            step(act, "act", act.activation(S5["mag"], S5["mag"], ACT.Exp))
            step(act, "act", act.activation(S5["sn"], S5["r"], ACT.Sin))
            mark(act, act.activation(S5["hs"], S5["r"], ACT.Sin, scale=0.5), s5_sin)
            zero = ones[:, 0:P].unsqueeze(1).to_broadcast([P, NSTATE, P])
            for m in (Bz[:, 0], Bz[:, 1], Cz[0], Cz[1]):
                step(act, "act", act.activation(m, zero, ACT.Copy, scale=0.0))
            act_gelu(act, 1)
            act.wait_ge(s5_bbar, 1)
            for r in range(2):
                for g in range(2):
                    for q in range(4):
                        ins = act.activation(*blocks(r, g, q, "b"), ACT.Copy)
                        if (r, g, q) != (1, 1, 3):
                            step(act, "act", ins)
            mark(act, ins, s5_b)
            for r in range(2):
                job = jobs["CT"] + r
                wait_bank_full(act, job)
                read_out(act, act.activation(CT[:, r, :, :], ps(job)[:, :].rearrange("p (a b) -> p a b", a=4), ACT.Copy), job)
            for r in range(2):
                for g in range(2):
                    for q in range(4):
                        ins = act.activation(*blocks(r, g, q, "c"), ACT.Copy, scale=1.0 - 2.0 * r)
                        if (r, g, q) != (1, 1, 3):
                            step(act, "act", ins)
            mark(act, ins, s5_c)
            for r in range(2):
                for g in range(4):
                    job = jobs["BT"] + 4 * r + g
                    wait_bank_full(act, job)
                    read_out(act, act.activation(BT[:, r, 4 * g:4 * g + 4, :],
                                                 ps(job)[:, :].rearrange("p (a b) -> p a b", a=4), ACT.Copy), job)
            act.wait_ge(s5_table, 1)
            load_norm_pair(act, 0)

        def act_s5(act):
            norm_sqrt(act, "post2", 1.0)
            act_rms(act, 0)
            act_transposed(act, "ssm", hT_s, 2)
            for j in range(2):
                job = jobs["ssm_in"] + j
                wait_bank_full(act, job)
                read_out(act, act.activation(uT[:, 2 * j:2 * j + 2, :],
                                             ps(job)[:, :].rearrange("p (a b) -> p a b", a=2), ACT.Copy), job)
            for a in range(4):
                wait_read_out(act, jobs[f"y{a}"])
                mark(act, act.activation(zT[:, a, :], zT[:, a, :], ACT.Gelu_apprx_tanh), z_ready)
            sg = rt.rearrange("p a b t -> p (a b) t")
            for j in range(2):
                job = jobs["glu"] + j
                wait_bank_full(act, job)
                read_out(act, act.activation(sg[:, 2 * j:2 * j + 2, :],
                                             ps(job)[:, :].rearrange("p (a b) -> p a b", a=2), ACT.Sigmoid), job)
            act_split(act, 0)
            act_tail(act, "ssm_out")
            act_rms(act, 1)
            load_norm_pair(act, 1)

        def split_waits(act, q):
            old = q - SPLIT_SLOTS
            if old >= 0:
                if split_back[old] is None:
                    act.wait_ge(w_used, split_back[:old + 1].count(None))
                else:
                    wait_bank_full(act, split_back[old])

        tile_at = {q: n for n, q in split_no.items()}
        AHEAD_OF = {"mlp0": 1, "att": 2, "atto": 0, "mlp1": 2}

        def act_split(act, q):
            split_waits(act, q)
            wait_weights(act, tile_at[q])
            cols = stream[tile_at[q]].shape[2]
            mark(act, act.activation(w_split[q % SPLIT_SLOTS][:, 0, :, 0:cols], wtile(tile_at[q], cols), ACT.Copy), w_high)

        def act_split_first(act, name, q0):
            if AHEAD_OF[name] == 0:
                act_split(act, q0)
            for j in range(4):
                job = jobs[f"T_{name}"] + j
                wait_bank_full(act, job)
                t, g = j // 2, j % 2
                mark(act, act.activation(x_split[0][:, 4 * g:4 * g + 4, t * P:(t + 1) * P],
                                         ps(job)[:, :].rearrange("p (k t) -> p k t", k=4), ACT.Copy), x_high)
            for q in range(max(1, AHEAD_OF[name]), 3):
                act_split(act, q0 + q)

        def act_split_tokens(act, name, q0, blocks, store):
            act_split_first(act, name, q0)
            for n in range(blocks):
                if n < blocks - 1:
                    act_split(act, q0 + 2 * n + 3)
                store(n)
                if n < blocks - 2:
                    act_split(act, q0 + 2 * n + 4)
                elif name == "atto" and n == 0:
                    for q in range(AHEAD_OF["mlp1"]):
                        act_split(act, q0 + 4 + q)

        def act_mlp(act, i):
            q0 = split_no[tile_no[f"mlp{i}a0"]]
            act_rms(act, 4 * i + 2)
            act_split_first(act, f"mlp{i}", q0)
            for n in range(8):
                act_split(act, q0 + 2 * n + 3)
                for j in range(2 * n, 2 * n + 2):
                    if j >= 3:
                        act.wait_ge(ff_ready, 16 * i + j - 2)
                    for b in range(2):
                        job = jobs[f"mlp{i}a"] + 2 * j + b
                        wait_bank_full(act, job)
                        read_out(act, act.activation(ff_tmp[:, j % 3, b, :], ps(job)[:, 0:L], ACT.Relu), job)
                act_split(act, q0 + 2 * n + 4)
            for q in range(q0 + 19, q0 + 32 + (AHEAD_OF["att"] if i == 0 else 0)):
                act_split(act, q)
            act_tail(act, f"mlp{i}b")
            act_rms(act, 4 * i + 3)

        def act_attention(act):
            load_norm_pair(act, 2)
            act_rms(act, 4)
            act.dma_start(rope, A["rope_table"].rearrange("(t p) c d -> p t c d", p=P)).then_inc(load_rope, 16)

            def store(n):
                cols = min(WIDE, ATT_COLS - n * WIDE)
                for t in range(TT):
                    job = jobs["att"] + 2 * n + t
                    wait_bank_full(act, job)
                    read_out(act, act.activation(proj[:, t, n * WIDE:n * WIDE + cols], ps(job)[:, 0:cols], ACT.Copy), job)
            act_split_tokens(act, "att", split_no[tile_no["att0"]], 5, store)
            for t in range(TT):
                dst = [qTa[:, 0:4], qTa[:, 4:8], qiT[:, 0:4], kTa[:, 0:4], kTa[:, 4:5]]
                for g in range(5):
                    job = jobs["rT"] + 5 * t + g
                    n = 4 if g < 4 else 1
                    wait_bank_full(act, job)
                    read_out(act, act.activation(dst[g][:, :, t * P:(t + 1) * P],
                                                 ps(job)[:, 0:n * P].rearrange("p (a b) -> p a b", a=n), ACT.Copy), job)
            for j in range(8):
                job = jobs["idx"] + j
                wait_bank_full(act, job)
                if j >= 2:
                    act.wait_ge(rel_used, j - 1)
                keys = seen(j // 4)
                read_out(act, act.activation(rel[:, j % 2, :, keys], ps(job)[:, :].rearrange("p (a b) -> p a b", a=2)[:, :, keys],
                                             ACT.Relu), job)
            for t in range(TT):
                act.wait_ge(logits_ready, t + 1)
                for h in range(N_HEADS):
                    ins = act.activation(prob[:, t, h, seen(t)], prob[:, t, h, seen(t)], ACT.Exp, bias=mx16[:, t, h:h + 1],
                                         accum_out=sum16[:, t, h:h + 1])
                    if h < N_HEADS - 1:
                        step(act, "act", ins)
                mark(act, ins, prob_ready)
            for t in range(TT):
                for s in range(t + 1):
                    for g in range(4):
                        job = jobs[f"pT{t}"] + 4 * s + g
                        wait_bank_full(act, job)
                        read_out(act, act.activation(pT[:, s, 4 * g:4 * g + 4, :],
                                                     ps(job)[:, :].rearrange("p (a b) -> p a b", a=4), ACT.Copy), job)
            act_split_tokens(act, "atto", split_no[tile_no["att_out0"]], 2, lambda n: act_tail_block(act, "att_out", n))
            act_rms(act, 5)
            load_norm_pair(act, 3)

        @block.scalar
        def _(act):
            act.dma_start(crow[0:8, 0, :], A["c"][0].rearrange("(k p) -> k p", p=P)).then_inc(load_c, 16)
            act.dma_start(crow[8:16, 0, :], A["c_ctx"].rearrange("(k p) -> k p", p=P)).then_inc(load_c, 16)
            act.dma_start(x_ctx, A["ctx"][0].rearrange("(t p) d -> p t d", p=P)).then_inc(load_x, 16)
            act.dma_start(x_lat, A["x"][0].rearrange("(t p) d -> p t d", p=P)).then_inc(load_x, 16)
            act.dma_start(w_rank, w_in[:, 4096:4128].rearrange("(k p) n -> p k n", p=P)).then_inc(load_gate, 16)
            act.wait_ge(gk2_zero, 1)
            for d in range(2):
                act.dma_start(gk2[RANK * d:RANK * (d + 1), d, :], A["w_gk2"][0, d]).then_inc(load_gate, 16)
            act.dma_start(bgk_raw[0:4, :], A["b_gk"][0].rearrange("d (j p) -> (d j) p", p=P)).then_inc(load_gate, 16)
            act.dma_start(lb_raw[0:8, :], A["hg_lower_bounds"][:, 0, :].rearrange("d (j p) -> (d j) p", p=P)).then_inc(load_gate, 16)
            act.dma_start(gain[:, 0, :], A["hg_norm"].to_broadcast([P, P])).then_inc(load_gain, 16)
            act.dma_start(gain[:, 1, :], A["gla_norm"].to_broadcast([P, P])).then_inc(load_gain, 16)
            act_ada(act)
            act_gates(act)
            act_project(act)
            act_states(act)
            act_scores(act)
            act_experts(act)
            act_s5_setup(act)
            act_s5(act)
            act_mlp(act, 0)
            act_attention(act)
            act_mlp(act, 1)

        @block.vector
        def _(dve):
            def do(ins):
                step(dve, "dve", ins)

            def go(ins):
                counts["dve"] += 1
                ins.then_inc(dve_step, 1)

            def wait_done():
                dve.wait_ge(dve_step, counts["dve"])

            def tt(o, a, b, op):
                return dve.tensor_tensor(o, a, b, op)

            def invert_std(name):
                cols = dict(NORM_USES)[name]
                dve.wait_ge(std_ready, norm_no[name] + 1)
                do(dve.reciprocal(stat[:, 0:cols], stat[:, 0:cols]))

            def layer_stats(tiles):
                for i, x in enumerate(tiles):
                    do(dve.bn_stats(stat[:, 24:30], x[:, 0:512]))
                    do(dve.bn_stats(stat[:, 30:36], x[:, 512:1024]))
                    do(dve.bn_aggr(stat[:, 40 + 2 * i:42 + 2 * i], stat[:, 24:36].rearrange("p (a b) -> p a b", a=2)))
                    ins = dve.tensor_copy(stat[:, i:i + 1], stat[:, 41 + 2 * i:42 + 2 * i])
                    if i < len(tiles) - 1:
                        do(ins)
                mark(dve, ins, var_ready)

            def normalized(o, x, i):
                return dve.tensor_scalar(o, x, stat[:, 40 + 2 * i:41 + 2 * i], stat[:, i:i + 1], ALU.subtract, ALU.mult)

            def square_sums(tiles, junk):
                for t, x in enumerate(tiles):
                    ins = dve.scalar_tensor_tensor(out=junk[:, t, :], in0=x, scalar=1.0, in1=x, op0=ALU.mult,
                                                   op1=ALU.mult, accum_out=stat[:, t:t + 1])
                    if t == 0:
                        do(ins)
                mark(dve, ins, var_ready)

            dve.wait_ge(consts, 7)
            do(tt(it_x, it_t, it_s, ALU.bitwise_xor))
            do(dve.tensor_copy(it_f, it_x))
            for d, op in enumerate((ALU.is_ge, ALU.is_le)):
                do(tt(it_g, it_s, it_t, op))
                do(dve.scalar_tensor_tensor(out=it_g, in0=it_g, scalar=1000.0, in1=it_f, op0=ALU.mult, op1=ALU.add))
                for i, h in enumerate(LEVELS):
                    ins = dve.tensor_scalar(level_mask[:, d, i, :], it_g, float(2 * h), None, ALU.is_lt)
                    if (d, i) != (1, len(LEVELS) - 1):
                        do(ins)
            mark(dve, ins, masks_ready)

            dve.wait_ge(load_x, 32)
            toks = [x_ctx[:, 0, :], x_ctx[:, 1, :], x_lat[:, 0, :], x_lat[:, 1, :]]
            layer_stats(toks)
            invert_std("ln_in")

            def modulated(i):
                w = 1 if i < 2 else 0
                do(normalized(h_in[:, i, :], toks[i], i))
                do(tt(h_in[:, i, :], h_in[:, i, :], mod1[:, 2 + w, :], ALU.mult))
                mark(dve, tt(h_in[:, i, :], h_in[:, i, :], mod1[:, w, :], ALU.add), tok_ready)

            for n in range(4):
                for w in range(2):
                    wait_read_out(dve, jobs[f"adab{n}"] + w)
            for i in range(4):
                modulated(i)

            job = jobs["lb"]
            wait_bank_full(dve, job)
            do(dve.tensor_copy(lb, ps(job)[:, 0:8]))
            read_out(dve, dve.tensor_copy(bgk, ps(job)[:, 8:12]), job)
            mark(dve, tt(lb_t, lb, lb, ALU.subtract), lb_sum)
            dve.wait_ge(lb_exp, 1)
            do(dve.reciprocal(lb, lb_t))
            do(tt(lb_t, lb, lb_t, ALU.mult))
            do(tt(lb, lb_t, lb_t, ALU.subtract))
            do(dve.tensor_scalar(lb, lb, 0.0, 1.0 - 1e-6, ALU.max, ALU.min))
            do(dve.tensor_scalar(one_lb, lb, -1.0, 1.0, ALU.mult, ALU.add))
            mark(dve, dve.tensor_scalar(log_lb, lb, 1e-30, None, ALU.max), lb_sum)
            dve.wait_ge(lb_log, 1)
            do(dve.tensor_scalar(log_lb, log_lb, -50.0 * 0.6931471805599453, None, ALU.add))

            def first(j):
                u = j % 4 + UNITS * (j // 4)
                job = jobs["hff"] + j
                T, S = gate_tmp[:, j % 2, 0, :], gate_tmp[:, j % 2, 1, :]
                wait_bank_full(dve, job)
                dve.wait_ge(gate_abs, j + 1)
                do(dve.scalar_tensor_tensor(out=S, in0=ps(job)[:, :], scalar=0.0, in1=T, op0=ALU.min, op1=ALU.subtract))
                read_out(dve, tt(key[:, :, u, :], S.rearrange("p (s t) -> p s t", s=2),
                                 ps(job)[:, :].rearrange("p (s t) -> p s t", s=2), ALU.subtract), job)
                do(dve.tensor_scalar(S, S, log1m_lb[:, j:j + 1], None, ALU.add))
                mark(dve, dve.tensor_scalar(T, S, log_lb[:, j:j + 1], None, ALU.subtract), gate_diff)

            def second(j):
                u = j % 4 + UNITS * (j // 4)
                T, S = gate_tmp[:, j % 2, 0, :], gate_tmp[:, j % 2, 1, :]
                dve.wait_ge(gate_k, j + 1)
                do(dve.tensor_scalar(key[:, :, u, :], key[:, :, u, :], one_lb[:, j:j + 1], None, ALU.mult))
                dve.wait_ge(gate_log, j + 1)
                mark(dve, dve.scalar_tensor_tensor(out=decay[:, :, u, :], in0=S.rearrange("p (s t) -> p s t", s=2),
                                                   scalar=log_lb[:, j:j + 1], in1=T.rearrange("p (s t) -> p s t", s=2),
                                                   op0=ALU.max, op1=ALU.add), gate_done)

            for j in range(9):
                if j < 8:
                    first(j)
                if j:
                    second(j - 1)
            for j in range(4):
                u = UNITS * (j // 2) + HG_HEADS + j % 2
                job = jobs["gla_gate"] + j
                T, S = gate_tmp[:, j % 2, 0, :], gate_tmp[:, j % 2, 1, :]
                wait_bank_full(dve, job)
                dve.wait_ge(gate_abs, 8 + j + 1)
                read_out(dve, dve.tensor_scalar(S, ps(job)[:, :], bgk[:, j:j + 1], 0.0, ALU.add, ALU.min), job)
                do(tt(S, S, T, ALU.subtract))
                mark(dve, dve.tensor_scalar(decay[:, :, u, :], S.rearrange("p (s t) -> p s t", s=2), 1.0 / 16.0, None,
                                            ALU.mult), gate_done)
            for u in range(2 * UNITS):
                for s in range(2):
                    a = decay[:, s, u, :] if u < UNITS else decay[:, s, u, ::-1]
                    do(dve.tensor_tensor_scan(a, ones[:, :], a, 0.0, ALU.mult, ALU.add))
            do(dve.tensor_copy(b_end[:, 0:UNITS], decay[:, 0, 0:UNITS, L - 1]))
            mark(dve, dve.tensor_copy(b_end[:, UNITS:2 * UNITS], decay[:, 0, UNITS:2 * UNITS, 0]), scans_done)
            for b in (2, 3):
                wait_read_out(dve, jobs["gqk"] + b)
            do(dve.tensor_copy(key[:, :, UNITS + HG_HEADS:2 * UNITS, :], key[:, :, HG_HEADS:UNITS, :]))
            dve.wait_ge(ctx_exp, 1)
            mark(dve, tt(decay[:, 0, :, :], decay[:, 0, :, :], key[:, 0, :, :], ALU.mult), ctx_key)

            bL = decay[:, 1, :, :].rearrange("p u t -> p (u t)")
            kL = key[:, 1, :, :].rearrange("p u t -> p (u t)")
            qL = qry.rearrange("p u t -> p (u t)")
            EL = lvlE.rearrange("p d u t -> p (d u t)")
            WL = lvlW.rearrange("p d u t -> p (d u t)")
            span = UNITS * L

            def halves(flat, d, h):
                return flat[:, d * span:(d + 1) * span].rearrange("p (n c h) -> p n c h", c=2, h=h)

            def exponents(i, h):
                for d in range(2):
                    b, e = halves(bL, d, h), halves(EL, d, h)
                    n = span // (2 * h)
                    seam = (b[:, :, 0, h - 1:h] if d == 0 else b[:, :, 1, 0:1]).to_broadcast([P, n, h])
                    near, far = (0, 1) if d == 0 else (1, 0)
                    do(tt(e[:, :, near, :], seam, b[:, :, near, :], ALU.subtract))
                    ins = tt(e[:, :, far, :], b[:, :, far, :], seam, ALU.subtract)
                    if d == 0:
                        do(ins)
                mark(dve, ins, lvl_diff)

            def decayed(i, h):
                dve.wait_ge(lvl_exp, i + 1)
                for d in range(2):
                    w, e, k, q = halves(WL, d, h), halves(EL, d, h), halves(kL, d, h), halves(qL, 0, h)
                    near, far = (0, 1) if d == 0 else (1, 0)
                    do(tt(w[:, :, near, :], e[:, :, near, :], k[:, :, near, :], ALU.mult))
                    ins = tt(w[:, :, far, :], e[:, :, far, :], q[:, :, far, :], ALU.mult)
                    if d == 0:
                        do(ins)
                mark(dve, ins, lvl_ready)

            levels = [P] + LEVELS
            exponents_after = lambda i: exponents(i + 1, levels[i + 1]) if i + 1 < len(levels) else None
            dve.wait_ge(q_exp, 1)
            for b in range(2):
                wait_read_out(dve, jobs["gqk"] + b)
            for b in range(4):
                wait_read_out(dve, jobs["hq"] + b)
            do(tt(q_state[:, 0:UNITS, :], q_state[:, 0:UNITS, :], qry[:, :, :], ALU.mult))
            mark(dve, tt(q_state[:, UNITS:, :], q_state[:, UNITS:, :], qry[:, :, :], ALU.mult), q_state_ready)
            wait_bank_full(dve, jobs["gg"] + 1)
            exponents(0, P)
            wait_bank_full(dve, jobs["state"] + 3)
            decayed(0, P)
            exponents_after(0)
            for i, h in enumerate(LEVELS):
                if i == 0:
                    wait_bank_full(dve, jobs["scx"] + 3)
                decayed(i + 1, h)
                exponents_after(i + 1)
                if i == 0:
                    for j in range(4):
                        wait_read_out(dve, jobs["diag"] + j)
                for j in range(4):
                    job = jobs[f"lvl{i}"] + j
                    wait_bank_full(dve, job)
                    for d in ((j,) if j < 2 else (0, 1)):
                        places, c0, n = (slice(0, 4), 0, 8) if j < 2 else (slice(2 * j, 2 * j + 2), 4 * 64 * d, 4)
                        dst = far_half(sc_in[:, places, :, :].rearrange("p h t c -> p (h t) c"), d, h)
                        m = far_half(level_mask[:, d, i, :], d, h).unsqueeze(1).to_broadcast([P, n, 64 // h, h])
                        ins = dve.copy_predicated(dst, m, ps(job)[:, c0:c0 + 64 * n].rearrange("p (b n h) -> p b n h", b=n, h=h))
                        if j >= 2 and d == 0:
                            do(ins)
                    read_out(dve, ins, job)

            for t in range(TT):
                for g in range(2):
                    job = jobs["o"] + 2 * t + g
                    wait_bank_full(dve, job)
                    o = o_mix[:, t, g * WIDE:(g + 1) * WIDE]
                    if t == 0 and g == 0:
                        for j in range(6):
                            wait_read_out(dve, jobs["inter"] + j)
                    read_out(dve, tt(o, ps(job)[:, :], o, ALU.add), job)
            for t in range(TT):
                do(tt(sq_tmp[:, t, :], o_mix[:, t, :], o_mix[:, t, :], ALU.mult))
                ins = dve.tensor_reduce(stat[:, HEADS * t:HEADS * (t + 1)],
                                        sq_tmp[:, t, :].rearrange("p (h c) -> p h c", h=HEADS), AX_X, ALU.add)
                if t == 0:
                    do(ins)
            mark(dve, ins, var_ready)
            invert_std("head")
            dve.wait_ge(load_gain, 32)
            for name in ("hg", "gg"):
                for j in range(2):
                    wait_read_out(dve, jobs[name] + j)
            for t in range(TT):
                o = o_mix[:, t, :].rearrange("p (h c) -> p h c", h=HEADS)
                do(tt(o, o, stat[:, HEADS * t:HEADS * (t + 1)].unsqueeze(2).to_broadcast([P, HEADS, P]), ALU.mult))
                for g in range(2):
                    do(tt(o[:, 4 * g:4 * g + 4, :], o[:, 4 * g:4 * g + 4, :], gain[:, g:g + 1, :].to_broadcast([P, 4, P]), ALU.mult))
                mark(dve, tt(o_mix[:, t, :], o_mix[:, t, :], gate_out[:, t, :], ALU.mult), tok_ready)

            for n in range(4, 6):
                wait_read_out(dve, jobs[f"adab{n}"])
            for n in range(2):
                c = slice(n * WIDE, (n + 1) * WIDE)
                for t in range(TT):
                    job = jobs["out"] + 2 * n + t
                    wait_bank_full(dve, job)
                    read_out(dve, tt(sq_tmp[:, t, c], ps(job)[:, :], mods[:, 0, c], ALU.mult), job)
                    do(dve.scalar_tensor_tensor(out=x_lat[:, t, c], in0=x_lat[:, t, c], scalar=ALPHA,
                                                in1=sq_tmp[:, t, c], op0=ALU.mult, op1=ALU.add))

            def scaled_norm(name, load_count):
                layer_stats([x_lat[:, t, :] for t in range(TT)])
                invert_std(name)
                dve.wait_ge(load_rows, load_count)
                for t in range(TT):
                    go(normalized(x_lat[:, t, :], x_lat[:, t, :], t))
                wait_done()
                for t in range(TT):
                    go(tt(x_lat[:, t, :], x_lat[:, t, :], row_a[:, 0, :], ALU.mult))
                wait_done()
                for t in range(TT):
                    ins = tt(x_lat[:, t, :], x_lat[:, t, :], row_a[:, 1, :], ALU.add)
                    if name == "post2":
                        mark(dve, ins, x_ready)
                    else:
                        do(ins)

            scaled_norm("post1", 32)
            for n in range(4, 12):
                wait_read_out(dve, jobs[f"adab{n}"])
            layer_stats([x_lat[:, t, :] for t in range(TT)])
            invert_std("mod2")
            for t in range(TT):
                do(normalized(h2[:, t, :], x_lat[:, t, :], t))
                do(tt(h2[:, t, :], h2[:, t, :], mods[:, 2, :], ALU.mult))
                mark(dve, tt(h2[:, t, :], h2[:, t, :], mods[:, 1, :], ALU.add), tok_ready)

            s = S5

            def s5_dt_rows():
                dve.wait_ge(load_s5, 16 * 10)
                mark(dve, dve.tensor_copy(s5_raw[0:16, 2, :].rearrange("p (g n) -> p g n", g=2),
                                          dt_raw[0:16, :].unsqueeze(2).to_broadcast([16, 2, 64])), s5_dt)

            def s5_angles():
                job = jobs["s5p"]
                wait_bank_full(dve, job)
                do(dve.tensor_copy(small[:, 0:48], ps(job)[:, 0:48]))
                do(dve.tensor_copy(d_col, ps(job)[:, 48:52]))
                read_out(dve, dve.tensor_copy(s["t1"], ps(job)[:, 32:48]), job)
                dve.wait_ge(s5_exp, 1)
                do(tt(s["mag"], s["lr"], s["dt"], ALU.mult))
                do(tt(s["th"], s["li"], s["dt"], ALU.mult))
                magic = 12582912.0
                do(dve.tensor_scalar(s["kk"], s["th"], 1.0 / (2 * pi), magic, ALU.mult, ALU.add))
                do(dve.tensor_scalar(s["kk"], s["kk"], magic, None, ALU.subtract))
                do(dve.scalar_tensor_tensor(out=s["r"], in0=s["kk"], scalar=-6.28125, in1=s["th"], op0=ALU.mult, op1=ALU.add))
                do(dve.scalar_tensor_tensor(out=s["r"], in0=s["kk"], scalar=-(2 * pi - 6.28125), in1=s["r"], op0=ALU.mult, op1=ALU.add))
                ins = dve.tensor_scalar(s["r"], s["r"], 3.1415925, -3.1415925, ALU.min, ALU.max)
                mark(dve, ins, s5_theta)

            def s5_factors():
                dve.wait_ge(s5_sin, 1)
                do(tt(s["cs"], s["hs"], s["hs"], ALU.mult))
                do(dve.tensor_scalar(s["cs"], s["cs"], -2.0, 1.0, ALU.mult, ALU.add))
                do(tt(s["t1"], s["cs"], s["cs"], ALU.mult))
                do(tt(s["t2"], s["sn"], s["sn"], ALU.mult))
                do(tt(s["t1"], s["t1"], s["t2"], ALU.add))
                do(dve.tensor_scalar(s["t1"], s["t1"], -0.5, 1.5, ALU.mult, ALU.add))
                do(tt(s["cs"], s["cs"], s["t1"], ALU.mult))
                do(tt(s["sn"], s["sn"], s["t1"], ALU.mult))
                do(tt(s["ar"], s["mag"], s["cs"], ALU.mult))
                do(tt(s["ai"], s["mag"], s["sn"], ALU.mult))
                do(dve.tensor_scalar(s["nr"], s["ar"], -1.0, None, ALU.add))
                do(tt(s["t1"], s["lr"], s["lr"], ALU.mult))
                do(tt(s["t2"], s["li"], s["li"], ALU.mult))
                do(tt(s["den"], s["t1"], s["t2"], ALU.add))
                do(dve.reciprocal(s["den"], s["den"]))
                do(tt(s["t1"], s["nr"], s["lr"], ALU.mult))
                do(tt(s["t2"], s["ai"], s["li"], ALU.mult))
                do(tt(s["fr"], s["t1"], s["t2"], ALU.add))
                do(tt(s["fr"], s["fr"], s["den"], ALU.mult))
                do(tt(s["t1"], s["ai"], s["lr"], ALU.mult))
                do(tt(s["t2"], s["nr"], s["li"], ALU.mult))
                do(tt(s["fi"], s["t1"], s["t2"], ALU.subtract))
                do(tt(s["fi"], s["fi"], s["den"], ALU.mult))

            def s5_inputs():
                wide = [P, NSTATE, 16]
                fr, fi = s["fr"].unsqueeze(2).to_broadcast(wide), s["fi"].unsqueeze(2).to_broadcast(wide)
                tmp = b_tmp
                do(tt(bbar[:, 0, :, :], braw[:, 0, :, :], fr, ALU.mult))
                do(tt(tmp, braw[:, 1, :, :], fi, ALU.mult))
                do(tt(bbar[:, 0, :, :], bbar[:, 0, :, :], tmp, ALU.subtract))
                do(tt(bbar[:, 1, :, :], braw[:, 1, :, :], fr, ALU.mult))
                do(tt(tmp, braw[:, 0, :, :], fi, ALU.mult))
                mark(dve, tt(bbar[:, 1, :, :], bbar[:, 1, :, :], tmp, ALU.add), s5_bbar)

            def s5_powers(first, last, start=False, half=None):
                if start:
                    for j in range(8):
                        wait_read_out(dve, jobs["BT"] + j)
                    dve.wait_ge(s5_c, 1)
                    go(dve.memset(er[:, :, 0:1], 1.0))
                    go(dve.memset(ei[:, :, 0:1], 0.0))
                    go(dve.tensor_copy(s["pr"], s["cs"]))
                    do(dve.tensor_copy(s["pi"], s["sn"]))
                tiles = slice(0, NSTATE) if half is None else slice(8 * half, 8 * half + 8)
                m = tiles.stop - tiles.start
                for level in range(first, last):
                    n = 2 ** level
                    pr, pi_ = [s[x][:, tiles].unsqueeze(2).to_broadcast([P, m, n]) for x in ("pr", "pi")]
                    e0, f0, e1, f1 = er[:, tiles, 0:n], ei[:, tiles, 0:n], er[:, tiles, n:2 * n], ei[:, tiles, n:2 * n]
                    tmp, tmp2 = [e_tmp[:, D * i:D * i + m * n].rearrange("p (j t) -> p j t", j=m) for i in range(2)]
                    go(tt(e1, e0, pr, ALU.mult))
                    go(tt(f1, f0, pr, ALU.mult))
                    go(tt(tmp, f0, pi_, ALU.mult))
                    do(tt(tmp2, e0, pi_, ALU.mult))
                    go(tt(e1, e1, tmp, ALU.subtract))
                    ins = tt(f1, f1, tmp2, ALU.add)
                    if level == 7:
                        if half == 1:
                            mark(dve, ins, s5_table)
                        else:
                            do(ins)
                        continue
                    go(ins)
                    go(tt(s["qr"], s["pr"], s["pr"], ALU.mult))
                    go(tt(s["qi"], s["pi"], s["pi"], ALU.mult))
                    do(tt(s["t1"], s["pr"], s["pi"], ALU.mult))
                    go(tt(s["pr"], s["qr"], s["qi"], ALU.subtract))
                    do(dve.tensor_scalar(s["pi"], s["t1"], 2.0, None, ALU.mult))

            do(tt(iota_f, ones[:, 0:TOPK], ones[:, 0:TOPK], ALU.subtract))
            do(dve.tensor_tensor_scan(iota_f, ones[:, 0:TOPK], ones[:, 0:TOPK], -1.0, ALU.mult, ALU.add))

            def best16(searches):
                for k, (x, work, v, i) in enumerate(searches):
                    go(dve.max(v[:, 0:8], x))
                wait_done()
                for x, work, v, i in searches:
                    go(dve.match_replace(work, v[:, 0:8], x, -3.0e38))
                wait_done()
                for x, work, v, i in searches:
                    go(dve.max_index(i[:, 0:8], v[:, 0:8], x))
                    go(dve.max(v[:, 8:16], work))
                wait_done()
                for x, work, v, i in searches:
                    go(dve.max_index(i[:, 8:16], v[:, 8:16], work))
                wait_done()

            def choose(t, h):
                if h % 2 == 0:
                    wait_read_out(dve, jobs[f"skey{h // 2}"] + t)
                best16([(s_key[t][:, 2 * h + c, :], s_work[:, c, :], top_v[:, c, :], top_i[:, c, :]) for c in range(2)])
                sq, pair = [P, TOPK, TOPK], [P, 2, TOPK, TOPK]
                go(dve.tensor_copy(top_f, top_i))
                do(tt(cand, top_v[:, 0, :].unsqueeze(2).to_broadcast(sq), top_v[:, 1, :].unsqueeze(1).to_broadcast(sq), ALU.add))
                best16([(cand.rearrange("p i j -> p (i j)"), c_work, best_v[:, h, :], best_p)])
                go(dve.tensor_scalar(part_i[:, 0, :], best_p, 4, None, ALU.logical_shift_right))
                do(dve.tensor_scalar(part_i[:, 1, :], best_p, 15, None, ALU.bitwise_and))
                do(dve.tensor_copy(part_f, part_i))
                do(tt(onehot, part_f.unsqueeze(3).to_broadcast(pair),
                      iota_f.unsqueeze(1).unsqueeze(1).to_broadcast(pair), ALU.is_equal))
                do(tt(onehot, onehot, top_f.unsqueeze(2).to_broadcast(pair), ALU.mult))
                do(dve.tensor_reduce(pick, onehot, AX_X, ALU.add))
                do(dve.scalar_tensor_tensor(out=pick[:, 0, :], in0=pick[:, 0, :], scalar=float(NKEYS), in1=pick[:, 1, :],
                                            op0=ALU.mult, op1=ALU.add))
                mark(dve, dve.tensor_copy(rows_i[:, t, TOPK * h:TOPK * (h + 1)], pick[:, 0, :]), rows_ready)
                if h == PEER_HEADS - 1:
                    gw = by_head(gate_w, t)
                    mark(dve, tt(gw, best_v, best_v[:, :, 0:1].to_broadcast([P, PEER_HEADS, TOPK]), ALU.subtract), best_ready)

            def by_head(x, t):
                return x[:, t, :].rearrange("p (h k) -> p h k", h=PEER_HEADS)

            def soften(t):
                gw = by_head(gate_w, t)
                dve.wait_ge(soft_ready, t + 1)
                do(dve.tensor_reduce(sm8[:, 0, :], gw, AX_X, ALU.add))
                do(dve.reciprocal(sm8[:, 1, :], sm8[:, 0, :]))
                do(tt(gw, gw, sm8[:, 1, :].unsqueeze(2).to_broadcast([P, PEER_HEADS, TOPK]), ALU.mult))

            def weigh(t):
                dve.wait_ge(gelu_done, t + 1)
                do(tt(act_w[:, t, :], act_w[:, t, :], gate_w[:, t, :], ALU.mult))

            def dots(t, first, last):
                base = 2 * t * GATHERS
                with dve.Fori(first, last) as head:
                    i = head * TOPK
                    for s in range(GSLOTS):
                        dve.wait_ge(gathered[s], i + (base + 16))
                        dve.scalar_tensor_tensor(out=gath[s], in0=gath[s], scalar=1.0, in1=h2[:, t, :],
                                                 op0=ALU.mult, op1=ALU.mult,
                                                 accum_out=act_w[:, t, bass.ds(i + s, 1)]).then_inc(row_used, 1)

            def add_rows(t, first, last):
                base = (2 * t + 1) * GATHERS
                with dve.Fori(first, last) as head:
                    i = head * TOPK
                    for s in range(GSLOTS):
                        dve.wait_ge(gathered[s], i + (base + 16))
                        dve.wait_ge(row_used, i + (base + s - 1))
                        dve.scalar_tensor_tensor(out=y_acc[:, s % 2, :], in0=gath[s],
                                                 scalar=act_w[:, t, bass.ds(i + s, 1)], in1=y_acc[:, s % 2, :],
                                                 op0=ALU.mult, op1=ALU.add).then_inc(row_used, 1)

            def add_experts(t):
                dve.wait_ge(row_used, 2 * (t + 1) * GATHERS)
                do(tt(y_acc[:, 0, :], y_acc[:, 0, :], y_acc[:, 1, :], ALU.add))
                do(tt(y_acc[:, 0, :], y_acc[:, 0, :], mods[:, 3, :], ALU.mult))
                do(dve.scalar_tensor_tensor(out=x_lat[:, t, :], in0=x_lat[:, t, :], scalar=ALPHA, in1=y_acc[:, 0, :],
                                            op0=ALU.mult, op1=ALU.add))

            AHEAD = 3
            for h in range(AHEAD):
                choose(0, h)
            go(dve.memset(y_acc, 0.0))
            for h in range(PEER_HEADS):
                if h + AHEAD < PEER_HEADS:
                    choose(0, h + AHEAD)
                if h == PEER_HEADS - AHEAD:
                    soften(0)
                dots(0, h, h + 1)
            choose(1, 0)
            weigh(0)
            add_rows(0, 0, 2)
            for h in range(2, PEER_HEADS, 2):
                choose(1, h // 2)
                add_rows(0, h, h + 2)
            choose(1, 4)
            dots(1, 0, 1)
            add_experts(0)
            go(dve.memset(y_acc, 0.0))
            dots(1, 1, 2)
            choose(1, 5)
            dots(1, 2, 3)
            choose(1, 6)
            dots(1, 3, 5)
            choose(1, 7)
            dots(1, 5, 6)
            soften(1)
            s5_dt_rows()
            dots(1, 6, 7)
            s5_angles()
            dots(1, 7, 8)
            s5_factors()
            weigh(1)
            add_rows(1, 0, 1)
            s5_inputs()
            add_rows(1, 1, 3)
            s5_powers(0, 6, True)
            add_rows(1, 3, 5)
            s5_powers(6, 7)
            add_rows(1, 5, 6)
            s5_powers(7, 8, False, 0)
            add_rows(1, 6, 7)
            s5_powers(7, 8, False, 1)
            add_rows(1, 7, 8)
            add_experts(1)
            scaled_norm("post2", 64)

            def split_low(q):
                dve.wait_ge(w_high, q + 1)
                w = w_split[q % SPLIT_SLOTS]
                cols = stream[tile_at[q]].shape[2]
                mark(dve, tt(w[:, 1, :, 0:cols], wtile(tile_at[q], cols), w[:, 0, :, 0:cols].bitcast(F32), ALU.subtract), w_low)

            def split_low_first(name, q0):
                if AHEAD_OF[name] == 0:
                    split_low(q0)
                for j in range(4):
                    job = jobs[f"T_{name}"] + j
                    counts["x_low"] = counts.get("x_low", 0) + 1
                    dve.wait_ge(x_high, counts["x_low"])
                    t, g = j // 2, j % 2
                    high, low = [x[:, 4 * g:4 * g + 4, t * P:(t + 1) * P] for x in x_split]
                    read_out(dve, tt(low, ps(job)[:, :].rearrange("p (k t) -> p k t", k=4), high.bitcast(F32), ALU.subtract), job)
                for q in range(max(1, AHEAD_OF[name]), 3):
                    split_low(q0 + q)

            def pre_norm(i, row, h_tok=h_tok):
                invert_std(f"rms{i}")
                dve.wait_ge(load_norm, 32 * (i // 2 + 1))
                for t in range(TT):
                    mark(dve, dve.scalar_tensor_tensor(out=h_tok[:, t, :], in0=x_lat[:, t, :], scalar=stat[:, t:t + 1],
                                                       in1=row_b[:, row, :], op0=ALU.mult, op1=ALU.mult), tok_ready)

            def post_norm(i, row, name, h_tok=h_tok):
                for j in range(4):
                    wait_read_out(dve, jobs[name] + j)
                square_sums([mix2[:, t, :] for t in range(TT)], h_tok)
                invert_std(f"rms{i}")
                for t in range(TT):
                    ins = dve.scalar_tensor_tensor(out=mix2[:, t, :], in0=mix2[:, t, :], scalar=stat[:, t:t + 1],
                                                   in1=row_b[:, row, :], op0=ALU.mult, op1=ALU.mult)
                    if t == 0:
                        go(ins)
                mark(dve, ins, rows_free)
                for t in range(TT):
                    ins = tt(x_lat[:, t, :], x_lat[:, t, :], mix2[:, t, :], ALU.add)
                    if i < 7:
                        mark(dve, ins, x_ready)
                    elif t == 0:
                        do(ins)
                    else:
                        mark(dve, ins, out_ready)

            pre_norm(0, 0, h_tok_s)

            def s5_out(a):
                job = jobs[f"y{a}"]
                wait_bank_full(dve, job)
                ins = dve.scalar_tensor_tensor(out=zT[:, a, :], in0=uT[:, a, :], scalar=d_col[:, a:a + 1],
                                               in1=ps(job)[:, 0:L], op0=ALU.mult, op1=ALU.add)
                read_out(dve, ins, job)

            for j in range(2):
                wait_read_out(dve, jobs["ssm_in"] + j)
            for j in range(NSTATE):
                job = jobs[f"bu{j}"]
                X, T = xs, turned[j % 2]
                E_ = er[:, j:j + 1, :].to_broadcast([P, 2, L])
                F_ = ei[:, j:j + 1, :].to_broadcast([P, 2, L])
                wait_bank_full(dve, job)
                b = ps(job)[:, :].rearrange("p (r t) -> p r t", r=2)
                go(tt(rt[:, 0, :, :], b, E_, ALU.mult))
                read_out(dve, tt(rt[:, 1, :, :], b, F_, ALU.mult), job)
                wait_done()
                go(tt(X[:, 0, :], rt[:, 0, 0, :], rt[:, 1, 1, :], ALU.add))
                do(tt(X[:, 1, :], rt[:, 0, 1, :], rt[:, 1, 0, :], ALU.subtract))
                r_ = s["mag"][:, j:j + 1].to_broadcast([P, L])
                for part in range(2):
                    go(dve.tensor_tensor_scan(X[:, part, :], r_, X[:, part, :], 0.0, ALU.mult, ALU.add))
                wait_done()
                if j >= 2:
                    if (j - 2) % 4 == 3:
                        wait_bank_full(dve, jobs[f"y{(j - 2) // 4}"])
                    else:
                        dve.wait_ge(y_used, j - 1 - (j - 2) // 4)
                go(tt(T[:, 0, :, :], X, E_, ALU.mult))
                go(tt(T[:, 1, 1, :], X[:, 0, :], ei[:, j, :], ALU.mult))
                ins = dve.scalar_tensor_tensor(out=T[:, 1, 0, :], in0=X[:, 1, :], scalar=-1.0, in1=ei[:, j, :],
                                               op0=ALU.mult, op1=ALU.mult)
                mark(dve, ins, x_state)
                if j % 4 == 0 and j:
                    s5_out(j // 4 - 1)
            s5_out(3)
            for j in range(2):
                wait_read_out(dve, jobs["glu"] + j)
            mark(dve, tt(zT, zT, rt.rearrange("p a b t -> p (a b) t"), ALU.mult), y_ready)
            split_low(0)
            post_norm(1, 1, "ssm_out")

            def mlp(i):
                q0 = split_no[tile_no[f"mlp{i}a0"]]
                pre_norm(4 * i + 2, 0)
                split_low_first(f"mlp{i}", q0)
                for n in range(8):
                    split_low(q0 + 2 * n + 3)
                    for j in range(2 * n, 2 * n + 2):
                        for b in range(2):
                            wait_read_out(dve, jobs[f"mlp{i}a"] + 2 * j + b)
                        x = ff_tmp[:, j % 3, :, :]
                        high, low = [ff_split[:, c, 2 * j:2 * j + 2, :] for c in range(2)]
                        go(tt(high, x, x, ALU.mult))
                        do(tt(x, x, x, ALU.mult))
                        mark(dve, tt(low, x, high.bitcast(F32), ALU.subtract), ff_ready)
                    split_low(q0 + 2 * n + 4)
                for q in range(q0 + 19, q0 + 32 + (AHEAD_OF["att"] if i == 0 else 0)):
                    split_low(q)
                post_norm(4 * i + 3, 1, f"mlp{i}b")

            mlp(0)

            pre_norm(4, 0)
            q0 = split_no[tile_no["att0"]]
            split_low_first("att", q0)
            for q in range(q0 + 3, q0 + 10):
                split_low(q)
            for j in range(10):
                wait_read_out(dve, jobs["att"] + j)
            dve.wait_ge(load_rope, 16)
            t1 = rope_t[:, 0, :]
            t2 = rope_t[:, 1, :]
            for t in range(TT):
                groups = [(0, 16, [roped[:, t, 0:16, :]]), (1536, 8, [roped[:, t, 16:24, :]]),
                          (1024, 4, [krope[:, t, 0:4, 0:HD], krope[:, t, 0:4, HD:]]),
                          (2048, 1, [krope[:, t, 4:5, 0:HD], krope[:, t, 4:5, HD:]])]
                for c0, nh, dsts in groups:
                    x = proj[:, t, c0:c0 + nh * HD].rearrange("p (h d) -> p h d", h=nh)
                    a = t1[:, 0:nh * HD].rearrange("p (h d) -> p h d", h=nh)
                    b = t2[:, 0:nh * HD].rearrange("p (h d) -> p h d", h=nh)
                    cos, sin = rope[:, t, 0:1, :], rope[:, t, 1:2, :]
                    go(tt(a, x, cos.to_broadcast([P, nh, HD]), ALU.mult))
                    go(tt(b[:, :, 0:32], x[:, :, 32:64], sin[:, :, 0:32].to_broadcast([P, nh, 32]), ALU.mult))
                    do(tt(b[:, :, 32:64], x[:, :, 0:32], sin[:, :, 32:64].to_broadcast([P, nh, 32]), ALU.mult))
                    for k, o in enumerate(dsts):
                        ins = tt(o, a, b, ALU.add)
                        if not (c0 == 2048 and k == 1):
                            do(ins)
                mark(dve, ins, roped_ready)
            scale_w = IDX_HEADS ** -0.5 * HD ** -0.5
            do(dve.tensor_scalar(wi_col, proj[:, :, 2112:2120], scale_w, None, ALU.mult))
            for t in range(TT):
                for g in range(4):
                    wait_read_out(dve, jobs["idx"] + 4 * t + g)
                    for b in range(2):
                        h = 4 * (g // 2) + 2 * b + g % 2
                        w = wi_col[:, t, h:h + 1]
                        x, total = rel[:, g % 2, b, seen(t)], idx_s[:, t, seen(t)]
                        if g == 0 and b == 0:
                            ins = dve.tensor_scalar(total, x, w, None, ALU.mult)
                        else:
                            ins = dve.scalar_tensor_tensor(out=total, in0=x, scalar=w, in1=total,
                                                           op0=ALU.mult, op1=ALU.add)
                        if b == 0:
                            do(ins)
                    mark(dve, ins, rel_used)
            for t in range(TT):
                dve.wait_ge(idx_causal, t + 1)
                src = idx_s
                for r in range(K_SEL // 8):
                    do(dve.max(m8, src[:, t, seen(t)]))
                    do(dve.match_replace(idx_w[:, t, seen(t)], m8, src[:, t, seen(t)], -3.0e38))
                    src = idx_w
                kept = keep[:, t, seen(t)]
                do(dve.tensor_scalar(kept, idx_w[:, t, seen(t)], -2.0e38, 1.0, ALU.is_le, ALU.subtract))
                mark(dve, dve.tensor_scalar(kept, kept, -NEG, None, ALU.mult), keep_ready)
                dve.wait_ge(keep_causal, t + 1)
                for g in range(8):
                    job = jobs[f"att_s{t}"] + g
                    wait_bank_full(dve, job)
                    read_out(dve, dve.scalar_tensor_tensor(
                        out=prob[:, t, 4 * (g // 2):4 * (g // 2) + 4, :].rearrange("p (b e) s -> p b e s", e=2)[:, :, g % 2, seen(t)],
                        in0=ps(job)[:, :].rearrange("p (a b) -> p a b", a=2)[:, :, seen(t)],
                        scalar=HD ** -0.5, in1=keep[:, t:t + 1, seen(t)].to_broadcast([P, 2, P * (t + 1)]), op0=ALU.mult, op1=ALU.add), job)
                do(dve.tensor_reduce(mx16[:, t, :], prob[:, t, :, seen(t)], AX_X, ALU.max))
                mark(dve, dve.tensor_scalar(mx16[:, t, :], mx16[:, t, :], -1.0, None, ALU.mult), logits_ready)
            for t in range(TT):
                dve.wait_ge(prob_ready, t + 1)
                do(dve.reciprocal(sum16[:, t, :], sum16[:, t, :]))
                for g in range(2):
                    job = jobs[f"pv{t}"] + g
                    wait_bank_full(dve, job)
                    read_out(dve, tt(o_att[:, t, 512 * g:512 * g + 512].rearrange("p (h d) -> p h d", h=8),
                                     ps(job)[:, :].rearrange("p (h d) -> p h d", h=8),
                                     sum16[:, t, 8 * g:8 * g + 8].unsqueeze(2).to_broadcast([P, 8, HD]), ALU.mult), job)
            q0 = split_no[tile_no["att_out0"]]
            split_low_first("atto", q0)
            for q in range(q0 + 3, q0 + 4 + AHEAD_OF["mlp1"]):
                split_low(q)
            post_norm(5, 1, "att_out")
            mlp(1)


_INS = ['x', 'c', 'ctx', 'c_ctx', 'w_ada', 'b_ada', 'w_in', 'w_gk2', 'b_gk', 'hg_lower_bounds', 'hg_norm', 'gla_norm',
        'w_out', 'ln_gamma', 'ln_beta', 'peer_w_query', 'peer_sub_keys', 'peer_u', 'peer_v', 'norm_g_2', 'mlp_w1_2',
        'mlp_w2_2', 'ssm_w_in_2', 'ssm_lam_re_2', 'ssm_lam_im_2', 'ssm_log_dt_2', 'ssm_b_re_2', 'ssm_b_im_2',
        'ssm_c_re_2', 'ssm_c_im_2', 'ssm_d_2', 'ssm_w_glu_2', 'ssm_w_out_2', 'att_w_in_2', 'att_w_out_2']


def kernel(**inputs):
    import numpy as _np
    import concourse.bacc as _bacc
    from concourse.bass_utils import run_bass_kernel_spmd as _run

    nc = _bacc.Bacc("TRN2", target_bir_lowering=False, num_devices=1)
    arrays, aps = {}, {}

    def give(name, a):
        arrays[f"in_{name}"] = a
        aps[name] = nc.dram_tensor(f"in_{name}", a.shape, mybir.dt.from_np(a.dtype), kind="ExternalInput").ap()

    for name in _INS:
        give(name, _np.ascontiguousarray(inputs[name]))
    half = HD // 2
    freq = _np.float32(10000.0) ** (-_np.arange(half, dtype=_np.float32) * _np.float32(2.0) / _np.float32(HD))
    ang = _np.arange(L, dtype=_np.float32)[:, None] * freq[None, :].astype(_np.float32)
    cos, sin = _np.cos(ang), _np.sin(ang)
    give("rope_table", _np.ascontiguousarray(
        _np.stack([_np.concatenate([cos, cos], 1), _np.concatenate([-sin, sin], 1)], 1).astype(_np.float32)))
    out = nc.dram_tensor("out_0", (1, L, D), F32, kind="ExternalOutput").ap()
    build(nc, aps, out)
    r = _run(nc, [arrays], core_ids=[0])
    return r.results[0]["out_0"]
```
